# Optimizing a Trainium2 kernel written in Bass

```python
import math
import jax
import jax.numpy as jnp
from jax import lax
import numpy as np

D_MODEL = 1024
BATCH = 1
SEQ = 512
DEPTH = 2

N_META = 16
D_FF = 4 * D_MODEL
GDN_HEADS = 4
GDN_DK = 128
GDN_DV = 128
GDN_CONV = 4
GDN_CHUNK = 64
SB_HEADS = 8
SB_DH = 64
SB_BLOCK = 128
HG_HEADS = 8
HG_DK = D_MODEL // HG_HEADS
HG_DV = D_MODEL // HG_HEADS
HG_CHUNK = 64

N_EVEN = (DEPTH + 1) // 2
N_ODD = DEPTH // 2
DN_ALPHA = float((2 * DEPTH) ** 0.25)
DN_BETA = float((8 * DEPTH) ** -0.25)
LN_EPS = 1e-5
RMS_EPS = 1e-6
L2_EPS = 1e-6

GDN_QK_W = GDN_HEADS * GDN_DK
GDN_V_W = GDN_HEADS * GDN_DV
SB_W = SB_HEADS * SB_DH
AB_SPLITS = (GDN_QK_W, GDN_QK_W, GDN_V_W, GDN_V_W, GDN_HEADS, GDN_HEADS, SB_W, SB_W, SB_W)
AB_IN = sum(AB_SPLITS)
AB_OUT_IN = GDN_V_W + SB_W
HG_K_W = HG_HEADS * HG_DK
HG_V_W = HG_HEADS * HG_DV
C_SPLITS = (HG_K_W, HG_K_W, HG_V_W, HG_V_W)
C_IN = sum(C_SPLITS)

kernel_name = "hybrid_gdn_stickbreak_hgrn2_deepnorm"

def _split(a, sizes):
    idx = np.cumsum(sizes)[:-1].tolist()
    return jnp.split(a, idx, axis=-1)

def _front_pad(a, pad):
    return jnp.pad(a, [(0, 0), (pad, 0)] + [(0, 0)] * (a.ndim - 2))

def _to_chunks(a, n, c):
    bn, _, h, d = a.shape
    return jnp.transpose(a.reshape(bn, n, c, h, d), (1, 0, 3, 2, 4))

def _from_chunks(o):
    n, bn, h, c, d = o.shape
    return jnp.transpose(o, (1, 0, 3, 2, 4)).reshape(bn, n * c, h, d)

def layer_norm(x, g, b):
    xf = x.astype(jnp.float32)
    mu = jnp.mean(xf, axis=-1, keepdims=True)
    var = jnp.mean(jnp.square(xf - mu), axis=-1, keepdims=True)
    y = (xf - mu) * lax.rsqrt(var + LN_EPS)
    return (y * g.astype(jnp.float32) + b.astype(jnp.float32)).astype(x.dtype)

def rms_norm(x, g):
    xf = x.astype(jnp.float32)
    y = xf * lax.rsqrt(jnp.mean(xf * xf, axis=-1, keepdims=True) + RMS_EPS)
    return y * g.astype(jnp.float32)

def l2_normalize(x):
    xf = x.astype(jnp.float32)
    return xf * lax.rsqrt(jnp.sum(xf * xf, axis=-1, keepdims=True) + L2_EPS)

def causal_depthwise_conv(x, w):
    k_w, ch = w.shape
    return lax.conv_general_dilated(
        x, w[:, None, :].astype(x.dtype), window_strides=(1,), padding=[(k_w - 1, 0)],
        dimension_numbers=("NWC", "WIO", "NWC"), feature_group_count=ch)

def gated_delta_rule_chunked(q, k, v, g, beta):
    bn, t_len, h, dk = q.shape
    dv = v.shape[-1]
    c = GDN_CHUNK
    n = t_len // c
    q, k, v = (_to_chunks(a, n, c) for a in (q, k, v))
    g, beta = (_to_chunks(a[..., None], n, c)[..., 0] for a in (g, beta))
    gc = jnp.cumsum(g, axis=-1)
    causal = jnp.tril(jnp.ones((c, c), dtype=bool))
    strict = jnp.tril(jnp.ones((c, c), dtype=bool), -1)
    decay = jnp.exp(jnp.where(causal, gc[..., :, None] - gc[..., None, :], -jnp.inf))
    kb = k * beta[..., None]
    m = jnp.where(strict, jnp.einsum("nbhid,nbhjd->nbhij", kb, k) * decay, 0.0)
    eye = jnp.broadcast_to(jnp.eye(c, dtype=jnp.float32), m.shape)
    t_inv = lax.linalg.triangular_solve(eye + m, eye, left_side=True, lower=True, unit_diagonal=True)
    u = jnp.einsum("nbhij,nbhjd->nbhid", t_inv, v * beta[..., None])
    w = jnp.einsum("nbhij,nbhjd->nbhid", t_inv, kb * jnp.exp(gc)[..., None])
    a_intra = jnp.einsum("nbhid,nbhjd->nbhij", q, k) * decay
    q_dec = q * jnp.exp(gc)[..., None]
    k_dec = k * jnp.exp(gc[..., -1:] - gc)[..., None]
    g_tot = jnp.exp(gc[..., -1])

    def step(s, xs):
        u_n, w_n, qd_n, kd_n, a_n, gt_n = xs
        v_new = u_n - jnp.einsum("bhcd,bhde->bhce", w_n, s)
        o_n = jnp.einsum("bhcd,bhde->bhce", qd_n, s) + jnp.einsum("bhij,bhje->bhie", a_n, v_new)
        s = s * gt_n[..., None, None] + jnp.einsum("bhcd,bhce->bhde", kd_n, v_new)
        return s, o_n

    s0 = jnp.zeros((bn, h, dk, dv), jnp.float32)
    _, o = lax.scan(step, s0, (u, w, q_dec, k_dec, a_intra, g_tot))
    return _from_chunks(o)

def stick_breaking_attention(q, k, v):
    bn, l_len, h, d = q.shape
    pad = (-l_len) % SB_BLOCK
    t_len = l_len + pad
    nb = t_len // SB_BLOCK
    to_bhtd = lambda a: jnp.moveaxis(_front_pad(a.astype(jnp.float32), pad), 1, 2)
    q, k, v = (to_bhtd(a) for a in (q, k, v))
    q = q * (d ** -0.5)
    key_pos = jnp.arange(t_len)
    q_blocks = jnp.moveaxis(q.reshape(bn, h, nb, SB_BLOCK, d), 2, 0)
    q_pos = jnp.arange(t_len).reshape(nb, SB_BLOCK)

    def block(args):
        qb, qp = args
        z = jnp.einsum("bhqd,bhkd->bhqk", qb, k)
        allowed = (key_pos[None, :] < qp[:, None]) & (key_pos[None, :] >= pad)
        log_1m = jnp.where(allowed, jax.nn.log_sigmoid(-z), 0.0)
        after = lax.cumsum(log_1m, axis=3, reverse=True) - log_1m
        wgt = jnp.where(allowed, jnp.exp(jax.nn.log_sigmoid(z) + after), 0.0)
        return jnp.einsum("bhqk,bhkd->bhqd", wgt, v)

    o = lax.map(block, (q_blocks, q_pos))
    o = jnp.moveaxis(o, 0, 2).reshape(bn, h, t_len, d)[:, :, pad:]
    return jnp.moveaxis(o, 1, 2).reshape(bn, l_len, h * d)

def hgrn2_chunked(q, k, v, logf):
    bn, t_len, h, dk = q.shape
    dv = v.shape[-1]
    c = HG_CHUNK
    n = t_len // c
    q, k, v, logf = (_to_chunks(a, n, c) for a in (q, k, v, logf))
    b = jnp.cumsum(logf, axis=3)
    causal = jnp.tril(jnp.ones((c, c), dtype=bool))[:, :, None]

    def step(s, xs):
        q_n, k_n, v_n, b_n = xs
        pair = jnp.exp(jnp.where(causal, b_n[:, :, :, None, :] - b_n[:, :, None, :, :], -jnp.inf))
        a_n = jnp.einsum("bhtc,bhsc,bhtsc->bhts", q_n, k_n, pair)
        b_last = b_n[:, :, -1:, :]
        o_n = (jnp.einsum("bhtc,bhce->bhte", q_n * jnp.exp(b_n), s)
               + jnp.einsum("bhts,bhse->bhte", a_n, v_n))
        s = (jnp.exp(b_last)[:, :, 0, :, None] * s
             + jnp.einsum("bhsc,bhse->bhce", k_n * jnp.exp(b_last - b_n), v_n))
        return s, o_n

    s0 = jnp.zeros((bn, h, dk, dv), jnp.float32)
    _, o = lax.scan(step, s0, (q, k, v, b))
    return _from_chunks(o)

def mixer_gdn_sb(h, w_in, conv_w, a_log, dt_bias, gnorm_g, w_out):
    bn, l_len, _ = h.shape
    qa, ka, va, za, ba, aa, qb, kb, vb = _split(h @ w_in, AB_SPLITS)
    qkv = jax.nn.silu(causal_depthwise_conv(jnp.concatenate([qa, ka, va], axis=-1), conv_w))
    qa, ka, va = _split(qkv, (GDN_QK_W, GDN_QK_W, GDN_V_W))
    qa = l2_normalize(qa.reshape(bn, l_len, GDN_HEADS, GDN_DK)) * (GDN_DK ** -0.5)
    ka = l2_normalize(ka.reshape(bn, l_len, GDN_HEADS, GDN_DK))
    va = va.reshape(bn, l_len, GDN_HEADS, GDN_DV).astype(jnp.float32)
    beta = jax.nn.sigmoid(ba.astype(jnp.float32))
    g = -jnp.exp(a_log.astype(jnp.float32)) * jax.nn.softplus(aa.astype(jnp.float32) + dt_bias.astype(jnp.float32))
    pad = (-l_len) % GDN_CHUNK
    oa = gated_delta_rule_chunked(*(_front_pad(a, pad) for a in (qa, ka, va, g, beta)))[:, pad:]
    oa = rms_norm(oa, gnorm_g) * jax.nn.silu(za.reshape(bn, l_len, GDN_HEADS, GDN_DV).astype(jnp.float32))
    oa = oa.reshape(bn, l_len, GDN_V_W)
    shp = (bn, l_len, SB_HEADS, SB_DH)
    ob = stick_breaking_attention(qb.reshape(shp), kb.reshape(shp), vb.reshape(shp))
    return jnp.concatenate([oa.astype(h.dtype), ob.astype(h.dtype)], axis=-1) @ w_out

def mixer_hgrn2(h, w_in, lb, gnorm_g, w_out):
    bn, l_len, _ = h.shape
    q, f, i, z = _split(h @ w_in, C_SPLITS)
    shp_k = (bn, l_len, HG_HEADS, HG_DK)
    shp_v = (bn, l_len, HG_HEADS, HG_DV)
    lbf = lb.astype(jnp.float32).reshape(HG_HEADS, HG_DK)
    fgate = lbf + (1.0 - lbf) * jax.nn.sigmoid(f.astype(jnp.float32).reshape(shp_k))
    logf = jnp.log(fgate)
    k = 1.0 - fgate
    q = jax.nn.silu(q.astype(jnp.float32)).reshape(shp_k)
    v = i.astype(jnp.float32).reshape(shp_v)
    pad = (-l_len) % HG_CHUNK
    o = hgrn2_chunked(*(_front_pad(a, pad) for a in (q, k, v, logf)))[:, pad:]
    o = rms_norm(o, gnorm_g) * jax.nn.silu(z.astype(jnp.float32).reshape(shp_v))
    return o.reshape(bn, l_len, HG_V_W).astype(h.dtype) @ w_out

def squared_relu_mlp(h, w1, w2):
    return jnp.square(jax.nn.relu(h @ w1)) @ w2

def setup_inputs(seed: int = 0) -> dict:
    key = jax.random.key(seed)
    ks = jax.random.split(key, 18)
    nrm = lambda k, shape, scale: jax.random.normal(k, shape, jnp.float32) * scale
    x = nrm(ks[0], (BATCH, SEQ, D_MODEL), 1.0)
    meta_tokens = nrm(ks[1], (N_META, D_MODEL), 1.0)
    ab_w_in = nrm(ks[2], (N_EVEN, D_MODEL, AB_IN), D_MODEL ** -0.5)
    ab_conv_w = nrm(ks[3], (N_EVEN, GDN_CONV, 2 * GDN_QK_W + GDN_V_W), GDN_CONV ** -0.5)
    ab_a_log = jnp.log(jax.random.uniform(ks[4], (N_EVEN, GDN_HEADS), jnp.float32, 1.0, 16.0))
    dt = jnp.exp(jax.random.uniform(ks[5], (N_EVEN, GDN_HEADS), jnp.float32, math.log(1e-3), math.log(1e-1)))
    ab_dt_bias = dt + jnp.log(-jnp.expm1(-dt))
    ab_gnorm_g = 1.0 + nrm(ks[6], (N_EVEN, GDN_DV), 0.02)
    ab_w_out = nrm(ks[7], (N_EVEN, AB_OUT_IN, D_MODEL), (AB_OUT_IN ** -0.5) * DN_BETA)
    c_w_in = nrm(ks[8], (N_ODD, D_MODEL, C_IN), D_MODEL ** -0.5)
    c_lb_raw = nrm(ks[9], (DEPTH, HG_K_W), 0.1)
    c_gnorm_g = 1.0 + nrm(ks[10], (N_ODD, HG_DV), 0.02)
    c_w_out = nrm(ks[11], (N_ODD, HG_V_W, D_MODEL), (HG_V_W ** -0.5) * DN_BETA)
    ln_mix_g = 1.0 + nrm(ks[12], (DEPTH, D_MODEL), 0.02)
    ln_mix_b = nrm(ks[13], (DEPTH, D_MODEL), 0.02)
    mlp_w1 = nrm(ks[14], (DEPTH, D_MODEL, D_FF), D_MODEL ** -0.5)
    mlp_w2 = nrm(ks[15], (DEPTH, D_FF, D_MODEL), (D_FF ** -0.5) * DN_BETA)
    ln_ffn_g = 1.0 + nrm(ks[16], (DEPTH, D_MODEL), 0.02)
    ln_ffn_b = nrm(ks[17], (DEPTH, D_MODEL), 0.02)
    return {"x": x, "meta_tokens": meta_tokens, "ab_w_in": ab_w_in, "ab_conv_w": ab_conv_w,
            "ab_a_log": ab_a_log, "ab_dt_bias": ab_dt_bias, "ab_gnorm_g": ab_gnorm_g, "ab_w_out": ab_w_out,
            "c_w_in": c_w_in, "c_lb_raw": c_lb_raw, "c_gnorm_g": c_gnorm_g, "c_w_out": c_w_out,
            "ln_mix_g": ln_mix_g, "ln_mix_b": ln_mix_b, "mlp_w1": mlp_w1, "mlp_w2": mlp_w2,
            "ln_ffn_g": ln_ffn_g, "ln_ffn_b": ln_ffn_b}

def reference(x, meta_tokens, ab_w_in, ab_conv_w, ab_a_log, ab_dt_bias, ab_gnorm_g, ab_w_out,
              c_w_in, c_lb_raw, c_gnorm_g, c_w_out, ln_mix_g, ln_mix_b, mlp_w1, mlp_w2,
              ln_ffn_g, ln_ffn_b):
    lb_all = jnp.cumsum(jax.nn.softmax(c_lb_raw.astype(jnp.float32), axis=0), axis=0)
    lb_all = lb_all - lb_all[0:1]
    meta = jnp.broadcast_to(meta_tokens[None].astype(x.dtype), (x.shape[0], N_META, D_MODEL))
    h = jnp.concatenate([meta, x], axis=1)
    for layer in range(DEPTH):
        j = layer // 2
        if layer % 2 == 0:
            mix = mixer_gdn_sb(h, ab_w_in[j], ab_conv_w[j], ab_a_log[j], ab_dt_bias[j], ab_gnorm_g[j], ab_w_out[j])
        else:
            mix = mixer_hgrn2(h, c_w_in[j], lb_all[layer], c_gnorm_g[j], c_w_out[j])
        h = layer_norm(DN_ALPHA * h + mix, ln_mix_g[layer], ln_mix_b[layer])
        h = layer_norm(DN_ALPHA * h + squared_relu_mlp(h, mlp_w1[layer], mlp_w2[layer]),
                       ln_ffn_g[layer], ln_ffn_b[layer])
    return h[:, N_META:]


_drawn_inputs = setup_inputs


def setup_inputs(seed=0):
    import zlib

    import numpy as np

    out = dict(_drawn_inputs(seed))
    spreads = {}
    factors = {'meta_tokens': 3.397,
     'ab_a_log': 3.828,
     'ab_gnorm_g': 23.311,
     'c_lb_raw': 8.0,
     'c_gnorm_g': 22.654}
    for name, (base, spread) in spreads.items():
        noise = np.random.default_rng([zlib.crc32(name.encode()), seed]).standard_normal(out[name].shape)
        drawn = base * np.exp(spread * noise) if base else spread * noise
        out[name] = jnp.asarray(drawn.astype(out[name].dtype))
    for name, factor in factors.items():
        out[name] = (out[name] * factor).astype(out[name].dtype)
    return out
```

```python
from contextlib import ExitStack

import concourse.bass as bass
from concourse import mybir

ALU = mybir.AluOpType
ACT = mybir.ActivationFunctionType
F32 = mybir.dt.float32
F32R = mybir.dt.float32r
BF16 = mybir.dt.bfloat16

P = 128
D = 1024
KT = D // P
SEQ, N_META = 512, 16
T = SEQ + N_META
HALF = T // 2
N_FULL = T // P
TAIL = T - N_FULL * P
DEPTH = 2
GH = 4
SH, SD = 8, 64
HH = 8
COLS = 256
ALPHA = float((2 * DEPTH) ** 0.25)
LN_EPS, RMS_EPS, L2_EPS = 1e-5, 1e-6, 1e-6
EXP_LN = "natural_log_exp_and_others"
LEVELS = [1, 2, 4, 8, 16, 32, 64]
NEG = -1e30

C_GE, C_SUFFIX, C_NEG, C_LEVEL = 0, P, 2 * P, 3 * P
C_SEL = C_LEVEL + len(LEVELS) * P
C_ALL = C_SEL + GH * P
P_LNG, P_LNB = 0, 4 * KT
P_CONV = 8 * KT
P_LB = P_CONV + 12 * 4
P_GN = P_LB + 2 * HH
P_ALL = P_GN + 2
ZW = 1376
Z_PARTS = [(0, 0, 512, 0), (1, 128, 400, 512), (0, 512, 16, 912), (4, 512, 16, 928),
           (2, 256, 272, 944), (3, 384, 160, 1216)]
Z_BANKS = [(0, 0, 512), (1, 512, 432), (2, 944, 432)]
QPAD = T + 16

N_CONST_LOADS = 6
PHASES = [("qkv", 6), ("z0", 2), ("qk", 4), ("v0", 2), ("out0", 4), ("mlp0", 32),
          ("f", 4), ("v1", 4), ("q1", 4), ("z1", 4), ("out1", 4), ("mlp1", 32)]
N_STAGES = sum(n for _, n in PHASES)


def _counts():
    at, stages, feature, evacs = {}, 0, 0, 1
    for name, n in PHASES:
        at[name] = (stages, feature, evacs)
        stages += n
        if name not in ("v0", "v1"):
            feature += n
            evacs += n // 2 + n // 4 if name.startswith("mlp") else n
    at["end"] = (stages, feature, evacs)
    return at


AT = _counts()


def z_where(col):
    for bank, first, n in Z_BANKS:
        if first <= col < first + n:
            return bank, col - first


def z_runs(tile, q0, q1):
    return [(c + max(s, q0) - s, max(s, q0), min(s + n, q1) - max(s, q0))
            for j, s, n, c in Z_PARTS if j == tile and max(s, q0) < min(s + n, q1)]


class Signal:

    def __init__(self, sem, per=1, step=1):
        self.sem, self.per, self.step = sem, per, step

    def at(self, i, k=None):
        k = self.per - 1 if k is None else k
        return i * (self.per * self.step) + (k + 1) * self.step


def hybrid_trunk(nc, h_in, wstream, wgate, consts, hmasks, params, gate_params, out):
    ctx = ExitStack()
    with ctx:
        def levels(n):
            return [(x, x + 1) for x, m in enumerate(LEVELS[1:]) if 2 * m <= n]

        def sb(name, shape, dt=F32, c=ctx):
            return c.enter_context(nc.sbuf_tensor(name, shape, dt))

        def sig(name, per=1, step=1):
            return Signal(ctx.enter_context(nc.semaphore(name)), per, step)

        PS = ctx.enter_context(nc.psum_tensor("banks", [P, 8, 512], F32))

        h = sb("h", [P, KT, T])
        x_hi = sb("x_hi", [P, KT, T], F32R)
        x_lo = sb("x_lo", [P, KT, T], F32R)
        w_raw = sb("w_raw", [P, 2, KT * COLS])
        w_hi = sb("w_hi", [P, 2, KT * COLS], F32R)
        w_lo = sb("w_lo", [P, 2, KT * COLS], F32R)
        ident = sb("ident", [P, P])
        hmask = sb("hmask", [P, len(LEVELS) + 3, HALF], mybir.dt.uint8)
        dmask = hmask[:, 8:10, :].rearrange("p a t -> p (a t)")
        par = sb("par", [P, P_ALL])
        ident_b = sb("ident_b", [P, P], BF16)
        neg_b = sb("neg_b", [P, P], BF16)
        ones = sb("ones", [P, P])
        ones_d = sb("ones_d", [P, P])
        ones_h = sb("ones_h", [P, P])
        small = sb("small", [P, 4])
        eps_ln, eps_rms = small[:, 0:1], small[:, 1:2]
        gp = sb("gp", [GH, 3])
        lbt = sb("lbt", [P, 8, HH])
        lb, one_minus_lb = lbt[:, 0, :], lbt[:, 1, :]

        m0 = ExitStack()
        qkv = sb("qkv", [P, 12, T], c=m0)
        z0 = sb("z0", [P, GH, T], c=m0)
        con = sb("con", [P, C_ALL], c=m0)
        mask_in = qkv[:, 0:5, :].rearrange("p c (a t) -> p (c a) t", a=2)
        ge_mask = con[:, C_GE:C_GE + P]
        suffix = con[:, C_SUFFIX:C_SUFFIX + P]

        def level_mask(n, l):
            return con[0:n, C_LEVEL + l * P:C_LEVEL + l * P + n]

        def heads(ap, n):
            return ap.rearrange("p (o n) -> p o n", o=1).broadcast_to((n, GH, n))

        def sel_of(a):
            return con[0:GH, C_SEL + a * P:C_SEL + (a + 1) * P]

        ga = ExitStack()
        wg = sb("wg", [P, KT, 36], c=ga)
        beta = sb("beta", [GH, T], c=ga)
        gcum = sb("gcum", [GH, T], c=ga)
        gtmp = sb("gtmp", [GH, 3, T], c=ga)
        colg = sb("colg", [P, N_FULL + 1, 2, GH], c=ga)
        cv = ExitStack()
        conv_in = sb("conv_in", [P, 2, T + 3], c=cv)
        conv_acc = sb("conv_acc", [P, 2, T], c=cv)
        nrm_a = sb("nrm_a", [P, GH, T], c=cv)
        cv.close()
        lp = ExitStack()
        kS, qS, vS, GB, BB, DM, MT, TT, TM, XS, AT0, KD, VB, EG, RR, VN, SS = (
            sb(n, [P, GH, P], c=lp) for n in ("kS", "qS", "vS", "GB", "BB", "DM", "MT", "TT", "TM", "XS", "AT0",
                                              "KD", "VB", "EG", "RR", "VN", "SS"))
        ML = sb("ML", [P, 2, GH, P], c=lp)
        gsm = sb("gsm", [P, 6, GH], c=lp)
        gcol, bcol, gdiff, kd4, eg4, nb4 = (gsm[:, x, :] for x in range(6))
        gsel = sb("gsel", [GH, 2, P], c=lp)
        lp.close()
        ga.close()
        at = ExitStack()
        qk = sb("qk", [P, 8, T], c=at)
        vt = sb("vt", [P, 5, SH * SD], c=at)
        sq_k = sb("sq_k", [P, 640], c=at)
        sq_q = sb("sq_q", [P, QPAD], c=at)
        sq_v = sb("sq_v", [P, 5, P], c=at)
        zs = sb("zs", [P, 2, ZW], c=at)
        sp = sb("sp", [P, 2, ZW], c=at)
        at.close()
        nb = ExitStack()
        nrm_b = sb("nrm_b", [P, GH, T], c=nb)
        nb.close()
        m0.close()
        ln = ExitStack()
        rstd = sb("rstd", [P, T], c=ln)
        lnsq = sb("lnsq", [P, 2, T], c=ln)
        ln.close()
        ml = ExitStack()
        hid_hi = sb("hid_hi", [P, 16, T], F32R, c=ml)
        hid_lo = sb("hid_lo", [P, 16, T], F32R, c=ml)
        relu = sb("relu", [P, 2, T], c=ml)
        sqr = sb("sqr", [P, 2, T], c=ml)
        ml.close()
        m1 = ExitStack()
        fg = sb("fg", [P, HH, T], c=m1)
        q1 = sb("q1", [P, HH, T], c=m1)
        z1 = sb("z1", [P, HH, T], c=m1)
        v1 = sb("v1", [P, 5, D], c=m1)
        hl = ExitStack()
        bc, kg, eb = (sb(n, [P, T], c=hl) for n in ("bc", "kg", "eb"))
        ee = sb("ee", [P, 2, T], c=hl)
        qt, kt = (sb(n, [P, 2, 640], c=hl) for n in ("qt", "kt"))
        aT = sb("aT", [P, 640], c=hl)
        khT, s1 = (sb(n, [P, 4, P], c=hl) for n in ("khT", "s1"))
        vh = sb("vh", [P, 5, P], c=hl)
        el = sb("el", [P, 4], c=hl)
        hl.close()
        nrm_c = sb("nrm_c", [P, GH, T], c=m1)
        m1.close()

        consts_loaded = sig("consts_loaded", step=16)
        wgate_loaded = sig("wgate_loaded", step=16)
        out_stored = sig("out_stored", step=16)
        w_loaded = [sig(f"w_loaded{u}", step=16) for u in range(2)]
        w_hi_made, w_lo_made = sig("w_hi_made"), sig("w_lo_made")
        half_done, stage_done = sig("half_done"), sig("stage_done")
        evac = [sig("evacuated0"), sig("evacuated1")]
        act_waited, dve_waited, pool_waited = sig("act_waited"), sig("dve_waited"), sig("pool_waited")
        tile_done = [half_done, stage_done]
        v_tile_done0 = sig("v_tile_done0", 4)
        v_tile_done1 = sig("v_tile_done1", 4)
        v_evacuated0 = sig("v_evacuated0", 5)
        v_evacuated1 = sig("v_evacuated1", 5)
        gdn_hi_made = sig("gdn_hi_made", GH)
        hg_hi_made = sig("hg_hi_made", HH)
        x_lo_made = sig("x_lo_made", KT)
        out_ready = sig("out_ready", KT)
        m_made = sig("m_made", 2)
        x_done = sig("x_done", 6)
        level_masked = sig("level_masked", 6)
        b_made = sig("b_made", 5)
        level_scaled = sig("level_scaled", 7)
        level_exponent = sig("level_exponent", 7)
        norm_squared = sig("norm_squared")
        norm_summed = sig("norm_summed")
        norm_logged = sig("norm_logged")
        ln_mean_ready = sig("ln_mean_ready")
        ln_squared = sig("ln_squared", KT)
        ln_square_used = sig("ln_square_used", KT)
        hidden_lo_made = sig("hidden_lo_made", 16)
        consts_made = sig("consts_made")
        gates_done = sig("gates_done")
        beta_made = sig("beta_made")
        gcum_made = sig("gcum_made", 5)
        columns_done = sig("columns_done")
        columns_made = sig("columns_made")
        gate_rows_staged = sig("gate_rows_staged")
        decay_rows_done = sig("decay_rows_done")
        beta_rows_done = sig("beta_rows_done")
        heads_staged = sig("heads_staged")
        kk_done = sig("kk_done")
        qk_done = sig("qk_done")
        k_turned = sig("k_turned")
        state_ready = sig("state_ready")
        v_turned = sig("v_turned")
        tt_first = sig("tt_first")
        t_turned = sig("t_turned")
        t_first = sig("t_first")
        t_updated = sig("t_updated", 5)
        tt_updated = sig("tt_updated", 6)
        x_copied = sig("x_copied", 6)
        p1_done = sig("p1_done", 5)
        p2_done = sig("p2_done", 6)
        ks_done = sig("ks_done")
        r_made = sig("r_made")
        a_made = sig("a_made")
        vnew_done = sig("vnew_done")
        vnew_copied = sig("vnew_copied")
        qd_made = sig("qd_made")
        kd_made = sig("kd_made")
        o_done = sig("o_done")
        kv_done = sig("kv_done")
        o_copied = sig("o_copied")
        pair_staged = sig("pair_staged")
        z_done = sig("z_done", 2)
        softplus_made = sig("softplus_made", 2)
        z_copied = sig("z_copied", 2)
        suffix_done = sig("suffix_done", 2)
        weights_made = sig("weights_made", 2)
        pair_done = sig("pair_done")
        pair_lo_made = sig("pair_lo_made")
        gdn_lo_made = sig("gdn_lo_made", GH)
        level_taken = sig("level_taken", 8)
        level_product = sig("level_product", 7)
        diag_product = sig("diag_product")
        kh_made = sig("kh_made")
        kh_turned = sig("kh_turned")
        kh_copied = sig("kh_copied")
        kv1_done = sig("kv1_done")
        states_made = sig("states_made", 4)
        qd1_made = sig("qd1_made")
        o1_done = sig("o1_done")
        o1_copied = sig("o1_copied")
        hg_lo_made = sig("hg_lo_made", HH)
        norm_scaled = sig("norm_scaled")
        ln_centered = sig("ln_centered", KT)
        ln_logged = sig("ln_logged")
        ln_rstd_made = sig("ln_rstd_made")
        ln_scaled = sig("ln_scaled", KT)
        x_hi_made = sig("x_hi_made", KT)
        hidden_squared = sig("hidden_squared", 16)
        hidden_hi_made = sig("hidden_hi_made", 16)
        wg_cleared = sig("wg_cleared")
        conv_tap_added = sig("conv_tap_added", 4)
        qkv_made = sig("qkv_made")
        rate_made = sig("rate_made")
        lb_exp = sig("lb_exp")
        decay_logit_made = sig("decay_logit_made")
        gate_soft = sig("gate_soft", 3)
        norm_applied = sig("norm_applied")
        gb_made = sig("gb_made")
        eg_made = sig("eg_made")
        bb_made = sig("bb_made")
        gdiff_made = sig("gdiff_made")
        col_decay_made = sig("col_decay_made")
        dm_exponent = sig("dm_exponent")
        dm_exp = sig("dm_exp")
        pads_cleared = sig("pads_cleared")
        z_abs = sig("z_abs", 2)
        z_exp = sig("z_exp", 2)
        z_log = sig("z_log", 2)
        logits_made = sig("logits_made", 2)
        pair_hi_made = sig("pair_hi_made")
        norm_gated = sig("norm_gated")
        f_made = sig("f_made")
        logf_made = sig("logf_made")
        v_staged = sig("v_staged")
        eb_made = sig("eb_made")
        level_exp = sig("level_exp", 7)
        kh_exponent = sig("kh_exponent")
        kh_exp = sig("kh_exp")
        ln_shifted = sig("ln_shifted", KT)
        lb_step = sig("lb_step", 9)
        softplus0 = sig("softplus0")
        g_made = sig("g_made")
        gcol_staged = sig("gcol_staged")
        dm_made = sig("dm_made")
        m_first = sig("m_first")
        vb_made = sig("vb_made")
        hg_cleared = sig("hg_cleared")
        k_made = sig("k_made")
        chunk_decay_made = sig("chunk_decay_made")

        block = ctx.enter_context(nc.Block())

        def part(ap, m, which):
            return ap.rearrange("p (b s r) -> p b s r", s=2, r=m)[:, :, which, :]

        def halves(ap):
            return ap.rearrange("p (a t) -> p a t", a=2)

        def pair(m):
            return PS[:, 2 * m:2 * m + 2, 0:HALF]

        @block.sync
        def _(sp_):
            def load_stage(n, u):
                sp_.dma_start(w_raw[:, u, :], wstream[n]).then_inc(w_loaded[u].sem, 16)

            sp_.dma_start(h[:], h_in).then_inc(consts_loaded.sem, 16)
            load_stage(0, 0)
            load_stage(1, 1)
            with sp_.Fori(1, N_STAGES // 2) as i:
                for u in range(2):
                    sp_.wait_ge(w_lo_made.sem, i * 2 + (u - 1))
                    load_stage(i * 2 + u, u)
            for k in range(KT):
                sp_.wait_ge(out_ready.sem, out_ready.at(0, k))
                sp_.dma_start(out[k], h[:, k, N_META:T]).then_inc(out_stored.sem, 16)
            sp_.wait_ge(out_stored.sem, 16 * KT)

        @block.gpsimd
        def _(pool):
            def split(n, u, first, round_):
                pool.wait_ge(w_loaded[u].sem, w_loaded[u].at(round_))
                if not first:
                    pool.wait_ge(stage_done.sem, n - 1)
                pool.sem_inc(pool_waited.sem, 1)
                pool.tensor_scalar(w_hi[:, u, :], w_raw[:, u, :], 1.0, 0.0, ALU.mult, ALU.add).then_inc(w_hi_made.sem, 1)
                pool.wait_ge(w_hi_made.sem, w_hi_made.at(n))
                pool.tensor_tensor(w_lo[:, u, :], w_raw[:, u, :], w_hi[:, u, :].bitcast(F32),
                                   ALU.subtract).then_inc(w_lo_made.sem, 1)

            def split_rounds(a, b):
                with pool.Fori(a, b) as i:
                    for u in range(2):
                        split(i * 2 + u, u, False, i)

            for u in range(2):
                split(u, u, True, 0)
            split_rounds(1, AT["z0"][0] // 2 + 1)

            def mask_levels(i, n):
                pool.wait_ge(m_made.sem, m_made.at(i))
                for l, x in levels(n):
                    if l > 1:
                        pool.wait_ge(x_done.sem, x_done.at(i, l - 2))
                    pool.tensor_tensor(ML[0:n, l % 2, :, 0:n], MT[0:n, :, 0:n], heads(level_mask(n, x), n),
                                       ALU.mult).then_inc(level_masked.sem, 1)

            with pool.Fori(0, N_FULL) as i:
                mask_levels(i, P)
            mask_levels(N_FULL, TAIL)
            split_rounds(AT["z0"][0] // 2 + 1, AT["out1"][0] // 2 + 1)

            with pool.Fori(0, HH) as i:
                pool.wait_ge(b_made.sem, b_made.at(i))
                for l, m in enumerate(LEVELS):
                    w = T if m < TAIL else N_FULL * P
                    first, second = part(bc[:, 0:w], m, 0), part(bc[:, 0:w], m, 1)
                    middle = first[:, :, m - 1:m].broadcast_to((P, w // (2 * m), m))
                    if l > 1:
                        pool.wait_ge(level_scaled.sem, level_scaled.at(i, l - 2))
                    pool.tensor_tensor(part(ee[:, l % 2, 0:w], m, 0), middle, first, ALU.subtract)
                    pool.tensor_tensor(part(ee[:, l % 2, 0:w], m, 1), second, middle,
                                       ALU.subtract).then_inc(level_exponent.sem, 1)
            split_rounds(AT["out1"][0] // 2 + 1, N_STAGES // 2)

        @block.tensor
        def _(pe):
            def stage_fm(n, u, rhs, evacuated, start=True, stop=True):
                pe.wait_ge(w_lo_made.sem, w_lo_made.at(n))
                for m in range(2):
                    if evacuated is not None:
                        pe.wait_ge(evac[m].sem, evacuated)
                    for k in range(KT):
                        w = slice(k * COLS + m * P, k * COLS + m * P + P)
                        hi, lo = rhs(k)
                        for w_part, x_part in ((w_hi, hi), (w_hi, lo), (w_lo, hi)):
                            for j in range(2):
                                mm = pe.matmul(PS[:, 2 * m + j, 0:HALF], w_part[:, u, w],
                                               x_part[:, j * HALF:(j + 1) * HALF],
                                               start=start and k == 0 and w_part is w_hi and x_part is hi,
                                               stop=stop and k == KT - 1 and w_part is w_lo)
                    mm.then_inc((stage_done if m else half_done).sem, 1)

            def x_tile(k):
                return x_hi[:, k, :], x_lo[:, k, :]

            def project(name, rounds, first=0):
                n0, _, e0 = AT[name]
                with pe.Fori(0, rounds) as i:
                    for u in range(2):
                        stage_fm(i * 2 + (n0 + u), u, x_tile, i * 2 + (e0 + u))

            def project_tokens(name, v_done, v_evac, rounds):
                n0 = AT[name][0]
                
                def stage(n, u, since, first):
                    pe.wait_ge(w_lo_made.sem, w_lo_made.at(n))
                    for j in range(5):
                        rows = min(P, T - j * P)
                        if not first:
                            pe.wait_ge(v_evac.sem, v_evac.at(since - 1, j))
                        for k in range(KT):
                            for x_part, w_part in ((x_hi, w_hi), (x_hi, w_lo), (x_lo, w_hi)):
                                mm = pe.matmul(PS[0:rows, j, 0:COLS], x_part[:, k, j * P:j * P + rows],
                                               w_part[:, u, k * COLS:(k + 1) * COLS],
                                               start=k == 0 and x_part is x_hi and w_part is w_hi,
                                               stop=k == KT - 1 and x_part is x_lo)
                        mm.then_inc((stage_done if j == 4 else v_done).sem, 1)

                for m in range(2):
                    pe.wait_ge(evac[m].sem, AT[name][2])
                stage(n0, 0, 0, True)
                stage(n0 + 1, 1, 1, False)
                if rounds > 1:
                    with pe.Fori(1, rounds) as i:
                        for u in range(2):
                            stage(i * 2 + (n0 + u), u, i * 2 + u, False)
                pe.wait_ge(v_evac.sem, v_evac.at(2 * rounds - 1))

            def head_norm_sums(r, sq, weight):
                pe.wait_ge(norm_squared.sem, norm_squared.at(r))
                for a in range(GH):
                    for j in range(2):
                        mm = pe.matmul(PS[:, 2 * a + j, 0:HALF], weight[:, :], sq[:, a, j * HALF:(j + 1) * HALF],
                                       start=True, stop=True)
                mm.then_inc(norm_summed.sem, 1)
                pe.wait_ge(norm_logged.sem, norm_logged.at(r))

            def layer_norm_sums(r, after):
                for m in range(2):
                    pe.wait_ge(evac[m].sem, AT[after][2])
                for j in range(2):
                    for k in range(KT):
                        mm = pe.matmul(PS[:, 4 + j, 0:HALF], ones_d[:, :], h[:, k, j * HALF:(j + 1) * HALF],
                                       start=k == 0, stop=k == KT - 1)
                mm.then_inc(ln_mean_ready.sem, 1)
                for k in range(KT):
                    pe.wait_ge(ln_squared.sem, ln_squared.at(r, k))
                    for j in range(2):
                        mm = pe.matmul(PS[:, 6 + j, 0:HALF], ones_d[:, :], lnsq[:, k % 2, j * HALF:(j + 1) * HALF],
                                       start=k == 0, stop=k == KT - 1)
                    mm.then_inc(ln_square_used.sem, 1)

            def mlp(name, r):
                n0, _, e0 = AT[name]
                for hf in range(2):
                    n1, e1 = n0 + 16 * hf, e0 + 12 * hf
                    with pe.Fori(0, 4) as i:
                        for u in range(2):
                            stage_fm(i * 2 + (n1 + u), u, x_tile, i * 2 + (e1 + u))
                    with pe.Fori(0, 4) as i:
                        for u in range(2):
                            pe.wait_ge(hidden_lo_made.sem, hidden_lo_made.at(r * 2 + hf, 8 * u + 7))
                            stage_fm(i * 2 + (n1 + 8 + u), u,
                                     lambda k: (hid_hi[:, 8 * u + k, :], hid_lo[:, 8 * u + k, :]),
                                     i + (e1 + 8) if u == 0 else None, start=u == 0, stop=u == 1)

            pe.wait_ge(consts_loaded.sem, consts_loaded.at(N_CONST_LOADS - 1))
            pe.wait_ge(consts_made.sem, consts_made.at(0))
            pe.wait_ge(x_lo_made.sem, x_lo_made.at(0))
            project("qkv", 3)

            pe.wait_ge(wgate_loaded.sem, 32)
            for j in range(2):
                for k in range(KT):
                    mm = pe.matmul(PS[0:36, 4 + j, 0:HALF], wg[:, k, :], h[:, k, j * HALF:(j + 1) * HALF],
                                   start=k == 0, stop=k == KT - 1)
            mm.then_inc(gates_done.sem, 1)
            pe.wait_ge(beta_made.sem, beta_made.at(0))
            pe.wait_ge(gcum_made.sem, gcum_made.at(0))
            for c in range(N_FULL + 1):
                n = min(P, T - c * P)
                pe.transpose(PS[0:n, 6, 8 * c:8 * c + 4], beta[:, c * P:c * P + n], ident[0:GH, 0:GH])
                mm = pe.transpose(PS[0:n, 6, 8 * c + 4:8 * c + 8], gcum[:, c * P:c * P + n], ident[0:GH, 0:GH])
            mm.then_inc(columns_done.sem, 1)
            pe.wait_ge(columns_made.sem, columns_made.at(0))
            for m in range(2):
                pe.wait_ge(evac[m].sem, AT["z0"][2])
            head_norm_sums(0, nrm_a, ones)
            head_norm_sums(1, nrm_a, ones)

            def gdn_chunk(i, n, last):
                def each(bank, lhs, rhs, width=P, rows=n, signal=None, start=True, stop=True):
                    for a in range(GH):
                        mm = pe.matmul(PS[0:rows, bank, a * P:a * P + width], lhs(a), rhs(a), start=start, stop=stop)
                    if signal is not None:
                        mm.then_inc(signal.sem, 1)

                pe.wait_ge(gate_rows_staged.sem, gate_rows_staged.at(i))
                each(0, lambda a: sel_of(a), lambda a: gsel[0:GH, 0, 0:n], n, P, decay_rows_done)
                each(1, lambda a: sel_of(a), lambda a: gsel[0:GH, 1, 0:n], n, P, beta_rows_done)
                pe.wait_ge(heads_staged.sem, heads_staged.at(i))
                each(2, lambda a: kS[:, a, 0:n], lambda a: kS[:, a, 0:n], n, n, kk_done)
                each(3, lambda a: kS[:, a, 0:n], lambda a: qS[:, a, 0:n], n, n, qk_done)
                for a in range(GH):
                    mm = pe.transpose(PS[0:n, 4, a * P:(a + 1) * P], kS[:, a, 0:n], ident[:, :])
                mm.then_inc(k_turned.sem, 1)
                pe.wait_ge(state_ready.sem, state_ready.at(i))
                for a in range(GH):
                    mm = pe.transpose(PS[0:n, 5, a * P:(a + 1) * P], vS[:, a, 0:n], ident[:, :])
                mm.then_inc(v_turned.sem, 1)
                pe.wait_ge(tt_first.sem, tt_first.at(i))
                for a in range(GH):
                    mm = pe.transpose(PS[0:n, 6, a * P:a * P + n], TT[0:n, a, 0:n], ident[0:n, 0:n])
                mm.then_inc(t_turned.sem, 1)
                pe.wait_ge(t_first.sem, t_first.at(i))
                last_level = len(levels(n)) - 1
                for l, _ in levels(n):
                    pe.wait_ge(level_masked.sem, level_masked.at(i, l))
                    if l:
                        pe.wait_ge(t_updated.sem, t_updated.at(i, l - 1))
                        pe.wait_ge(tt_updated.sem, tt_updated.at(i, l - 1))
                    each(7, lambda a: ML[0:n, l % 2, a, 0:n], lambda a: TM[0:n, a, 0:n], n, n, x_done)
                    pe.wait_ge(x_copied.sem, x_copied.at(i, l))
                    if l < last_level:
                        each(0, lambda a: TT[0:n, a, 0:n], lambda a: XS[0:n, a, 0:n], n, n, p1_done)
                    each(1, lambda a: XS[0:n, a, 0:n], lambda a: TT[0:n, a, 0:n], n, n, p2_done)
                pe.wait_ge(tt_updated.sem, tt_updated.at(i, last_level))
                each(2, lambda a: kS[:, a, 0:n], lambda a: SS[:, a, :], P, n, ks_done)
                pe.wait_ge(r_made.sem, r_made.at(i))
                pe.wait_ge(a_made.sem, a_made.at(i))
                each(3, lambda a: TT[0:n, a, 0:n], lambda a: RR[0:n, a, :], P, n, vnew_done)
                pe.wait_ge(vnew_copied.sem, vnew_copied.at(i))
                pe.wait_ge(qd_made.sem, qd_made.at(i))
                pe.wait_ge(kd_made.sem, kd_made.at(i))
                for a in range(GH):
                    pe.matmul(PS[:, 4, a * P:a * P + n], VN[0:n, a, :], AT0[0:n, a, 0:n], start=True, stop=False)
                    mm = pe.matmul(PS[:, 4, a * P:a * P + n], SS[:, a, :], qS[:, a, 0:n], start=False, stop=True)
                mm.then_inc(o_done.sem, 1)
                if not last:
                    each(5, lambda a: KD[0:n, a, :], lambda a: VN[0:n, a, :], P, P, kv_done)
                    pe.wait_ge(o_copied.sem, o_copied.at(i))

            with pe.Fori(0, N_FULL) as i:
                gdn_chunk(i, P, False)
            gdn_chunk(N_FULL, TAIL, True)
            pe.wait_ge(o_copied.sem, o_copied.at(N_FULL))

            project("z0", 1)
            project("qk", 2)
            project_tokens("v0", v_tile_done0, v_evacuated0, 1)

            with pe.Fori(0, SH // 2) as i:
                pe.wait_ge(pair_staged.sem, pair_staged.at(i))
                for a in range(2):
                    rows = slice(a * SD, (a + 1) * SD)
                    for j, q0, cnt, col in Z_PARTS:
                        bank, c = z_where(col)
                        diag = q0 == j * P
                        mm = pe.matmul(PS[:, 3 * a + bank, c:c + cnt], sq_k[rows, j * P:(j + 1) * P],
                                       sq_q[rows, q0:q0 + cnt], start=True, stop=not diag)
                        if diag:
                            w = min(P, cnt)
                            mm = pe.matmul(PS[:, 3 * a + bank, c:c + w], ident_b[:, :], neg_b[:, 0:w],
                                           start=False, stop=True)
                    mm.then_inc(z_done.sem, 1)
                for a in range(2):
                    pe.wait_ge(softplus_made.sem, softplus_made.at(i, a))
                    pe.wait_ge(z_copied.sem, z_copied.at(i, a))
                    for j, q0, cnt, col in Z_PARTS:
                        bank, c = z_where(col)
                        later = [(r, q, m) for jj in range(j + 1, 5) for r, q, m in z_runs(jj, q0, q0 + cnt)]
                        mm = pe.matmul(PS[:, 3 * a + bank, c:c + cnt], suffix[:, :], sp[:, a, col:col + cnt],
                                       start=True, stop=not later)
                        for x, (r, q, m) in enumerate(later):
                            mm = pe.matmul(PS[:, 3 * a + bank, c + q - q0:c + q - q0 + m], ones[:, :],
                                           sp[:, a, r:r + m], start=False, stop=x == len(later) - 1)
                    mm.then_inc(suffix_done.sem, 1)
                for a in range(2):
                    pe.wait_ge(weights_made.sem, weights_made.at(i, a))
                    rows = slice(a * SD, (a + 1) * SD)
                    for bank, qa, qb in ((6, 0, 512), (7, 512, T)):
                        runs = [(j, r, q, m) for j in range(5) for r, q, m in z_runs(j, qa, qb)]
                        for x, (j, r, q, m) in enumerate(runs):
                            mm = pe.matmul(PS[rows, bank, q - qa:q - qa + m], sq_v[:, j, rows], zs[:, a, r:r + m],
                                           start=x == 0, stop=x == len(runs) - 1)
                mm.then_inc(pair_done.sem, 1)
                pe.wait_ge(pair_lo_made.sem, pair_lo_made.at(i))

            head_norm_sums(2, nrm_b, ones_h)
            pe.wait_ge(gdn_lo_made.sem, gdn_lo_made.at(0))
            project("out0", 2)
            layer_norm_sums(0, "mlp0")
            pe.wait_ge(x_lo_made.sem, x_lo_made.at(1))
            mlp("mlp0", 0)
            layer_norm_sums(1, "f")
            pe.wait_ge(x_lo_made.sem, x_lo_made.at(2))

            project("f", 2)
            project_tokens("v1", v_tile_done1, v_evacuated1, 2)
            project("q1", 2)
            project("z1", 2)
            for m in range(2):
                pe.wait_ge(evac[m].sem, AT["out1"][2])

            with pe.Fori(0, HH) as i:
                for l, m in enumerate(LEVELS):
                    pe.wait_ge(level_scaled.sem, level_scaled.at(i, l))
                    if l > 1:
                        pe.wait_ge(level_taken.sem, level_taken.at(i, l - 2))
                    bank = l % 2
                    if m < TAIL:
                        pe.matmul(PS[:, bank, 256:264], kt[:, l % 2, 512:640],
                                  part(qt[:, l % 2, 512:T], m, 1), start=True, stop=True)
                    for c in range(N_FULL):
                        mm = pe.matmul(PS[:, bank, 64 * c:64 * c + 64], kt[:, l % 2, c * P:(c + 1) * P],
                                       part(qt[:, l % 2, c * P:(c + 1) * P], m, 1),
                                       start=True, stop=True)
                    mm.then_inc(level_product.sem, 1)
                for c in range(N_FULL):
                    pe.matmul(PS[:, 2, c * P:(c + 1) * P], kg[:, c * P:(c + 1) * P], q1[:, i, c * P:(c + 1) * P],
                              start=True, stop=True)
                mm = pe.matmul(PS[0:TAIL, 3, 0:TAIL], kg[:, 512:T], q1[:, i, 512:T], start=True, stop=True)
                mm.then_inc(diag_product.sem, 1)
                pe.wait_ge(kh_made.sem, kh_made.at(i))
                for c in range(N_FULL):
                    mm = pe.transpose(PS[:, 4, c * P:(c + 1) * P], ee[:, 0, c * P:(c + 1) * P], ident[:, :])
                mm.then_inc(kh_turned.sem, 1)
                pe.wait_ge(kh_copied.sem, kh_copied.at(i))
                for c in range(N_FULL):
                    mm = pe.matmul(PS[:, 5, c * P:(c + 1) * P], khT[:, c, :], vh[:, c, :], start=True, stop=True)
                mm.then_inc(kv1_done.sem, 1)
                pe.wait_ge(states_made.sem, states_made.at(i))
                pe.wait_ge(qd1_made.sem, qd1_made.at(i))
                pe.wait_ge(level_taken.sem, level_taken.at(i, 7))
                for c in range(N_FULL + 1):
                    n = min(P, T - c * P)
                    dst = PS[:, 6, c * P:c * P + n] if c < N_FULL else PS[:, 7, 0:n]
                    mm = pe.matmul(dst, vh[0:n, c, :], aT[0:n, c * P:c * P + n], start=True, stop=c == 0)
                    if c:
                        mm = pe.matmul(dst, s1[:, c - 1, :], eb[:, c * P:c * P + n], start=False, stop=True)
                mm.then_inc(o1_done.sem, 1)
                pe.wait_ge(o1_copied.sem, o1_copied.at(i))

            for g in range(2):
                head_norm_sums(3 + g, nrm_c, ones_h)
            pe.wait_ge(hg_lo_made.sem, hg_lo_made.at(0))
            project("out1", 2)
            layer_norm_sums(2, "mlp1")
            pe.wait_ge(x_lo_made.sem, x_lo_made.at(3))
            mlp("mlp1", 1)
            layer_norm_sums(3, "end")

        @block.scalar
        def _(act):
            def hold():
                act.sem_inc(act_waited.sem, 1)

            def from_tile(m, n, f, dst, func):
                act.wait_ge(tile_done[m].sem, (n if m else f) + 1)
                hold()
                act.activation(halves(dst), pair(m), func).then_inc(evac[m].sem, 1)

            def evacuate(name, rounds, dst, func):
                n0, f0, _ = AT[name]
                with act.Fori(0, rounds) as i:
                    for u in range(2):
                        for m in range(2):
                            from_tile(m, i * 2 + (n0 + u), i * 2 + (f0 + u), dst[:, i * 4 + (2 * u + m), :], func)

            def evacuate_tokens(name, v_done, v_evac, rounds, dst):
                n0 = AT[name][0]
                with act.Fori(0, rounds) as i:
                    for u in range(2):
                        for j in range(5):
                            rows = min(P, T - j * P)
                            if j < 4:
                                act.wait_ge(v_done.sem, v_done.at(i * 2 + u, j))
                            else:
                                act.wait_ge(stage_done.sem, i * 2 + (n0 + u + 1))
                            hold()
                            act.activation(dst[0:rows, j, bass.ds(i * (2 * COLS) + u * COLS, COLS)],
                                           PS[0:rows, j, 0:COLS],
                                           ACT.Copy).then_inc(v_evac.sem, 1)

            def head_norm(r, src, buf):
                act.activation(buf[:, :, :], src, ACT.Square).then_inc(norm_squared.sem, 1)
                act.wait_ge(norm_summed.sem, norm_summed.at(r))
                sums = PS[:, :, 0:HALF]
                act.activation(buf[:, :, :].rearrange("p h (a t) -> p (h a) t", a=2), sums, ACT.Ln,
                               bias=eps_rms).then_inc(norm_logged.sem, 1)
                act.wait_ge(norm_logged.sem, norm_logged.at(r))
                act.activation(buf[:, :, :], buf[:, :, :], ACT.Exp, scale=-0.5).then_inc(norm_scaled.sem, 1)

            def layer_norm(r):
                for k in range(KT):
                    act.wait_ge(ln_centered.sem, ln_centered.at(r, k))
                    if k > 1:
                        act.wait_ge(ln_square_used.sem, ln_square_used.at(r, k - 2))
                    act.activation(lnsq[:, k % 2, :], h[:, k, :], ACT.Square).then_inc(ln_squared.sem, 1)
                act.wait_ge(ln_square_used.sem, ln_square_used.at(r))
                act.activation(halves(rstd[:, :]), PS[:, 6:8, 0:HALF], ACT.Ln, bias=eps_ln).then_inc(ln_logged.sem, 1)
                act.wait_ge(ln_logged.sem, ln_logged.at(r))
                act.activation(rstd[:, :], rstd[:, :], ACT.Exp, scale=-0.5).then_inc(ln_rstd_made.sem, 1)
                if r == 3:
                    return
                for k in range(KT):
                    act.wait_ge(ln_scaled.sem, ln_scaled.at(r, k))
                    col = P_LNB + r * KT + k
                    act.activation(x_hi[:, k, :], h[:, k, :], ACT.Identity,
                                   bias=par[:, col:col + 1]).then_inc(x_hi_made.sem, 1)

            def mlp(name, r):
                n0, f0, _ = AT[name]
                for hf in range(2):
                    with act.Fori(0, 4) as i:
                        for u in range(2):
                            for m in range(2):
                                t = i * 4 + (2 * u + m)
                                from_tile(m, i * 2 + (n0 + 16 * hf + u), i * 2 + (f0 + 16 * hf + u), relu[:, m, :], ACT.Relu)
                                act.wait_ge(hidden_squared.sem, hidden_squared.at(r * 2 + hf, t))
                                hold()
                                act.activation(hid_hi[:, t, :], sqr[:, m, :],
                                               ACT.Copy).then_inc(hidden_hi_made.sem, 1)

            for dst, src in ((con[:], consts[:, P:]), (ident[:], consts[:, 0:P]), (mask_in, hmasks),
                             (par[:], params), (gp[:, 0:2], gate_params)):
                act.dma_start(dst, src).then_inc(consts_loaded.sem, 16)
            act.wait_ge(wg_cleared.sem, wg_cleared.at(0))
            act.dma_start(wg[:, :, 0:GH], wgate[0]).then_inc(wgate_loaded.sem, 16)
            act.dma_start(wg[:, :, 32:32 + GH], wgate[1]).then_inc(wgate_loaded.sem, 16)
            act.wait_ge(consts_loaded.sem, consts_loaded.at(N_CONST_LOADS - 1))
            for k in range(KT):
                act.activation(x_hi[:, k, :], h[:, k, :], ACT.Copy).then_inc(x_hi_made.sem, 1)

            act.wait_ge(consts_made.sem, consts_made.at(0))
            n0, f0, _ = AT["qkv"]
            with act.Fori(0, 3) as i:
                for u in range(2):
                    for m in range(2):
                        from_tile(m, i * 2 + (n0 + u), i * 2 + (f0 + u), conv_in[:, m, 3:3 + T], ACT.Copy)
                        act.wait_ge(conv_tap_added.sem, conv_tap_added.at(i * 4 + (2 * u + m)))
                        hold()
                        act.activation(qkv[:, i * 4 + (2 * u + m), :], conv_acc[:, m, :], ACT.Silu).then_inc(qkv_made.sem, 1)
            act.wait_ge(gates_done.sem, gates_done.at(0))
            act.activation(halves(beta[:, :]), PS[0:GH, 4:6, 0:HALF], ACT.Sigmoid).then_inc(beta_made.sem, 1)
            act.preload_act_table_set(EXP_LN)
            act.activation(gp[:, 2:3], gp[:, 0:1], ACT.Exp).then_inc(rate_made.sem, 1)
            act.activation(lbt[:, 6, :], lbt[:, 3, :], ACT.Exp)
            act.activation(lbt[:, 7, :], lbt[:, 4, :], ACT.Exp).then_inc(lb_exp.sem, 1)
            act.wait_ge(decay_logit_made.sem, decay_logit_made.at(0))
            act.activation(gtmp[:, 1, :], gtmp[:, 0, :], ACT.Abs).then_inc(gate_soft.sem, 1)
            act.wait_ge(gate_soft.sem, gate_soft.at(0, 0))
            act.activation(gtmp[:, 1, :], gtmp[:, 1, :], ACT.Exp, scale=-1.0).then_inc(gate_soft.sem, 1)
            act.wait_ge(gate_soft.sem, gate_soft.at(0, 1))
            act.activation(gtmp[:, 1, :], gtmp[:, 1, :], ACT.Ln, bias=small[0:GH, 2:3]).then_inc(gate_soft.sem, 1)
            act.wait_ge(columns_done.sem, columns_done.at(0))
            full = PS[:, 6, 0:8 * N_FULL].rearrange("p (c w h) -> p c w h", c=N_FULL, w=2)
            act.activation(colg[:, 0:N_FULL, :, :], full, ACT.Copy)
            act.activation(colg[0:TAIL, N_FULL, :, :], PS[0:TAIL, 6, 8 * N_FULL:8 * N_FULL + 8].rearrange("p (w h) -> p w h", w=2),
                           ACT.Copy).then_inc(columns_made.sem, 1)
            act.wait_ge(qkv_made.sem, qkv_made.at(11))
            head_norm(0, qkv[:, 0:GH, :], nrm_a)
            act.wait_ge(norm_applied.sem, norm_applied.at(0))
            head_norm(1, qkv[:, GH:2 * GH, :], nrm_a)
            act.wait_ge(norm_applied.sem, norm_applied.at(1))

            def gdn_chunk(i, n, last):
                cols = bass.ds(i * P, n)
                act.activation(gsel[:, 0, 0:n], gcum[:, cols], ACT.Copy)
                act.activation(gsel[:, 1, 0:n], beta[:, cols], ACT.Copy).then_inc(gate_rows_staged.sem, 1)
                for g, dst in ((1, kS), (0, qS), (2, vS)):
                    ins = act.activation(dst[:, :, 0:n], qkv[:, g * GH:(g + 1) * GH, cols], ACT.Copy)
                ins.then_inc(heads_staged.sem, 1)
                act.wait_ge(decay_rows_done.sem, decay_rows_done.at(i))
                rows = PS[:, 0, :].rearrange("p (h t) -> p h t", h=GH)[:, :, 0:n]
                act.activation(GB[:, :, 0:n], rows, ACT.Copy).then_inc(gb_made.sem, 1)
                act.wait_ge(state_ready.sem, state_ready.at(i))
                act.activation(EG[:, :, 0:n], rows, ACT.Exp).then_inc(eg_made.sem, 1)
                act.wait_ge(beta_rows_done.sem, beta_rows_done.at(i))
                rows = PS[:, 1, :].rearrange("p (h t) -> p h t", h=GH)[:, :, 0:n]
                act.activation(BB[:, :, 0:n], rows, ACT.Copy).then_inc(bb_made.sem, 1)
                act.wait_ge(gdiff_made.sem, gdiff_made.at(i))
                act.activation(kd4[0:n], gdiff[0:n], ACT.Exp, scale=-1.0)
                act.activation(eg4[0:n], gcol[0:n], ACT.Exp).then_inc(col_decay_made.sem, 1)
                act.wait_ge(dm_exponent.sem, dm_exponent.at(i))
                act.activation(DM[0:n, :, 0:n], DM[0:n, :, 0:n], ACT.Exp).then_inc(dm_exp.sem, 1)
                act.wait_ge(t_turned.sem, t_turned.at(i))
                bank = [PS[0:n, b, :].rearrange("p (h t) -> p h t", h=GH) for b in range(8)]
                act.activation(TM[0:n, :, 0:n], bank[6][:, :, 0:n], ACT.Copy).then_inc(t_first.sem, 1)
                for l, _ in levels(n):
                    act.wait_ge(x_done.sem, x_done.at(i, l))
                    act.activation(XS[0:n, :, 0:n], bank[7][:, :, 0:n], ACT.Copy).then_inc(x_copied.sem, 1)
                act.wait_ge(vnew_done.sem, vnew_done.at(i))
                act.activation(VN[0:n, :, :], bank[3], ACT.Copy).then_inc(vnew_copied.sem, 1)
                act.wait_ge(o_done.sem, o_done.at(i))
                o = PS[:, 4, :].rearrange("p (h t) -> p h t", h=GH)[:, :, 0:n]
                hold()
                act.activation(qkv[:, 0:GH, cols], o, ACT.Copy).then_inc(o_copied.sem, 1)

            with act.Fori(0, N_FULL) as i:
                gdn_chunk(i, P, False)
            gdn_chunk(N_FULL, TAIL, True)

            evacuate("z0", 1, z0, ACT.Silu)
            evacuate("qk", 2, qk, ACT.Copy)
            act.wait_ge(pads_cleared.sem, pads_cleared.at(0))
            evacuate_tokens("v0", v_tile_done0, v_evacuated0, 1, vt)
            act.preload_act_table_set(EXP_LN)
            with act.Fori(0, SH // 2) as i:
                act.activation(sq_k[:, 0:T], qk[:, i + GH, :], ACT.Copy)
                act.activation(sq_q[:, 0:T], qk[:, i, :], ACT.Copy)
                act.activation(sq_v[:, :, :], vt[:, :, bass.ds(i * P, P)], ACT.Copy).then_inc(pair_staged.sem, 1)
                for a in range(2):
                    act.wait_ge(z_copied.sem, z_copied.at(i, a))
                    act.activation(sp[:, a, :], zs[:, a, :], ACT.Abs).then_inc(z_abs.sem, 1)
                    act.wait_ge(z_abs.sem, z_abs.at(i, a))
                    act.activation(sp[:, a, :], sp[:, a, :], ACT.Exp, scale=-1.0).then_inc(z_exp.sem, 1)
                    act.wait_ge(z_exp.sem, z_exp.at(i, a))
                    act.activation(sp[:, a, :], sp[:, a, :], ACT.Ln, bias=small[:, 2:3]).then_inc(z_log.sem, 1)
                for a in range(2):
                    act.wait_ge(logits_made.sem, logits_made.at(i, a))
                    act.activation(zs[:, a, :], zs[:, a, :], ACT.Exp).then_inc(weights_made.sem, 1)
                act.wait_ge(pair_done.sem, pair_done.at(i))
                hold()
                act.activation(x_hi[:, i + GH, 0:512], PS[:, 6, :], ACT.Copy)
                act.activation(x_hi[:, i + GH, 512:T], PS[:, 7, 0:TAIL], ACT.Copy).then_inc(pair_hi_made.sem, 1)

            def gate(r, buf, base, hi_made, lo_made, g):
                act.wait_ge(norm_gated.sem, norm_gated.at(r - 2))
                for a in range(GH):
                    act.activation(x_hi[:, base + a, :], buf[:, a, :], ACT.Copy).then_inc(hi_made.sem, 1)
                act.wait_ge(lo_made.sem, lo_made.at(0, g * GH + GH - 1))

            act.wait_ge(o_copied.sem, o_copied.at(N_FULL))
            head_norm(2, qkv[:, 0:GH, :], nrm_b)
            gate(2, nrm_b, 0, gdn_hi_made, gdn_lo_made, 0)
            layer_norm(0)
            mlp("mlp0", 0)
            act.preload_act_table_set(EXP_LN)
            layer_norm(1)

            evacuate("f", 2, fg, ACT.Sigmoid)
            evacuate_tokens("v1", v_tile_done1, v_evacuated1, 2, v1)
            evacuate("q1", 2, q1, ACT.Silu)
            evacuate("z1", 2, z1, ACT.Silu)
            act.preload_act_table_set(EXP_LN)
            act.wait_ge(f_made.sem, f_made.at(HH - 1))
            with act.Fori(0, HH) as i:
                act.activation(ee[:, 0, :], fg[:, i, :], ACT.Ln).then_inc(logf_made.sem, 1)
                act.activation(vh[:, 0:N_FULL, :], v1[:, 0:N_FULL, bass.ds(i * P, P)], ACT.Copy)
                act.activation(vh[0:TAIL, N_FULL, :], v1[0:TAIL, N_FULL, bass.ds(i * P, P)], ACT.Copy).then_inc(v_staged.sem, 1)
                act.wait_ge(b_made.sem, b_made.at(i))
                act.activation(eb[:, :], bc[:, :], ACT.Exp).then_inc(eb_made.sem, 1)
                for l, m in enumerate(LEVELS):
                    w = T if m < TAIL else N_FULL * P
                    act.wait_ge(level_exponent.sem, level_exponent.at(i, l))
                    act.activation(ee[:, l % 2, 0:w], ee[:, l % 2, 0:w], ACT.Exp).then_inc(level_exp.sem, 1)
                act.wait_ge(kh_exponent.sem, kh_exponent.at(i))
                act.activation(ee[:, 1, 0:512], ee[:, 1, 0:512], ACT.Exp, scale=-1.0).then_inc(kh_exp.sem, 1)
                act.wait_ge(kh_turned.sem, kh_turned.at(i))
                act.activation(khT[:, :, :], PS[:, 4, :].rearrange("p (c t) -> p c t", c=4), ACT.Copy).then_inc(kh_copied.sem, 1)
                act.wait_ge(o1_done.sem, o1_done.at(i))
                hold()
                act.activation(fg[:, i, 0:512], PS[:, 6, :], ACT.Copy)
                act.activation(fg[:, i, 512:T], PS[:, 7, 0:TAIL], ACT.Copy).then_inc(o1_copied.sem, 1)
            act.wait_ge(o1_copied.sem, o1_copied.at(HH - 1))
            for g in range(2):
                head_norm(3 + g, fg[:, g * GH:(g + 1) * GH, :], nrm_c)
                gate(3 + g, nrm_c, g * GH, hg_hi_made, hg_lo_made, g)
            layer_norm(2)
            mlp("mlp1", 1)
            act.preload_act_table_set(EXP_LN)
            layer_norm(3)

        @block.vector
        def _(dve):
            def hold():
                dve.sem_inc(dve_waited.sem, 1)

            def head_norm(r, src, buf, scale):
                dve.wait_ge(norm_scaled.sem, norm_scaled.at(r))
                dve.scalar_tensor_tensor(src, src, scale, buf[:, :, :], ALU.mult, ALU.mult).then_inc(norm_applied.sem, 1)

            def gate(r, src, buf, z, gain, base, hi_made, lo_made):
                dve.wait_ge(norm_scaled.sem, norm_scaled.at(r))
                dve.scalar_tensor_tensor(buf[:, :, :], src, gain, buf[:, :, :], ALU.mult, ALU.mult).then_inc(norm_applied.sem, 1)
                dve.wait_ge(norm_applied.sem, norm_applied.at(r))
                dve.tensor_tensor(buf[:, :, :], buf[:, :, :], z, ALU.mult).then_inc(norm_gated.sem, 1)
                dve.wait_ge(norm_gated.sem, norm_gated.at(r - 2))
                for a in range(GH):
                    dve.wait_ge(hi_made.sem, hi_made.at(0, base + a))
                    dve.tensor_tensor(x_lo[:, base + a, :], buf[:, a, :], x_hi[:, base + a, :].bitcast(F32),
                                      ALU.subtract).then_inc(lo_made.sem, 1)

            def add_residual(m, n, f, tile, scale):
                dve.wait_ge(tile_done[m].sem, (n if m else f) + 1)
                hold()
                dve.scalar_tensor_tensor(halves(h[:, tile, :]), halves(h[:, tile, :]), scale, pair(m),
                                         ALU.mult, ALU.add).then_inc(evac[m].sem, 1)

            def out_projection(name):
                n0, f0, _ = AT[name]
                with dve.Fori(0, 2) as i:
                    for u in range(2):
                        for m in range(2):
                            add_residual(m, i * 2 + (n0 + u), i * 2 + (f0 + u), i * 4 + (2 * u + m), ALPHA)

            def layer_norm(r, after):
                for m in range(2):
                    dve.wait_ge(evac[m].sem, AT[after][2])
                dve.wait_ge(ln_mean_ready.sem, ln_mean_ready.at(r))
                for k in range(KT):
                    dve.tensor_tensor(halves(h[:, k, :]), halves(h[:, k, :]), PS[:, 4:6, 0:HALF],
                                      ALU.subtract).then_inc(ln_centered.sem, 1)
                dve.wait_ge(ln_rstd_made.sem, ln_rstd_made.at(r))
                dve.wait_ge(ln_centered.sem, ln_centered.at(r))
                for k in range(KT):
                    gain = par[:, P_LNG + r * KT + k:P_LNG + r * KT + k + 1]
                    dve.scalar_tensor_tensor(h[:, k, :], h[:, k, :], gain, rstd[:, :],
                                             ALU.mult, ALU.mult).then_inc(ln_scaled.sem, 1)
                for k in range(KT):
                    shift = par[:, P_LNB + r * KT + k:P_LNB + r * KT + k + 1]
                    dve.wait_ge(ln_scaled.sem, ln_scaled.at(r, k))
                    if r < 3:
                        dve.wait_ge(x_hi_made.sem, x_hi_made.at(r + 1, k))
                        dve.scalar_tensor_tensor(x_lo[:, k, :], h[:, k, :], shift, x_hi[:, k, :].bitcast(F32),
                                                 ALU.add, ALU.subtract).then_inc(x_lo_made.sem, 1)
                    done = ln_shifted if r < 3 else out_ready
                    dve.tensor_scalar(h[:, k, :], h[:, k, :], shift, None, ALU.add).then_inc(done.sem, 1)
                if r < 3:
                    dve.wait_ge(ln_shifted.sem, ln_shifted.at(r))

            def mlp(name, r):
                n0, f0, e0 = AT[name]
                for hf in range(2):
                    n1, f1, e1, rr = n0 + 16 * hf, f0 + 16 * hf, e0 + 12 * hf, r * 2 + hf
                    with dve.Fori(0, 4) as i:
                        for u in range(2):
                            for m in range(2):
                                t = i * 4 + (2 * u + m)
                                dve.wait_ge(evac[m].sem, i * 2 + (e1 + u + 1))
                                dve.tensor_tensor(sqr[:, m, :], relu[:, m, :], relu[:, m, :],
                                                  ALU.mult).then_inc(hidden_squared.sem, 1)
                                dve.wait_ge(hidden_hi_made.sem, hidden_hi_made.at(rr, t))
                                dve.wait_ge(hidden_squared.sem, hidden_squared.at(rr, t))
                                dve.tensor_tensor(hid_lo[:, t, :], sqr[:, m, :], hid_hi[:, t, :].bitcast(F32),
                                                  ALU.subtract).then_inc(hidden_lo_made.sem, 1)
                    with dve.Fori(0, 4) as i:
                        for m in range(2):
                            add_residual(m, i * 2 + (n1 + 9), i * 2 + (f1 + 9), i * 2 + m, ALPHA if hf == 0 else 1.0)
                    if hf == 0:
                        for m in range(2):
                            dve.wait_ge(evac[m].sem, AT[name][2] + 12)

            dve.memset(wg[:, :, :], 0.0).then_inc(wg_cleared.sem, 1)
            dve.memset(ones[:, :], 1.0)
            dve.memset(ones_d[:, :], 1.0 / D)
            dve.memset(ones_h[:, :], 1.0 / P)
            dve.memset(small[:, 0:1], LN_EPS)
            dve.memset(small[:, 1:2], RMS_EPS)
            dve.memset(small[:, 2:3], 1.0)
            dve.memset(conv_in[:, :, 0:3], 0.0)
            dve.wait_ge(consts_loaded.sem, consts_loaded.at(N_CONST_LOADS - 1))
            dve.tensor_copy(hmask[:, :, :], mask_in)
            dve.tensor_copy(ident_b[:, :], ident[:, :]).then_inc(evac[0].sem, 1)
            dve.tensor_copy(neg_b[:, :], con[:, C_NEG:C_NEG + P]).then_inc(evac[1].sem, 1)
            raw0, raw1 = par[:, P_LB:P_LB + HH], par[:, P_LB + HH:P_LB + 2 * HH]
            L = [lbt[:, x, :] for x in range(8)]
            lbs = lb_step
            dve.tensor_tensor(L[2], raw0, raw1, ALU.max).then_inc(lbs.sem, 1)
            dve.wait_ge(lbs.sem, lbs.at(0, 0))
            dve.tensor_tensor(L[3], raw0, L[2], ALU.subtract)
            dve.tensor_tensor(L[4], raw1, L[2], ALU.subtract).then_inc(consts_made.sem, 1)
            for k in range(KT):
                dve.wait_ge(x_hi_made.sem, x_hi_made.at(0, k))
                dve.tensor_tensor(x_lo[:, k, :], h[:, k, :], x_hi[:, k, :].bitcast(F32),
                                  ALU.subtract).then_inc(x_lo_made.sem, 1)

            e0 = AT["qkv"][2]
            with dve.Fori(0, 3) as i:
                for u in range(2):
                    for m in range(2):
                        q = i * 4 + (2 * u + m)
                        dve.wait_ge(evac[m].sem, i * 2 + (e0 + u + 1))
                        hold()
                        for tap in range(4):
                            weight = par[:, bass.ds(q * 4 + (P_CONV + tap), 1)]
                            x = conv_in[:, m, tap:tap + T]
                            if tap == 0:
                                ins = dve.tensor_scalar(conv_acc[:, m, :], x, weight, None, ALU.mult)
                            else:
                                dve.wait_ge(conv_tap_added.sem, conv_tap_added.at(q, tap - 1))
                                ins = dve.scalar_tensor_tensor(conv_acc[:, m, :], x, weight, conv_acc[:, m, :],
                                                               ALU.mult, ALU.add)
                            ins.then_inc(conv_tap_added.sem, 1)

            dve.wait_ge(gates_done.sem, gates_done.at(0))
            dve.tensor_scalar(halves(gtmp[:, 0, :]), PS[32:32 + GH, 4:6, 0:HALF], gp[:, 1:2], None,
                              ALU.add).then_inc(decay_logit_made.sem, 1)
            dve.wait_ge(gate_soft.sem, gate_soft.at(0))
            dve.wait_ge(decay_logit_made.sem, decay_logit_made.at(0))
            dve.scalar_tensor_tensor(gtmp[:, 2, :], gtmp[:, 0, :], 0.0, gtmp[:, 1, :], ALU.max, ALU.add).then_inc(softplus0.sem, 1)
            dve.wait_ge(softplus0.sem, softplus0.at(0))
            dve.wait_ge(rate_made.sem, rate_made.at(0))
            dve.tensor_scalar(gtmp[:, 0, :], gtmp[:, 2, :], gp[:, 2:3], -1.0, ALU.mult, ALU.mult).then_inc(g_made.sem, 1)
            dve.wait_ge(g_made.sem, g_made.at(0))
            for c in range(N_FULL + 1):
                n = min(P, T - c * P)
                dve.tensor_tensor_scan(gcum[:, c * P:c * P + n], ones[0:GH, 0:n], gtmp[:, 0, c * P:c * P + n], 0.0,
                                       ALU.mult, ALU.add).then_inc(gcum_made.sem, 1)
            head_norm(0, qkv[:, 0:GH, :], nrm_a, P ** -0.5)
            head_norm(1, qkv[:, GH:2 * GH, :], nrm_a, 1.0)
            dve.wait_ge(norm_applied.sem, norm_applied.at(1))
            dve.memset(SS[:, :, :], 0.0).then_inc(state_ready.sem, 1)

            def gdn_chunk(i, n, last):
                bank = [PS[0:n, b, :].rearrange("p (h t) -> p h t", h=GH) for b in range(8)]
                dve.tensor_copy(gcol[0:n], colg[0:n, i, 1, :])
                dve.tensor_copy(bcol[0:n], colg[0:n, i, 0, :]).then_inc(gcol_staged.sem, 1)
                dve.wait_ge(gb_made.sem, gb_made.at(i))
                dve.wait_ge(gcol_staged.sem, gcol_staged.at(i))
                dve.tensor_tensor(gdiff[0:n], gcol[0:n], GB[0:n, :, n - 1], ALU.subtract).then_inc(gdiff_made.sem, 1)
                for a in range(GH):
                    ins = dve.tensor_scalar(DM[0:n, a, 0:n], GB[0:n, a, 0:n], gcol[0:n, a:a + 1], 0.0, ALU.subtract, ALU.min)
                ins.then_inc(dm_exponent.sem, 1)
                dve.wait_ge(dm_exp.sem, dm_exp.at(i))
                dve.tensor_tensor(DM[0:n, :, 0:n], DM[0:n, :, 0:n], heads(ge_mask[0:n, 0:n], n), ALU.mult).then_inc(dm_made.sem, 1)
                dve.wait_ge(kk_done.sem, kk_done.at(i))
                dve.wait_ge(dm_made.sem, dm_made.at(i))
                dve.tensor_tensor(MT[0:n, :, 0:n], bank[2][:, :, 0:n], DM[0:n, :, 0:n], ALU.mult).then_inc(m_made.sem, 1)
                dve.wait_ge(m_made.sem, m_made.at(i, 0))
                dve.wait_ge(bb_made.sem, bb_made.at(i))
                dve.tensor_tensor(MT[0:n, :, 0:n], MT[0:n, :, 0:n], BB[0:n, :, 0:n], ALU.mult).then_inc(m_made.sem, 1)
                dve.wait_ge(m_made.sem, m_made.at(i, 1))
                dve.tensor_tensor(XS[0:n, :, 0:n], MT[0:n, :, 0:n], heads(level_mask(n, 0), n), ALU.mult).then_inc(m_first.sem, 1)
                dve.wait_ge(m_first.sem, m_first.at(i))
                dve.tensor_tensor(TT[0:n, :, 0:n], heads(ident[0:n, 0:n], n), XS[0:n, :, 0:n], ALU.subtract).then_inc(tt_first.sem, 1)
                dve.wait_ge(qk_done.sem, qk_done.at(i))
                dve.tensor_tensor(AT0[0:n, :, 0:n], bank[3][:, :, 0:n], DM[0:n, :, 0:n], ALU.mult).then_inc(a_made.sem, 1)
                dve.wait_ge(col_decay_made.sem, col_decay_made.at(i))
                dve.wait_ge(k_turned.sem, k_turned.at(i))
                for a in range(GH):
                    ins = dve.tensor_scalar(KD[0:n, a, :], bank[4][:, a, :], kd4[0:n, a:a + 1], None, ALU.mult)
                ins.then_inc(kd_made.sem, 1)
                dve.wait_ge(v_turned.sem, v_turned.at(i))
                for a in range(GH):
                    dve.tensor_scalar(VB[0:n, a, :], bank[5][:, a, :], bcol[0:n, a:a + 1], None, ALU.mult)
                dve.scalar_tensor_tensor(nb4[0:n], eg4[0:n], -1.0, bcol[0:n], ALU.mult, ALU.mult).then_inc(vb_made.sem, 1)
                dve.wait_ge(eg_made.sem, eg_made.at(i))
                dve.tensor_tensor(qS[:, :, 0:n], qS[:, :, 0:n], EG[:, :, 0:n], ALU.mult).then_inc(qd_made.sem, 1)
                lv = levels(n)
                for l, _ in lv:
                    if l < len(lv) - 1:
                        dve.wait_ge(p1_done.sem, p1_done.at(i, l))
                        if l == 0:
                            dve.wait_ge(t_first.sem, t_first.at(i))
                        else:
                            dve.wait_ge(t_updated.sem, t_updated.at(i, l - 1))
                        dve.tensor_tensor(TM[0:n, :, 0:n], TM[0:n, :, 0:n], bank[0][:, :, 0:n], ALU.subtract).then_inc(t_updated.sem, 1)
                    dve.wait_ge(p2_done.sem, p2_done.at(i, l))
                    if l == 0:
                        dve.wait_ge(tt_first.sem, tt_first.at(i))
                    else:
                        dve.wait_ge(tt_updated.sem, tt_updated.at(i, l - 1))
                    dve.tensor_tensor(TT[0:n, :, 0:n], TT[0:n, :, 0:n], bank[1][:, :, 0:n], ALU.subtract).then_inc(tt_updated.sem, 1)
                dve.wait_ge(ks_done.sem, ks_done.at(i))
                dve.wait_ge(vb_made.sem, vb_made.at(i))
                for a in range(GH):
                    ins = dve.scalar_tensor_tensor(RR[0:n, a, :], bank[2][:, a, :], nb4[0:n, a:a + 1], VB[0:n, a, :], ALU.mult, ALU.add)
                ins.then_inc(r_made.sem, 1)
                if not last:
                    dve.wait_ge(kv_done.sem, kv_done.at(i))
                    dve.wait_ge(state_ready.sem, state_ready.at(i))
                    for a in range(GH):
                        ins = dve.scalar_tensor_tensor(SS[:, a, :], SS[:, a, :], EG[:, a, n - 1:n], PS[:, 5, a * P:(a + 1) * P],
                                                       ALU.mult, ALU.add)
                    ins.then_inc(state_ready.sem, 1)

            with dve.Fori(0, N_FULL) as i:
                gdn_chunk(i, P, False)
            gdn_chunk(N_FULL, TAIL, True)

            dve.wait_ge(o_copied.sem, o_copied.at(N_FULL))
            dve.memset(vt[:, 4, :], 0.0)
            dve.memset(sq_k[:, T:640], 0.0)
            dve.memset(sq_q[:, T:QPAD], 0.0).then_inc(pads_cleared.sem, 1)
            with dve.Fori(0, SH // 2) as i:
                tail = [r.rearrange("p (b t) -> p b t", b=2) for r in (zs[:, 0, 512:ZW], zs[:, 1, 512:ZW])]
                for a in range(2):
                    dve.wait_ge(z_done.sem, z_done.at(i, a))
                    dve.tensor_scalar(zs[:, a, 0:512], PS[:, 3 * a, :], SD ** -0.5, None, ALU.mult)
                    dve.tensor_scalar(tail[a], PS[:, 3 * a + 1:3 * a + 3, 0:432], SD ** -0.5, None,
                                      ALU.mult).then_inc(z_copied.sem, 1)
                for a in range(2):
                    dve.wait_ge(z_log.sem, z_log.at(i, a))
                    dve.wait_ge(z_copied.sem, z_copied.at(i, a))
                    dve.scalar_tensor_tensor(sp[:, a, :], zs[:, a, :], 0.0, sp[:, a, :], ALU.max, ALU.add).then_inc(softplus_made.sem, 1)
                for a in range(2):
                    dve.wait_ge(suffix_done.sem, suffix_done.at(i, a))
                    dve.tensor_tensor(zs[:, a, 0:512], zs[:, a, 0:512], PS[:, 3 * a, :], ALU.subtract)
                    dve.tensor_tensor(tail[a], tail[a], PS[:, 3 * a + 1:3 * a + 3, 0:432],
                                      ALU.subtract).then_inc(logits_made.sem, 1)
                dve.wait_ge(pair_hi_made.sem, pair_hi_made.at(i))
                hold()
                dve.tensor_tensor(x_lo[:, i + GH, 0:512], PS[:, 6, :], x_hi[:, i + GH, 0:512].bitcast(F32), ALU.subtract)
                dve.tensor_tensor(x_lo[:, i + GH, 512:T], PS[:, 7, 0:TAIL], x_hi[:, i + GH, 512:T].bitcast(F32),
                                  ALU.subtract).then_inc(pair_lo_made.sem, 1)

            gate(2, qkv[:, 0:GH, :], nrm_b, z0[:, :, :], par[:, P_GN:P_GN + 1], 0, gdn_hi_made, gdn_lo_made)
            out_projection("out0")
            layer_norm(0, "mlp0")
            mlp("mlp0", 0)
            layer_norm(1, "f")

            L = [lbt[:, x, :] for x in range(8)]
            dve.wait_ge(lb_exp.sem, lb_exp.at(0))
            steps = [(L[5], L[6], L[7], ALU.add), None, (L[6], L[6], L[5], ALU.mult), (L[7], L[7], L[5], ALU.mult),
                     (L[7], L[6], L[7], ALU.add), (L[0], L[7], L[6], ALU.subtract), None]
            for x, step in enumerate(steps):
                if x == 1:
                    ins = dve.reciprocal(L[5], L[5])
                elif x == 6:
                    ins = dve.tensor_scalar(L[1], L[0], -1.0, 1.0, ALU.mult, ALU.add)
                else:
                    ins = dve.tensor_tensor(*step)
                ins.then_inc(lbs.sem, 1)
                dve.wait_ge(lbs.sem, lbs.at(0, x + 1))
            _, _, e0 = AT["f"]
            with dve.Fori(0, 2) as i:
                for u in range(2):
                    for m in range(2):
                        t = i * 4 + (2 * u + m)
                        dve.wait_ge(evac[m].sem, i * 2 + (e0 + u + 1))
                        hold()
                        dve.tensor_scalar(fg[:, t, :], fg[:, t, :], lbt[:, 1, bass.ds(t, 1)], lbt[:, 0, bass.ds(t, 1)],
                                          ALU.mult, ALU.add).then_inc(f_made.sem, 1)
            dve.memset(aT[:, :], 0.0)
            dve.memset(kt[:, :, :], 0.0)
            dve.memset(qt[:, :, :], 0.0).then_inc(hg_cleared.sem, 1)
            dve.wait_ge(hg_cleared.sem, hg_cleared.at(0))
            dve.wait_ge(f_made.sem, f_made.at(HH - 1))
            for m in range(2):
                dve.wait_ge(evac[m].sem, AT["out1"][2])
            with dve.Fori(0, HH) as i:
                dve.wait_ge(logf_made.sem, logf_made.at(i))
                for c in range(N_FULL + 1):
                    n = min(P, T - c * P)
                    dve.tensor_tensor_scan(bc[:, c * P:c * P + n], ones[:, 0:n], ee[:, 0, c * P:c * P + n], 0.0,
                                           ALU.mult, ALU.add).then_inc(b_made.sem, 1)
                dve.tensor_scalar(kg[:, :], fg[:, i, :], -1.0, 1.0, ALU.mult, ALU.add).then_inc(k_made.sem, 1)
                dve.wait_ge(eb_made.sem, eb_made.at(i))
                dve.tensor_copy(el[:, :], eb[:, P - 1:N_FULL * P:P]).then_inc(chunk_decay_made.sem, 1)
                dve.wait_ge(chunk_decay_made.sem, chunk_decay_made.at(i))
                hold()
                dve.tensor_tensor(eb[:, :], eb[:, :], q1[:, i, :], ALU.mult).then_inc(qd1_made.sem, 1)
                dve.wait_ge(k_made.sem, k_made.at(i))

                def take(l):
                    m = LEVELS[l]
                    w = T if m < TAIL else N_FULL * P
                    dve.wait_ge(level_product.sem, level_product.at(i, l))
                    if l:
                        dve.wait_ge(level_taken.sem, level_taken.at(i, l - 1))

                    def blocks(ap):
                        return ap.rearrange("p (b r) -> p b r", r=m)
                    hold()
                    dve.copy_predicated(part(aT[:, 0:w], m, 1), blocks(hmask[:, l, 0:w // 2]),
                                        blocks(PS[:, l % 2, 0:w // 2])).then_inc(level_taken.sem, 1)

                for l, m in enumerate(LEVELS):
                    w = T if m < TAIL else N_FULL * P
                    dve.wait_ge(level_exp.sem, level_exp.at(i, l))
                    if l > 1:
                        dve.wait_ge(level_product.sem, level_product.at(i, l - 2))
                    hold()
                    dve.tensor_tensor(part(kt[:, l % 2, 0:w], m, 0), part(kg[:, 0:w], m, 0), part(ee[:, l % 2, 0:w], m, 0), ALU.mult)
                    dve.tensor_tensor(part(qt[:, l % 2, 0:w], m, 1), part(q1[:, i, 0:w], m, 1), part(ee[:, l % 2, 0:w], m, 1),
                                      ALU.mult).then_inc(level_scaled.sem, 1)
                    if l:
                        take(l - 1)
                last = bc[:, 0:512].rearrange("p (c t) -> p c t", c=4)[:, :, P - 1:P].broadcast_to((P, 4, P))
                dve.tensor_tensor(ee[:, 1, 0:512].rearrange("p (c t) -> p c t", c=4), bc[:, 0:512].rearrange("p (c t) -> p c t", c=4),
                                  last, ALU.subtract).then_inc(kh_exponent.sem, 1)
                take(6)
                dve.wait_ge(kh_exp.sem, kh_exp.at(i))
                dve.wait_ge(level_scaled.sem, level_scaled.at(i))
                dve.tensor_tensor(ee[:, 0, 0:512], kg[:, 0:512], ee[:, 1, 0:512], ALU.mult).then_inc(kh_made.sem, 1)
                dve.wait_ge(diag_product.sem, diag_product.at(i))
                dve.wait_ge(level_taken.sem, level_taken.at(i, 6))
                hold()
                dve.copy_predicated(aT[:, 0:512], dmask[:, 0:512], PS[:, 2, :])
                dve.copy_predicated(aT[0:TAIL, 512:T], dmask[0:TAIL, 512:T], PS[0:TAIL, 3, 0:TAIL]).then_inc(level_taken.sem, 1)
                dve.wait_ge(kv1_done.sem, kv1_done.at(i))
                for c in range(N_FULL):
                    if c == 0:
                        ins = dve.tensor_copy(s1[:, 0, :], PS[:, 5, 0:P])
                    else:
                        dve.wait_ge(states_made.sem, states_made.at(i, c - 1))
                        ins = dve.scalar_tensor_tensor(s1[:, c, :], s1[:, c - 1, :], el[:, c:c + 1], PS[:, 5, c * P:(c + 1) * P],
                                                       ALU.mult, ALU.add)
                    ins.then_inc(states_made.sem, 1)
            for g in range(2):
                gate(3 + g, fg[:, g * GH:(g + 1) * GH, :], nrm_c, z1[:, g * GH:(g + 1) * GH, :],
                     par[:, P_GN + 1:P_GN + 2], g * GH, hg_hi_made, hg_lo_made)
            out_projection("out1")
            layer_norm(2, "mlp1")
            mlp("mlp1", 1)
            layer_norm(3, "end")


def _columns(a):
    return a.reshape(-1, P).T


def kernel(x, meta_tokens, ab_w_in, ab_conv_w, ab_a_log, ab_dt_bias, ab_gnorm_g, ab_w_out, c_w_in, c_lb_raw,
           c_gnorm_g, c_w_out, ln_mix_g, ln_mix_b, mlp_w1, mlp_w2, ln_ffn_g, ln_ffn_b):
    import numpy as np
    import concourse.bacc as bacc
    from concourse.bass_utils import run_bass_kernel_spmd

    w_ab, w_c = ab_w_in[0], c_w_in[0]
    cut = 2048

    def stages(w):
        k, n = w.shape
        return w.reshape(k // D, KT, P, n // COLS, COLS).transpose(3, 0, 2, 1, 4).reshape(-1, P, KT * COLS)

    def mlp(l):
        for half in range(2):
            yield stages(mlp_w1[l][:, half * 2048:(half + 1) * 2048])
            yield stages(mlp_w2[l][half * 2048:(half + 1) * 2048])

    sb_at = cut + 2 * GH
    stream = [stages(w_ab[:, 0:1536]), stages(w_ab[:, 1536:2048]), stages(w_ab[:, sb_at:sb_at + 1024]),
              stages(w_ab[:, sb_at + 1024:sb_at + 1536]), stages(ab_w_out[0]), *mlp(0),
              stages(w_c[:, 1024:2048]), stages(w_c[:, 2048:3072]), stages(w_c[:, 0:1024]), stages(w_c[:, 3072:4096]),
              stages(c_w_out[0]), *mlp(1)]
    wstream = np.ascontiguousarray(np.concatenate(stream))
    gates = w_ab[:, cut:sb_at].reshape(KT, P, 2, GH).transpose(2, 1, 0, 3)

    j, i = np.arange(P)[:, None], np.arange(P)[None, :]
    tables = [j == i, i >= j, j >= i, np.where(j >= i, NEG, 0.0)]
    tables += [(j // (2 * m) == i // (2 * m)) & (j % (2 * m) < m) & (i % (2 * m) >= m) for m in LEVELS]
    tables += [j * np.ones((1, P)) == a for a in range(GH)]
    consts = np.concatenate([np.asarray(t, np.float32) for t in tables], 1)
    hmasks = np.zeros((P, 10, HALF), np.float32)
    for l, m in enumerate(LEVELS):
        t = np.arange(T).reshape(-1, 2 * m)[:, m:].reshape(-1) if m < TAIL else np.arange(512).reshape(-1, 2 * m)[:, m:].reshape(-1)
        t = t % P
        hmasks[:, l, :len(t)] = (j // (2 * m) == t[None] // (2 * m)) & (j % (2 * m) < m)
    hmasks[:, 8:10, :] = (j == np.arange(T)[None] % P).reshape(P, 2, HALF)

    lngs = [ln_mix_g[0], ln_ffn_g[0], ln_mix_g[1], ln_ffn_g[1]]
    lnbs = [ln_mix_b[0], ln_ffn_b[0], ln_mix_b[1], ln_ffn_b[1]]
    conv = ab_conv_w[0].reshape(4, 12, P).transpose(2, 1, 0).reshape(P, 48)
    params = np.concatenate([_columns(g) for g in lngs] + [_columns(b) for b in lnbs]
                            + [conv, _columns(c_lb_raw[0]), _columns(c_lb_raw[1]), ab_gnorm_g.T, c_gnorm_g.T], 1)
    h_in = np.concatenate([meta_tokens, x[0]]).T.reshape(KT, P, T).transpose(1, 0, 2)

    arrays = {"h_in": h_in, "wstream": wstream, "wgate": gates, "consts": consts, "hmasks": hmasks,
              "params": params, "gate_params": np.stack([ab_a_log[0], ab_dt_bias[0]], 1)}
    arrays = {k: np.ascontiguousarray(v) for k, v in arrays.items()}
    nc = bacc.Bacc("TRN2", target_bir_lowering=False, num_devices=1)
    args = [nc.dram_tensor(k, v.shape, mybir.dt.from_np(v.dtype), kind="ExternalInput").ap() for k, v in arrays.items()]
    out = nc.dram_tensor("out", (KT, P, SEQ), F32, kind="ExternalOutput").ap()
    hybrid_trunk(nc, *args, out)
    result = run_bass_kernel_spmd(nc, [arrays], core_ids=[0])
    got = result.results[0]["out"]
    return np.ascontiguousarray(got.reshape(D, SEQ).T.reshape(1, SEQ, D))
```

```python
from contextlib import ExitStack

import concourse.bass as bass
from concourse import mybir

ALU = mybir.AluOpType
ACT = mybir.ActivationFunctionType
F32 = mybir.dt.float32
F32R = mybir.dt.float32r
BF16 = mybir.dt.bfloat16

P = 128
D = 1024
KT = D // P
SEQ, N_META = 512, 16
T = SEQ + N_META
HALF = T // 2
N_FULL = T // P
TAIL = T - N_FULL * P
DEPTH = 2
GH = 4
SH, SD = 8, 64
HH = 8
COLS = 256
ALPHA = float((2 * DEPTH) ** 0.25)
LN_EPS, RMS_EPS, L2_EPS = 1e-5, 1e-6, 1e-6
EXP_LN = "natural_log_exp_and_others"
LEVELS = [1, 2, 4, 8, 16, 32, 64]
NEG = -1e30

C_GE, C_SUFFIX, C_NEG, C_LEVEL = 0, P, 2 * P, 3 * P
C_SEL = C_LEVEL + len(LEVELS) * P
C_ALL = C_SEL + GH * P
P_LNG, P_LNB = 0, 4 * KT
P_CONV = 8 * KT
P_LB = P_CONV + 12 * 4
P_GN = P_LB + 2 * HH
P_ALL = P_GN + 2
ZW = 1376
Z_PARTS = [(0, 0, 512, 0), (1, 128, 400, 512), (0, 512, 16, 912), (4, 512, 16, 928),
           (2, 256, 272, 944), (3, 384, 160, 1216)]
Z_BANKS = [(0, 0, 512), (1, 512, 432), (2, 944, 432)]
QPAD = T + 16
KH = T - P

FILLED = 3
STEPS = 2 * KT

N_CONST_LOADS = 6
PHASES = [("qkv", 6), ("z0", 2), ("qk", 4), ("v0", 2), ("out0", 4), ("mlp0", 32),
          ("f", 4), ("v1", 4), ("q1", 4), ("z1", 4), ("out1", 4), ("mlp1", 32)]
N_STAGES = sum(n for _, n in PHASES)


def _counts():
    at, stages, feature, evacs = {}, 0, 0, 1
    for name, n in PHASES:
        at[name] = (stages, feature, evacs)
        stages += n
        if name not in ("v0", "v1"):
            feature += n
            evacs += n // 2 + n // 4 if name.startswith("mlp") else n
    at["end"] = (stages, feature, evacs)
    return at


AT = _counts()


def z_where(col):
    for bank, first, n in Z_BANKS:
        if first <= col < first + n:
            return bank, col - first


def z_runs(tile, q0, q1):
    return [(c + max(s, q0) - s, max(s, q0), min(s + n, q1) - max(s, q0))
            for j, s, n, c in Z_PARTS if j == tile and max(s, q0) < min(s + n, q1)]


class Signal:

    def __init__(self, sem, per=1, step=1):
        self.sem, self.per, self.step = sem, per, step

    def at(self, i, k=None):
        k = self.per - 1 if k is None else k
        return i * (self.per * self.step) + (k + 1) * self.step


class HeadSignal:

    def __init__(self, both, a, together):
        self.sem, self.both, self.a, self.together = both.sem, both, a, together

    def at(self, i, k=None):
        per = self.both.per // 2
        k = per - 1 if k is None else k
        return self.both.at(i, self.a * per + k if self.together else 2 * k + self.a)


class HeadBuffers:

    FIRST, SECOND = 3 * T + 5 * SEQ, 5 * SEQ + P + 4

    def __init__(self, first, second):
        self.b, self.k, self.e = (first[:, x * T:(x + 1) * T] for x in range(3))
        rest = first[:, 3 * T:self.FIRST]
        self.ee, self.kt = (rest[:, x * 2 * SEQ:(x + 1) * 2 * SEQ].rearrange("p (s t) -> p s t", s=2) for x in range(2))
        self.qt = rest[:, 4 * SEQ:5 * SEQ].rearrange("p (s t) -> p s t", s=2)
        self.scores, kh_turned, states, self.kh = (second[:, x * SEQ:(x + 1) * SEQ] for x in range(4))
        self.kh_turned, self.states = (x.rearrange("p (c t) -> p c t", c=4) for x in (kh_turned, states))
        self.v = second[:, 4 * SEQ:5 * SEQ + P].rearrange("p (c t) -> p c t", c=5)
        self.decay = second[:, 5 * SEQ + P:5 * SEQ + P + 3]


def hybrid_trunk(nc, h_in, wstream, wgate, consts, hmasks, params, gate_params, out):
    ctx = ExitStack()
    with ctx:
        def levels(n):
            return [(x, x + 1) for x, m in enumerate(LEVELS[1:]) if 2 * m <= n]

        def sb(name, shape, dt=F32, c=ctx):
            return c.enter_context(nc.sbuf_tensor(name, shape, dt))

        def sig(name, per=1, step=1):
            return Signal(ctx.enter_context(nc.semaphore(name)), per, step)

        def head_sigs(name, per=1, together=False):
            both = sig(name, 2 * per)
            return [HeadSignal(both, a, together) for a in range(2)]

        PS = ctx.enter_context(nc.psum_tensor("banks", [P, 8, 512], F32))

        xs = ExitStack()
        x_hi = sb("x_hi", [P, KT, T], F32R, c=xs)
        x_lo = sb("x_lo", [P, KT, T], F32R, c=xs)
        xs.close()
        head_1 = sb("head_1", [P, 2 * KT * T])
        h = sb("h", [P, KT, T])
        w_raw = sb("w_raw", [P, 2, KT * COLS])
        w_hi = sb("w_hi", [P, 2, KT * COLS], F32R)
        w_lo = sb("w_lo", [P, 2, KT * COLS], F32R)
        ident = sb("ident", [P, P])
        hmask = sb("hmask", [P, len(LEVELS) + 3, HALF], mybir.dt.uint8)
        dmask = hmask[:, 8:10, :].rearrange("p a t -> p (a t)")[:, 0:SEQ]
        par = sb("par", [P, P_ALL])
        ident_b = sb("ident_b", [P, P], BF16)
        neg_b = sb("neg_b", [P, P], BF16)
        ones = sb("ones", [P, P])
        ones_d = sb("ones_d", [P, P])
        ones_h = sb("ones_h", [P, P])
        small = sb("small", [P, 4])
        eps_ln, eps_rms = small[:, 0:1], small[:, 1:2]
        gp = sb("gp", [GH, 3])
        lbt = sb("lbt", [P, 8, HH])
        lb, one_minus_lb = lbt[:, 0, :], lbt[:, 1, :]

        m0 = ExitStack()
        qkv = sb("qkv", [P, 12, T], c=m0)
        zqk = sb("zqk", [P, 3 * GH, T], c=m0)
        z0, qk = zqk[:, 0:GH, :], zqk[:, GH:3 * GH, :]
        con = sb("con", [P, C_ALL], c=m0)
        mask_in = qkv[:, 0:5, :].rearrange("p c (a t) -> p (c a) t", a=2)
        ge_mask = con[:, C_GE:C_GE + P]
        suffix = con[:, C_SUFFIX:C_SUFFIX + P]

        def level_mask(n, l):
            return con[0:n, C_LEVEL + l * P:C_LEVEL + l * P + n]

        def heads(ap, n):
            return ap.rearrange("p (o n) -> p o n", o=1).broadcast_to((n, GH, n))

        def sel_of(a):
            return con[0:GH, C_SEL + a * P:C_SEL + (a + 1) * P]

        ga = ExitStack()
        wg = sb("wg", [P, KT, 36], c=ga)
        beta = sb("beta", [GH, T], c=ga)
        gcum = sb("gcum", [GH, T], c=ga)
        colg = sb("colg", [P, N_FULL + 1, 2, GH], c=ga)
        cv = ExitStack()
        conv_in = sb("conv_in", [P, 2, T + 3], c=cv)
        conv_acc = sb("conv_acc", [P, 2, T], c=cv)
        nrm_a = sb("nrm_a", [P, 2, 2, T], c=cv)
        gtmp = sb("gtmp", [GH, 3, T], c=cv)
        cv.close()
        lp = ExitStack()
        kS, qS, vS, GB, BB, DM, MT, TT, TM, XS, AT0, KD, VB, EG, SS = (
            sb(n, [P, GH, P], c=lp) for n in ("kS", "qS", "vS", "GB", "BB", "DM", "MT", "TT", "TM", "XS", "AT0",
                                              "KD", "VB", "EG", "SS"))
        RR, VN = GB, MT
        ML = sb("ML", [P, 2, GH, P], c=lp)
        gsm = sb("gsm", [P, 6, GH], c=lp)
        gcol, bcol, gdiff, kd4, eg4, nb4 = (gsm[:, x, :] for x in range(6))
        gsel = sb("gsel", [GH, 2, P], c=lp)
        lp.close()
        ga.close()
        at = ExitStack()
        vt = sb("vt", [P, 5, SH * SD], c=at)
        sq_k = sb("sq_k", [P, 640], c=at)
        sq_q = sb("sq_q", [P, QPAD], c=at)
        sq_v = sb("sq_v", [P, 5, P], c=at)
        zs = sb("zs", [P, 2, ZW], c=at)
        sp = sb("sp", [P, 2, ZW], c=at)
        at.close()
        nb = ExitStack()
        nrm_b = sb("nrm_b", [P, 2, 2, T], c=nb)
        nb.close()
        m0.close()
        ln = ExitStack()
        rstd = sb("rstd", [P, T], c=ln)
        lnsq = sb("lnsq", [P, 2, T], c=ln)
        ln.close()
        ml = ExitStack()
        hid_hi = sb("hid_hi", [P, 16, T], F32R, c=ml)
        hid_lo = sb("hid_lo", [P, 16, T], F32R, c=ml)
        relu = sb("relu", [P, 2, T], c=ml)
        sqr = sb("sqr", [P, 2, T], c=ml)
        ln_sum = sb("ln_sum", [P, T], c=ml)
        ml.close()
        m1 = ExitStack()
        fg = sb("fg", [P, HH, T], c=m1)
        q1 = sb("q1", [P, HH, T], c=m1)
        z1 = sb("z1", [P, HH, T], c=m1)
        v1 = sb("v1", [P, 5, D], c=m1)
        hl = ExitStack()
        head_sets = [HeadBuffers(sb("head_0a", [P, HeadBuffers.FIRST], c=hl)[:, :],
                                 sb("head_0b", [P, HeadBuffers.SECOND], c=hl)[:, :]),
                     HeadBuffers(head_1[:, 0:HeadBuffers.FIRST], head_1[:, KT * T:KT * T + HeadBuffers.SECOND])]
        hl.close()
        nrm_c = sb("nrm_c", [P, 2, 2, T], c=m1)
        m1.close()

        consts_loaded = sig("consts_loaded", step=16)
        wgate_loaded = sig("wgate_loaded", step=16)
        out_stored = sig("out_stored", step=16)
        w_loaded = [sig(f"w_loaded{u}", step=16) for u in range(2)]
        w_hi_made, w_lo_made = sig("w_hi_made"), sig("w_lo_made")
        half_done, stage_done = sig("half_done"), sig("stage_done")
        evac = [sig("evacuated0"), sig("evacuated1")]
        act_waited, dve_waited, pool_waited = sig("act_waited"), sig("dve_waited"), sig("pool_waited")
        tile_done = [half_done, stage_done]
        v_tile_done0 = sig("v_tile_done0", 4)
        v_tile_done1 = sig("v_tile_done1", 4)
        v_evacuated0 = sig("v_evacuated0", 5)
        v_evacuated1 = sig("v_evacuated1", 5)
        gdn_hi_made = sig("gdn_hi_made", GH)
        hg_hi_made = sig("hg_hi_made", HH)
        x_lo_made = sig("x_lo_made", KT)
        out_ready = sig("out_ready", KT)
        m_made = sig("m_made", 2)
        x_done = sig("x_done", 6)
        level_masked = sig("level_masked", 6)
        b_made = head_sigs("b_made", 5, together=True)
        level_scaled = head_sigs("level_scaled", 7)
        level_exponent = head_sigs("level_exponent", 7)
        norm_squared = sig("norm_squared")
        norm_summed = sig("norm_summed")
        norm_logged = sig("norm_logged")
        ln_mean_ready = sig("ln_mean_ready")
        ln_squared = sig("ln_squared", KT)
        ln_square_used = sig("ln_square_used", KT)
        hidden_lo_made = sig("hidden_lo_made", 16)
        consts_made = sig("consts_made")
        gates_done = sig("gates_done")
        beta_made = sig("beta_made")
        gcum_made = sig("gcum_made", 5)
        columns_done = sig("columns_done")
        columns_made = sig("columns_made")
        gate_rows_staged = sig("gate_rows_staged")
        decay_rows_done = sig("decay_rows_done")
        beta_rows_done = sig("beta_rows_done")
        heads_staged = sig("heads_staged")
        kk_done = sig("kk_done")
        qk_done = sig("qk_done")
        k_turned = sig("k_turned")
        state_ready = sig("state_ready")
        v_turned = sig("v_turned")
        tt_first = sig("tt_first")
        t_turned = sig("t_turned")
        t_first = sig("t_first")
        t_updated = sig("t_updated", 5)
        tt_updated = sig("tt_updated", 6)
        x_copied = sig("x_copied", 6)
        p1_done = sig("p1_done", 5)
        p2_done = sig("p2_done", 6)
        ks_done = sig("ks_done")
        r_made = sig("r_made")
        a_made = sig("a_made")
        vnew_done = sig("vnew_done")
        vnew_copied = sig("vnew_copied")
        qd_made = sig("qd_made")
        kd_made = sig("kd_made")
        o_done = sig("o_done")
        kv_done = sig("kv_done")
        o_copied = sig("o_copied")
        pair_staged = sig("pair_staged")
        z_done = sig("z_done", 2)
        softplus_made = sig("softplus_made", 2)
        z_copied = sig("z_copied", 2)
        suffix_done = sig("suffix_done", 2)
        weights_made = sig("weights_made", 2)
        pair_done = sig("pair_done")
        pair_lo_made = sig("pair_lo_made")
        gdn_lo_made = sig("gdn_lo_made", GH)
        level_taken = head_sigs("level_taken", 8)
        level_product = head_sigs("level_product", 7)
        diag_product = head_sigs("diag_product")
        kh_made = head_sigs("kh_made")
        kh_turned = head_sigs("kh_turned")
        kh_copied = head_sigs("kh_copied")
        kv1_done = head_sigs("kv1_done")
        states_made = head_sigs("states_made", 4, together=True)
        qd1_made = head_sigs("qd1_made")
        o1_done = head_sigs("o1_done")
        o1_copied = head_sigs("o1_copied")
        hg_lo_made = sig("hg_lo_made", HH)
        norm_scaled = sig("norm_scaled")
        ln_centered = sig("ln_centered", KT)
        ln_logged = sig("ln_logged")
        ln_rstd_made = sig("ln_rstd_made")
        ln_scaled = sig("ln_scaled", KT)
        x_hi_made = sig("x_hi_made", KT)
        hidden_squared = sig("hidden_squared", 16)
        hidden_hi_made = sig("hidden_hi_made", 16)
        wg_cleared = sig("wg_cleared")
        conv_tap_added = sig("conv_tap_added", 4)
        qkv_made = sig("qkv_made")
        rate_made = sig("rate_made")
        lb_exp = sig("lb_exp")
        decay_logit_made = sig("decay_logit_made")
        gate_soft = sig("gate_soft", 3)
        norm_applied = sig("norm_applied")
        gb_made = sig("gb_made")
        eg_made = sig("eg_made")
        bb_made = sig("bb_made")
        gdiff_made = sig("gdiff_made")
        col_decay_made = sig("col_decay_made")
        dm_exponent = sig("dm_exponent")
        dm_exp = sig("dm_exp")
        pads_cleared = sig("pads_cleared")
        z_abs = sig("z_abs", 2)
        z_exp = sig("z_exp", 2)
        z_log = sig("z_log", 2)
        logits_made = sig("logits_made", 2)
        pair_hi_made = sig("pair_hi_made")
        norm_gated = sig("norm_gated")
        ln_partial = sig("ln_partial", KT + 1)
        f_made = sig("f_made")
        logf_made = head_sigs("logf_made")
        v_staged = head_sigs("v_staged")
        eb_made = head_sigs("eb_made")
        level_exp = head_sigs("level_exp", 7)
        kh_exponent = head_sigs("kh_exponent")
        kh_exp = head_sigs("kh_exp")
        ln_shifted = sig("ln_shifted", KT)
        lb_step = sig("lb_step", 9)
        softplus0 = sig("softplus0")
        g_made = sig("g_made")
        gcol_staged = sig("gcol_staged")
        dm_made = sig("dm_made")
        m_first = sig("m_first")
        vb_made = sig("vb_made")
        hg_cleared = sig("hg_cleared", 2)
        k_made = head_sigs("k_made")
        chunk_decay_made = head_sigs("chunk_decay_made")

        block = ctx.enter_context(nc.Block())

        def part(ap, m, which):
            return ap.rearrange("p (b s r) -> p b s r", s=2, r=m)[:, :, which, :]

        def halves(ap):
            return ap.rearrange("p (a t) -> p a t", a=2)

        def pair(m):
            return PS[:, 2 * m:2 * m + 2, 0:HALF]

        @block.sync
        def _(sp_):
            def load_stage(n, u):
                sp_.dma_start(w_raw[:, u, :], wstream[n]).then_inc(w_loaded[u].sem, 16)

            sp_.dma_start(h[:], h_in).then_inc(consts_loaded.sem, 16)
            load_stage(0, 0)
            load_stage(1, 1)
            with sp_.Fori(1, N_STAGES // 2) as i:
                for u in range(2):
                    sp_.wait_ge(w_lo_made.sem, i * 2 + (u - 1))
                    load_stage(i * 2 + u, u)
            for k in range(KT):
                sp_.wait_ge(out_ready.sem, out_ready.at(0, k))
                sp_.dma_start(out[k], h[:, k, N_META:T]).then_inc(out_stored.sem, 16)
            sp_.wait_ge(out_stored.sem, 16 * KT)

        @block.gpsimd
        def _(pool):
            def split_hi(n, u, first, round_):
                pool.wait_ge(w_loaded[u].sem, w_loaded[u].at(round_))
                if not first:
                    pool.wait_ge(stage_done.sem, n - 1)
                pool.sem_inc(pool_waited.sem, 1)
                pool.tensor_scalar(w_hi[:, u, :], w_raw[:, u, :], 1.0, 0.0, ALU.mult, ALU.add).then_inc(w_hi_made.sem, 1)

            def split_lo(n, u):
                pool.wait_ge(w_hi_made.sem, w_hi_made.at(n))
                pool.tensor_tensor(w_lo[:, u, :], w_raw[:, u, :], w_hi[:, u, :].bitcast(F32),
                                   ALU.subtract).then_inc(w_lo_made.sem, 1)

            def split(n, u, first, round_):
                split_hi(n, u, first, round_)
                split_lo(n, u)

            def split_rounds(a, b):
                with pool.Fori(a, b) as i:
                    for u in range(2):
                        split(i * 2 + u, u, False, i)

            for u in range(2):
                split(u, u, True, 0)
            split_rounds(1, AT["z0"][0] // 2 + 1)

            def mask_level(i, n, l):
                pool.wait_ge(m_made.sem, m_made.at(i))
                if l > 1:
                    pool.wait_ge(x_done.sem, x_done.at(i, l - 2))
                pool.tensor_tensor(ML[0:n, l % 2, :, 0:n], MT[0:n, :, 0:n], heads(level_mask(n, l + 1), n),
                                   ALU.mult).then_inc(level_masked.sem, 1)

            n0 = AT["z0"][0]
            with pool.Fori(0, FILLED) as i:
                mask_level(i, P, 0)
                mask_level(i, P, 1)
                mask_level(i, P, 2)
                mask_level(i, P, 3)
                mask_level(i, P, 4)
                split_hi(i * 2 + (n0 + 2), 0, False, i + (n0 // 2 + 1))
                mask_level(i, P, 5)
                split_lo(i * 2 + (n0 + 2), 0)
                split(i * 2 + (n0 + 3), 1, False, i + (n0 // 2 + 1))
            for i, n in ((FILLED, P), (N_FULL, TAIL)):
                for l, _ in levels(n):
                    mask_level(i, n, l)
            split_rounds(n0 // 2 + 1 + FILLED, AT["out1"][0] // 2 + 1)

            with pool.Fori(0, HH // 2) as i:
                for l, m in enumerate(LEVELS):
                    for a, hb in enumerate(head_sets):
                        first, second = part(hb.b[:, N_META:T], m, 0), part(hb.b[:, N_META:T], m, 1)
                        middle = first[:, :, m - 1:m].broadcast_to((P, SEQ // (2 * m), m))
                        if l == 0:
                            pool.wait_ge(b_made[a].sem, b_made[a].at(i))
                        if l > 1:
                            pool.wait_ge(level_scaled[a].sem, level_scaled[a].at(i, l - 2))
                        pool.tensor_tensor(part(hb.ee[:, l % 2, :], m, 0), middle, first, ALU.subtract)
                        pool.tensor_tensor(part(hb.ee[:, l % 2, :], m, 1), second, middle,
                                           ALU.subtract).then_inc(level_exponent[a].sem, 1)
            split_rounds(AT["out1"][0] // 2 + 1, N_STAGES // 2)

        @block.tensor
        def _(pe):
            def stage_fm(n, u, rhs, evacuated, start=True, stop=True, fresh=None):
                pe.wait_ge(w_lo_made.sem, w_lo_made.at(n))
                for m in range(2):
                    if evacuated is not None:
                        pe.wait_ge(evac[m].sem, evacuated)
                    for k in range(KT):
                        w = slice(k * COLS + m * P, k * COLS + m * P + P)
                        hi, lo = rhs(k)
                        if fresh is not None and m == 0:
                            pe.wait_ge(x_lo_made.sem, x_lo_made.at(fresh, k))
                        for w_part, x_part in ((w_hi, hi), (w_hi, lo), (w_lo, hi)):
                            for j in range(2):
                                mm = pe.matmul(PS[:, 2 * m + j, 0:HALF], w_part[:, u, w],
                                               x_part[:, j * HALF:(j + 1) * HALF],
                                               start=start and k == 0 and w_part is w_hi and x_part is hi,
                                               stop=stop and k == KT - 1 and w_part is w_lo)
                    mm.then_inc((stage_done if m else half_done).sem, 1)

            def x_tile(k):
                return x_hi[:, k, :], x_lo[:, k, :]

            def project(name, rounds, fresh=None):
                n0, _, e0 = AT[name]
                if fresh is not None:
                    for u in range(2):
                        stage_fm(n0 + u, u, x_tile, e0 + u, fresh=fresh if u == 0 else None)
                with pe.Fori(0 if fresh is None else 1, rounds) as i:
                    for u in range(2):
                        stage_fm(i * 2 + (n0 + u), u, x_tile, i * 2 + (e0 + u))

            def project_tokens(name, v_done, v_evac, rounds, first_full):
                n0 = AT[name][0]
                
                def stage(n, u, since, first):
                    pe.wait_ge(w_lo_made.sem, w_lo_made.at(n))
                    for j in range(5):
                        rows = min(P, T - j * P)
                        if not first:
                            pe.wait_ge(v_evac.sem, v_evac.at(since - 1, j))
                        at = first_full + j * P if j < N_FULL else (T - TAIL if first_full == 0 else 0)
                        for k in range(KT):
                            for x_part, w_part in ((x_hi, w_hi), (x_hi, w_lo), (x_lo, w_hi)):
                                mm = pe.matmul(PS[0:rows, j, 0:COLS], x_part[:, k, at:at + rows],
                                               w_part[:, u, k * COLS:(k + 1) * COLS],
                                               start=k == 0 and x_part is x_hi and w_part is w_hi,
                                               stop=k == KT - 1 and x_part is x_lo)
                        mm.then_inc((stage_done if j == 4 else v_done).sem, 1)

                for m in range(2):
                    pe.wait_ge(evac[m].sem, AT[name][2])
                stage(n0, 0, 0, True)
                stage(n0 + 1, 1, 1, False)
                if rounds > 1:
                    with pe.Fori(1, rounds) as i:
                        for u in range(2):
                            stage(i * 2 + (n0 + u), u, i * 2 + u, False)
                pe.wait_ge(v_evac.sem, v_evac.at(2 * rounds - 1))

            def head_norm_sums(r, groups, sq, weight):
                for g in range(groups):
                    pe.wait_ge(norm_squared.sem, norm_squared.at(r + g))
                    if g > 1:
                        pe.wait_ge(norm_logged.sem, norm_logged.at(r + g - 2))
                    for a in range(2):
                        for j in range(2):
                            mm = pe.matmul(PS[:, 4 * (g % 2) + 2 * a + j, 0:HALF], weight[:, :],
                                           sq[:, g % 2, a, j * HALF:(j + 1) * HALF], start=True, stop=True)
                    mm.then_inc(norm_summed.sem, 1)
                pe.wait_ge(norm_logged.sem, norm_logged.at(r + groups - 1))

            def layer_norm_sums(r, after):
                for m in range(2):
                    pe.wait_ge(evac[m].sem, AT[after][2])
                pe.wait_ge(ln_partial.sem, ln_partial.at(r))
                for j in range(2):
                    mm = pe.matmul(PS[:, 4 + j, 0:HALF], ones_d[:, :], ln_sum[:, j * HALF:(j + 1) * HALF],
                                   start=True, stop=True)
                mm.then_inc(ln_mean_ready.sem, 1)
                for k in range(KT):
                    pe.wait_ge(ln_squared.sem, ln_squared.at(r, k))
                    for j in range(2):
                        mm = pe.matmul(PS[:, 6 + j, 0:HALF], ones_d[:, :], lnsq[:, k % 2, j * HALF:(j + 1) * HALF],
                                       start=k == 0, stop=k == KT - 1)
                    mm.then_inc(ln_square_used.sem, 1)

            def mlp(name, r, fresh):
                n0, _, e0 = AT[name]
                for hf in range(2):
                    n1, e1 = n0 + 16 * hf, e0 + 12 * hf
                    if hf == 0:
                        for u in range(2):
                            stage_fm(n1 + u, u, x_tile, e1 + u, fresh=fresh if u == 0 else None)
                    with pe.Fori(1 if hf == 0 else 0, 4) as i:
                        for u in range(2):
                            stage_fm(i * 2 + (n1 + u), u, x_tile, i * 2 + (e1 + u))
                    with pe.Fori(0, 4) as i:
                        for u in range(2):
                            pe.wait_ge(hidden_lo_made.sem, hidden_lo_made.at(r * 2 + hf, 8 * u + 7))
                            stage_fm(i * 2 + (n1 + 8 + u), u,
                                     lambda k: (hid_hi[:, 8 * u + k, :], hid_lo[:, 8 * u + k, :]),
                                     i + (e1 + 8) if u == 0 else None, start=u == 0, stop=u == 1)

            pe.wait_ge(consts_loaded.sem, consts_loaded.at(N_CONST_LOADS - 1))
            pe.wait_ge(consts_made.sem, consts_made.at(0))
            project("qkv", 3, 0)

            pe.wait_ge(wgate_loaded.sem, 32)
            for j in range(2):
                for k in range(KT):
                    mm = pe.matmul(PS[0:36, 4 + j, 0:HALF], wg[:, k, :], h[:, k, j * HALF:(j + 1) * HALF],
                                   start=k == 0, stop=k == KT - 1)
            mm.then_inc(gates_done.sem, 1)
            pe.wait_ge(beta_made.sem, beta_made.at(0))
            pe.wait_ge(gcum_made.sem, gcum_made.at(0))
            for c in range(N_FULL + 1):
                n = min(P, T - c * P)
                pe.transpose(PS[0:n, 6, 8 * c:8 * c + 4], beta[:, c * P:c * P + n], ident[0:GH, 0:GH])
                mm = pe.transpose(PS[0:n, 6, 8 * c + 4:8 * c + 8], gcum[:, c * P:c * P + n], ident[0:GH, 0:GH])
            mm.then_inc(columns_done.sem, 1)
            pe.wait_ge(columns_made.sem, columns_made.at(0))
            for m in range(2):
                pe.wait_ge(evac[m].sem, AT["z0"][2])
            head_norm_sums(0, 4, nrm_a, ones)

            def gdn_chunk(i, n, last, filled):
                n0, _, e0 = AT["z0"]

                def fill(s0, s1):
                    if not filled:
                        return
                    for step in range(s0, s1):
                        u, m, k = step // STEPS, step // KT % 2, step % KT
                        if m == 0 and k == 0:
                            pe.wait_ge(w_lo_made.sem, w_lo_made.at(i * 2 + (n0 + u)))
                        if k == 0:
                            pe.wait_ge(evac[m].sem, i * 2 + (e0 + u))
                        w = slice(k * COLS + m * P, k * COLS + m * P + P)
                        for w_part, x_part in ((w_hi, x_hi), (w_hi, x_lo), (w_lo, x_hi)):
                            for j in range(2):
                                mm = pe.matmul(PS[:, 2 * m + j, 0:HALF], w_part[:, u, w],
                                               x_part[:, k, j * HALF:(j + 1) * HALF],
                                               start=k == 0 and w_part is w_hi and x_part is x_hi,
                                               stop=k == KT - 1 and w_part is w_lo)
                        if k == KT - 1:
                            mm.then_inc(tile_done[m].sem, 1)

                def each(bank, lhs, rhs, width=P, rows=n, signal=None, start=True, stop=True):
                    for a in range(GH):
                        mm = pe.matmul(PS[0:rows, bank, a * P:a * P + width], lhs(a), rhs(a), start=start, stop=stop)
                    if signal is not None:
                        mm.then_inc(signal.sem, 1)

                fill(0, 2)
                pe.wait_ge(gate_rows_staged.sem, gate_rows_staged.at(i))
                each(4, lambda a: sel_of(a), lambda a: gsel[0:GH, 0, 0:n], n, P, decay_rows_done)
                pe.wait_ge(state_ready.sem, state_ready.at(i))
                each(5, lambda a: sel_of(a), lambda a: gsel[0:GH, 1, 0:n], n, P, beta_rows_done)
                pe.wait_ge(heads_staged.sem, heads_staged.at(i))
                each(6, lambda a: kS[:, a, 0:n], lambda a: kS[:, a, 0:n], n, n, kk_done)
                each(7, lambda a: kS[:, a, 0:n], lambda a: qS[:, a, 0:n], n, n, qk_done)
                pe.wait_ge(gb_made.sem, gb_made.at(i))
                pe.wait_ge(eg_made.sem, eg_made.at(i))
                for a in range(GH):
                    mm = pe.transpose(PS[0:n, 4, a * P:(a + 1) * P], kS[:, a, 0:n], ident[:, :])
                mm.then_inc(k_turned.sem, 1)
                pe.wait_ge(bb_made.sem, bb_made.at(i))
                for a in range(GH):
                    mm = pe.transpose(PS[0:n, 5, a * P:(a + 1) * P], vS[:, a, 0:n], ident[:, :])
                mm.then_inc(v_turned.sem, 1)
                fill(2, 4)
                pe.wait_ge(tt_first.sem, tt_first.at(i))
                for a in range(GH):
                    mm = pe.transpose(PS[0:n, 6, a * P:a * P + n], TT[0:n, a, 0:n], ident[0:n, 0:n])
                mm.then_inc(t_turned.sem, 1)
                fill(4, 5)
                pe.wait_ge(t_first.sem, t_first.at(i))
                pe.wait_ge(a_made.sem, a_made.at(i))
                last_level = len(levels(n)) - 1
                for l, _ in levels(n):
                    pe.wait_ge(level_masked.sem, level_masked.at(i, l))
                    if l:
                        pe.wait_ge(t_updated.sem, t_updated.at(i, l - 1))
                        pe.wait_ge(tt_updated.sem, tt_updated.at(i, l - 1))
                    each(7, lambda a: ML[0:n, l % 2, a, 0:n], lambda a: TM[0:n, a, 0:n], n, n, x_done)
                    fill(4 * l + 5, 4 * l + 7)
                    pe.wait_ge(x_copied.sem, x_copied.at(i, l))
                    if l == 0:
                        pe.wait_ge(kd_made.sem, kd_made.at(i))
                        pe.wait_ge(vb_made.sem, vb_made.at(i))
                    if l < last_level:
                        each(4, lambda a: TT[0:n, a, 0:n], lambda a: XS[0:n, a, 0:n], n, n, p1_done)
                    each(5, lambda a: XS[0:n, a, 0:n], lambda a: TT[0:n, a, 0:n], n, n, p2_done)
                    fill(4 * l + 7, 4 * l + 9)
                each(6, lambda a: kS[:, a, 0:n], lambda a: SS[:, a, :], P, n, ks_done)
                fill(29, 30)
                pe.wait_ge(tt_updated.sem, tt_updated.at(i, last_level))
                pe.wait_ge(r_made.sem, r_made.at(i))
                each(7, lambda a: TT[0:n, a, 0:n], lambda a: RR[0:n, a, :], P, n, vnew_done)
                fill(30, 31)
                pe.wait_ge(vnew_copied.sem, vnew_copied.at(i))
                pe.wait_ge(qd_made.sem, qd_made.at(i))
                for a in range(GH):
                    pe.matmul(PS[:, 4, a * P:a * P + n], VN[0:n, a, :], AT0[0:n, a, 0:n], start=True, stop=False)
                    mm = pe.matmul(PS[:, 4, a * P:a * P + n], SS[:, a, :], qS[:, a, 0:n], start=False, stop=True)
                mm.then_inc(o_done.sem, 1)
                if not last:
                    each(5, lambda a: KD[0:n, a, :], lambda a: VN[0:n, a, :], P, P, kv_done)
                    fill(31, 32)
                    pe.wait_ge(o_copied.sem, o_copied.at(i))

            with pe.Fori(0, FILLED) as i:
                gdn_chunk(i, P, False, True)
            gdn_chunk(FILLED, P, False, False)
            gdn_chunk(N_FULL, TAIL, True, False)
            pe.wait_ge(o_copied.sem, o_copied.at(N_FULL))

            project_tokens("v0", v_tile_done0, v_evacuated0, 1, 0)

            with pe.Fori(0, SH // 2) as i:
                pe.wait_ge(pair_staged.sem, pair_staged.at(i))
                for a in range(2):
                    rows = slice(a * SD, (a + 1) * SD)
                    for j, q0, cnt, col in Z_PARTS:
                        bank, c = z_where(col)
                        diag = q0 == j * P
                        mm = pe.matmul(PS[:, 3 * a + bank, c:c + cnt], sq_k[rows, j * P:(j + 1) * P],
                                       sq_q[rows, q0:q0 + cnt], start=True, stop=not diag)
                        if diag:
                            w = min(P, cnt)
                            mm = pe.matmul(PS[:, 3 * a + bank, c:c + w], ident_b[:, :], neg_b[:, 0:w],
                                           start=False, stop=True)
                    mm.then_inc(z_done.sem, 1)
                for a in range(2):
                    pe.wait_ge(softplus_made.sem, softplus_made.at(i, a))
                    pe.wait_ge(z_copied.sem, z_copied.at(i, a))
                    for j, q0, cnt, col in Z_PARTS:
                        bank, c = z_where(col)
                        later = [(r, q, m) for jj in range(j + 1, 5) for r, q, m in z_runs(jj, q0, q0 + cnt)]
                        mm = pe.matmul(PS[:, 3 * a + bank, c:c + cnt], suffix[:, :], sp[:, a, col:col + cnt],
                                       start=True, stop=not later)
                        for x, (r, q, m) in enumerate(later):
                            mm = pe.matmul(PS[:, 3 * a + bank, c + q - q0:c + q - q0 + m], ones[:, :],
                                           sp[:, a, r:r + m], start=False, stop=x == len(later) - 1)
                    mm.then_inc(suffix_done.sem, 1)
                for a in range(2):
                    pe.wait_ge(weights_made.sem, weights_made.at(i, a))
                    rows = slice(a * SD, (a + 1) * SD)
                    for bank, qa, qb in ((6, 0, 512), (7, 512, T)):
                        runs = [(j, r, q, m) for j in range(5) for r, q, m in z_runs(j, qa, qb)]
                        for x, (j, r, q, m) in enumerate(runs):
                            mm = pe.matmul(PS[rows, bank, q - qa:q - qa + m], sq_v[:, j, rows], zs[:, a, r:r + m],
                                           start=x == 0, stop=x == len(runs) - 1)
                mm.then_inc(pair_done.sem, 1)
                pe.wait_ge(pair_lo_made.sem, pair_lo_made.at(i))

            head_norm_sums(4, 2, nrm_b, ones_h)
            pe.wait_ge(gdn_lo_made.sem, gdn_lo_made.at(0))
            project("out0", 2)
            layer_norm_sums(0, "mlp0")
            mlp("mlp0", 0, 1)
            layer_norm_sums(1, "f")

            project("f", 2, 2)
            project_tokens("v1", v_tile_done1, v_evacuated1, 2, N_META)
            project("q1", 2)
            project("z1", 2)
            for m in range(2):
                pe.wait_ge(evac[m].sem, AT["out1"][2])

            with pe.Fori(0, HH // 2) as i:
                def chunk(c):
                    return slice(N_META + c * P, N_META + (c + 1) * P)

                for a, hb in enumerate(head_sets):
                    pe.wait_ge(k_made[a].sem, k_made[a].at(i))
                    for c in range(N_FULL):
                        mm = pe.matmul(PS[:, 6 + a, c * P:(c + 1) * P], hb.k[:, chunk(c)], q1[:, i * 2 + a, chunk(c)],
                                       start=True, stop=True)
                    mm.then_inc(diag_product[a].sem, 1)
                for l, m in enumerate(LEVELS):
                    for a, hb in enumerate(head_sets):
                        pe.wait_ge(level_scaled[a].sem, level_scaled[a].at(i, l))
                        if l > 1:
                            pe.wait_ge(level_taken[a].sem, level_taken[a].at(i, l - 1))
                        for c in range(N_FULL):
                            mm = pe.matmul(PS[:, 2 * a + l % 2, 64 * c:64 * c + 64], hb.kt[:, l % 2, c * P:(c + 1) * P],
                                           hb.qt[:, l % 2, 64 * c:64 * c + 64], start=True, stop=True)
                        mm.then_inc(level_product[a].sem, 1)
                    if l == 0:
                        for a, hb in enumerate(head_sets):
                            pe.wait_ge(kh_made[a].sem, kh_made[a].at(i))
                            for c in range(N_FULL - 1):
                                pe.transpose(PS[:, 4 + a, c * P:(c + 1) * P], hb.kh[:, chunk(c)], ident[:, :])
                            mm = pe.transpose(PS[0:N_META, 4 + a, 3 * P:4 * P], hb.kh[:, 0:N_META], ident[:, :])
                            mm.then_inc(kh_turned[a].sem, 1)
                    if l == 1:
                        for a, hb in enumerate(head_sets):
                            pe.wait_ge(kh_copied[a].sem, kh_copied[a].at(i))
                            pe.wait_ge(level_taken[a].sem, level_taken[a].at(i, 0))
                            for c in range(N_FULL - 1):
                                pe.matmul(PS[:, 6 + a, c * P:(c + 1) * P], hb.kh_turned[:, c, :], hb.v[:, c, :],
                                          start=True, stop=True)
                            mm = pe.matmul(PS[:, 6 + a, 3 * P:4 * P], hb.kh_turned[0:N_META, 3, :], hb.v[0:N_META, 4, :],
                                           start=True, stop=True)
                            mm.then_inc(kv1_done[a].sem, 1)
                for a, hb in enumerate(head_sets):
                    pe.wait_ge(states_made[a].sem, states_made[a].at(i))
                    pe.wait_ge(qd1_made[a].sem, qd1_made[a].at(i))
                    pe.wait_ge(level_taken[a].sem, level_taken[a].at(i))
                    for c in range(N_FULL):
                        dst = PS[:, 4 + a, c * P:(c + 1) * P]
                        pe.matmul(dst, hb.v[:, c, :], hb.scores[:, c * P:(c + 1) * P], start=True, stop=False)
                        mm = pe.matmul(dst, hb.states[:, c, :], hb.e[:, chunk(c)], start=False, stop=True)
                    mm.then_inc(o1_done[a].sem, 1)
                for a in range(2):
                    pe.wait_ge(o1_copied[a].sem, o1_copied[a].at(i))

            head_norm_sums(6, 4, nrm_c, ones_h)
            pe.wait_ge(hg_lo_made.sem, hg_lo_made.at(0))
            project("out1", 2)
            layer_norm_sums(2, "mlp1")
            mlp("mlp1", 1, 3)
            layer_norm_sums(3, "end")

        @block.scalar
        def _(act):
            def hold():
                act.sem_inc(act_waited.sem, 1)

            def from_tile(m, n, f, dst, func):
                act.wait_ge(tile_done[m].sem, (n if m else f) + 1)
                hold()
                act.activation(halves(dst), pair(m), func).then_inc(evac[m].sem, 1)

            def evacuate(name, rounds, dst, func):
                n0, f0, _ = AT[name]
                with act.Fori(0, rounds) as i:
                    for u in range(2):
                        for m in range(2):
                            from_tile(m, i * 2 + (n0 + u), i * 2 + (f0 + u), dst[:, i * 4 + (2 * u + m), :], func)

            def evacuate_tokens(name, v_done, v_evac, rounds, dst):
                n0 = AT[name][0]
                with act.Fori(0, rounds) as i:
                    for u in range(2):
                        for j in range(5):
                            rows = min(P, T - j * P)
                            if j < 4:
                                act.wait_ge(v_done.sem, v_done.at(i * 2 + u, j))
                            else:
                                act.wait_ge(stage_done.sem, i * 2 + (n0 + u + 1))
                            hold()
                            act.activation(dst[0:rows, j, bass.ds(i * (2 * COLS) + u * COLS, COLS)],
                                           PS[0:rows, j, 0:COLS],
                                           ACT.Copy).then_inc(v_evac.sem, 1)

            def head_norms(r, groups, src, buf):
                for g in range(groups + 1):
                    if g < groups:
                        if g > 1:
                            act.wait_ge(norm_applied.sem, norm_applied.at(r + g - 2))
                        act.activation(buf[:, g % 2, :, :], src[:, 2 * g:2 * g + 2, :],
                                       ACT.Square).then_inc(norm_squared.sem, 1)
                    if g:
                        b = (g - 1) % 2
                        act.wait_ge(norm_summed.sem, norm_summed.at(r + g - 1))
                        act.activation(buf[:, b, :, :].rearrange("p h (a t) -> p (h a) t", a=2),
                                       PS[:, 4 * b:4 * b + 4, 0:HALF], ACT.Ln, bias=eps_rms).then_inc(norm_logged.sem, 1)
                        act.wait_ge(norm_logged.sem, norm_logged.at(r + g - 1))
                        act.activation(buf[:, b, :, :], buf[:, b, :, :], ACT.Exp, scale=-0.5).then_inc(norm_scaled.sem, 1)

            def layer_norm(r):
                for k in range(KT):
                    act.wait_ge(ln_centered.sem, ln_centered.at(r, k))
                    if k > 1:
                        act.wait_ge(ln_square_used.sem, ln_square_used.at(r, k - 2))
                    act.activation(lnsq[:, k % 2, :], h[:, k, :], ACT.Square).then_inc(ln_squared.sem, 1)
                act.wait_ge(ln_square_used.sem, ln_square_used.at(r))
                act.activation(halves(rstd[:, :]), PS[:, 6:8, 0:HALF], ACT.Ln, bias=eps_ln).then_inc(ln_logged.sem, 1)
                act.wait_ge(ln_logged.sem, ln_logged.at(r))
                act.activation(rstd[:, :], rstd[:, :], ACT.Exp, scale=-0.5).then_inc(ln_rstd_made.sem, 1)
                for k in range(KT):
                    act.wait_ge(ln_scaled.sem, ln_scaled.at(r, k))
                    col = P_LNB + r * KT + k
                    dst, done = (x_hi, x_hi_made) if r < 3 else (h, out_ready)
                    act.activation(dst[:, k, :], h[:, k, :], ACT.Identity, bias=par[:, col:col + 1]).then_inc(done.sem, 1)

            def mlp(name, r):
                n0, f0, _ = AT[name]
                for hf in range(2):
                    with act.Fori(0, 4) as i:
                        for u in range(2):
                            for m in range(2):
                                t = i * 4 + (2 * u + m)
                                from_tile(m, i * 2 + (n0 + 16 * hf + u), i * 2 + (f0 + 16 * hf + u), relu[:, m, :], ACT.Relu)
                                act.wait_ge(hidden_squared.sem, hidden_squared.at(r * 2 + hf, t))
                                hold()
                                act.activation(hid_hi[:, t, :], sqr[:, m, :],
                                               ACT.Copy).then_inc(hidden_hi_made.sem, 1)

            for dst, src in ((con[:], consts[:, P:]), (ident[:], consts[:, 0:P]), (mask_in, hmasks),
                             (par[:], params), (gp[:, 0:2], gate_params)):
                act.dma_start(dst, src).then_inc(consts_loaded.sem, 16)
            act.wait_ge(wg_cleared.sem, wg_cleared.at(0))
            act.dma_start(wg[:, :, 0:GH], wgate[0]).then_inc(wgate_loaded.sem, 16)
            act.dma_start(wg[:, :, 32:32 + GH], wgate[1]).then_inc(wgate_loaded.sem, 16)
            act.wait_ge(consts_loaded.sem, consts_loaded.at(N_CONST_LOADS - 1))
            for k in range(KT):
                act.activation(x_hi[:, k, :], h[:, k, :], ACT.Copy).then_inc(x_hi_made.sem, 1)

            act.wait_ge(consts_made.sem, consts_made.at(0))
            n0, f0, _ = AT["qkv"]
            with act.Fori(0, 3) as i:
                for u in range(2):
                    for m in range(2):
                        from_tile(m, i * 2 + (n0 + u), i * 2 + (f0 + u), conv_in[:, m, 3:3 + T], ACT.Copy)
                        act.wait_ge(conv_tap_added.sem, conv_tap_added.at(i * 4 + (2 * u + m)))
                        hold()
                        act.activation(qkv[:, i * 4 + (2 * u + m), :], conv_acc[:, m, :], ACT.Silu).then_inc(qkv_made.sem, 1)
            act.wait_ge(gates_done.sem, gates_done.at(0))
            act.activation(halves(beta[:, :]), PS[0:GH, 4:6, 0:HALF], ACT.Sigmoid).then_inc(beta_made.sem, 1)
            act.preload_act_table_set(EXP_LN)
            act.activation(gp[:, 2:3], gp[:, 0:1], ACT.Exp).then_inc(rate_made.sem, 1)
            act.activation(lbt[:, 6, :], lbt[:, 3, :], ACT.Exp)
            act.activation(lbt[:, 7, :], lbt[:, 4, :], ACT.Exp).then_inc(lb_exp.sem, 1)
            act.wait_ge(decay_logit_made.sem, decay_logit_made.at(0))
            act.activation(gtmp[:, 1, :], gtmp[:, 0, :], ACT.Abs).then_inc(gate_soft.sem, 1)
            act.wait_ge(gate_soft.sem, gate_soft.at(0, 0))
            act.activation(gtmp[:, 1, :], gtmp[:, 1, :], ACT.Exp, scale=-1.0).then_inc(gate_soft.sem, 1)
            act.wait_ge(gate_soft.sem, gate_soft.at(0, 1))
            act.activation(gtmp[:, 1, :], gtmp[:, 1, :], ACT.Ln, bias=small[0:GH, 2:3]).then_inc(gate_soft.sem, 1)
            act.wait_ge(columns_done.sem, columns_done.at(0))
            full = PS[:, 6, 0:8 * N_FULL].rearrange("p (c w h) -> p c w h", c=N_FULL, w=2)
            act.activation(colg[:, 0:N_FULL, :, :], full, ACT.Copy)
            act.activation(colg[0:TAIL, N_FULL, :, :], PS[0:TAIL, 6, 8 * N_FULL:8 * N_FULL + 8].rearrange("p (w h) -> p w h", w=2),
                           ACT.Copy).then_inc(columns_made.sem, 1)
            act.wait_ge(qkv_made.sem, qkv_made.at(11))
            head_norms(0, 4, qkv[:, 0:2 * GH, :], nrm_a)
            act.wait_ge(norm_applied.sem, norm_applied.at(3))

            def gdn_chunk(i, n, last, filled):
                n0, f0, _ = AT["z0"]

                def take_tile(half):
                    if filled:
                        u, m = half // 2, half % 2
                        from_tile(m, i * 2 + (n0 + u), i * 2 + (f0 + u), zqk[:, i * 4 + half, :], ACT.Copy)

                cols = bass.ds(i * P, n)
                act.activation(gsel[:, 0, 0:n], gcum[:, cols], ACT.Copy)
                act.activation(gsel[:, 1, 0:n], beta[:, cols], ACT.Copy).then_inc(gate_rows_staged.sem, 1)
                for g, dst in ((1, kS), (0, qS), (2, vS)):
                    ins = act.activation(dst[:, :, 0:n], qkv[:, g * GH:(g + 1) * GH, cols], ACT.Copy)
                ins.then_inc(heads_staged.sem, 1)
                act.wait_ge(decay_rows_done.sem, decay_rows_done.at(i))
                rows = PS[:, 4, :].rearrange("p (h t) -> p h t", h=GH)[:, :, 0:n]
                act.activation(GB[:, :, 0:n], rows, ACT.Copy).then_inc(gb_made.sem, 1)
                act.wait_ge(state_ready.sem, state_ready.at(i))
                act.activation(EG[:, :, 0:n], rows, ACT.Exp).then_inc(eg_made.sem, 1)
                act.wait_ge(beta_rows_done.sem, beta_rows_done.at(i))
                rows = PS[:, 5, :].rearrange("p (h t) -> p h t", h=GH)[:, :, 0:n]
                act.activation(BB[:, :, 0:n], rows, ACT.Copy).then_inc(bb_made.sem, 1)
                act.wait_ge(gdiff_made.sem, gdiff_made.at(i))
                act.activation(kd4[0:n], gdiff[0:n], ACT.Exp, scale=-1.0)
                act.activation(eg4[0:n], gcol[0:n], ACT.Exp).then_inc(col_decay_made.sem, 1)
                act.wait_ge(dm_exponent.sem, dm_exponent.at(i))
                act.activation(DM[0:n, :, 0:n], DM[0:n, :, 0:n], ACT.Exp).then_inc(dm_exp.sem, 1)
                act.wait_ge(t_turned.sem, t_turned.at(i))
                bank = [PS[0:n, b, :].rearrange("p (h t) -> p h t", h=GH) for b in range(8)]
                act.activation(TM[0:n, :, 0:n], bank[6][:, :, 0:n], ACT.Copy).then_inc(t_first.sem, 1)
                for l, _ in levels(n):
                    act.wait_ge(x_done.sem, x_done.at(i, l))
                    act.activation(XS[0:n, :, 0:n], bank[7][:, :, 0:n], ACT.Copy).then_inc(x_copied.sem, 1)
                    if l % 2:
                        take_tile(l // 2)
                act.wait_ge(vnew_done.sem, vnew_done.at(i))
                act.activation(VN[0:n, :, :], bank[7], ACT.Copy).then_inc(vnew_copied.sem, 1)
                act.wait_ge(o_done.sem, o_done.at(i))
                o = PS[:, 4, :].rearrange("p (h t) -> p h t", h=GH)[:, :, 0:n]
                hold()
                act.activation(qkv[:, 0:GH, cols], o, ACT.Copy).then_inc(o_copied.sem, 1)
                take_tile(3)

            with act.Fori(0, FILLED) as i:
                gdn_chunk(i, P, False, True)
            gdn_chunk(FILLED, P, False, False)
            gdn_chunk(N_FULL, TAIL, True, False)

            act.activation(z0, z0, ACT.Silu)
            act.wait_ge(pads_cleared.sem, pads_cleared.at(0))
            evacuate_tokens("v0", v_tile_done0, v_evacuated0, 1, vt)
            act.preload_act_table_set(EXP_LN)
            with act.Fori(0, SH // 2) as i:
                act.activation(sq_k[:, 0:T], qk[:, i + GH, :], ACT.Copy)
                act.activation(sq_q[:, 0:T], qk[:, i, :], ACT.Copy)
                act.activation(sq_v[:, :, :], vt[:, :, bass.ds(i * P, P)], ACT.Copy).then_inc(pair_staged.sem, 1)
                for a in range(2):
                    act.wait_ge(z_copied.sem, z_copied.at(i, a))
                    act.activation(sp[:, a, :], zs[:, a, :], ACT.Abs).then_inc(z_abs.sem, 1)
                    act.wait_ge(z_abs.sem, z_abs.at(i, a))
                    act.activation(sp[:, a, :], sp[:, a, :], ACT.Exp, scale=-1.0).then_inc(z_exp.sem, 1)
                    act.wait_ge(z_exp.sem, z_exp.at(i, a))
                    act.activation(sp[:, a, :], sp[:, a, :], ACT.Ln, bias=small[:, 2:3]).then_inc(z_log.sem, 1)
                for a in range(2):
                    act.wait_ge(logits_made.sem, logits_made.at(i, a))
                    act.activation(zs[:, a, :], zs[:, a, :], ACT.Exp).then_inc(weights_made.sem, 1)
                act.wait_ge(pair_done.sem, pair_done.at(i))
                hold()
                act.activation(x_hi[:, i + GH, 0:512], PS[:, 6, :], ACT.Copy)
                act.activation(x_hi[:, i + GH, 512:T], PS[:, 7, 0:TAIL], ACT.Copy).then_inc(pair_hi_made.sem, 1)

            def gate(g0, src, tiles, hi_made):
                for a in range(tiles):
                    act.wait_ge(norm_gated.sem, norm_gated.at(g0 + a // 2))
                    act.activation(x_hi[:, a, :], src[:, a, :], ACT.Copy).then_inc(hi_made.sem, 1)

            act.wait_ge(o_copied.sem, o_copied.at(N_FULL))
            head_norms(4, 2, qkv[:, 0:GH, :], nrm_b)
            gate(0, qkv, GH, gdn_hi_made)
            act.wait_ge(gdn_lo_made.sem, gdn_lo_made.at(0))
            layer_norm(0)
            mlp("mlp0", 0)
            act.preload_act_table_set(EXP_LN)
            layer_norm(1)

            evacuate("f", 2, fg, ACT.Sigmoid)
            evacuate_tokens("v1", v_tile_done1, v_evacuated1, 2, v1)
            evacuate("q1", 2, q1, ACT.Silu)
            evacuate("z1", 2, z1, ACT.Silu)
            act.preload_act_table_set(EXP_LN)
            act.wait_ge(f_made.sem, f_made.at(HH - 1))
            with act.Fori(0, HH // 2) as i:
                for a, hb in enumerate(head_sets):
                    act.activation(hb.e, fg[:, i * 2 + a, :], ACT.Ln).then_inc(logf_made[a].sem, 1)
                for a, hb in enumerate(head_sets):
                    cols = bass.ds(i * (2 * P) + a * P, P)
                    act.activation(hb.v[:, 0:N_FULL, :], v1[:, 0:N_FULL, cols], ACT.Copy)
                    act.activation(hb.v[0:N_META, N_FULL, :], v1[0:N_META, N_FULL, cols],
                                   ACT.Copy).then_inc(v_staged[a].sem, 1)
                for a, hb in enumerate(head_sets):
                    act.wait_ge(b_made[a].sem, b_made[a].at(i))
                    act.activation(hb.e, hb.b, ACT.Exp).then_inc(eb_made[a].sem, 1)
                for l in range(len(LEVELS)):
                    for a, hb in enumerate(head_sets):
                        act.wait_ge(level_exponent[a].sem, level_exponent[a].at(i, l))
                        act.activation(hb.ee[:, l % 2, :], hb.ee[:, l % 2, :], ACT.Exp).then_inc(level_exp[a].sem, 1)
                    if l == 0:
                        for a, hb in enumerate(head_sets):
                            act.wait_ge(kh_exponent[a].sem, kh_exponent[a].at(i))
                            act.activation(hb.kh[:, 0:KH], hb.kh[:, 0:KH], ACT.Exp, scale=-1.0).then_inc(kh_exp[a].sem, 1)
                    if l == 1:
                        for a, hb in enumerate(head_sets):
                            act.wait_ge(kh_turned[a].sem, kh_turned[a].at(i))
                            turned = PS[:, 4 + a, :].rearrange("p (c t) -> p c t", c=4)
                            act.activation(hb.kh_turned[:, 0:3, :], turned[:, 0:3, :], ACT.Copy)
                            act.activation(hb.kh_turned[0:N_META, 3, :], turned[0:N_META, 3, :],
                                           ACT.Copy).then_inc(kh_copied[a].sem, 1)
                for a, hb in enumerate(head_sets):
                    act.wait_ge(o1_done[a].sem, o1_done[a].at(i))
                    hold()
                    act.activation(fg[:, i * 2 + a, N_META:T], PS[:, 4 + a, :], ACT.Copy).then_inc(o1_copied[a].sem, 1)
            for a in range(2):
                act.wait_ge(o1_copied[a].sem, o1_copied[a].at(HH // 2 - 1))
            head_norms(6, 4, fg, nrm_c)
            gate(2, fg, HH, hg_hi_made)
            act.wait_ge(hg_lo_made.sem, hg_lo_made.at(0))
            layer_norm(2)
            mlp("mlp1", 1)
            act.preload_act_table_set(EXP_LN)
            layer_norm(3)

        @block.vector
        def _(dve):
            def hold():
                dve.sem_inc(dve_waited.sem, 1)

            def head_norms(r, groups, src, buf, scale):
                for g in range(groups):
                    x = src[:, 2 * g:2 * g + 2, :]
                    dve.wait_ge(norm_scaled.sem, norm_scaled.at(r + g))
                    dve.scalar_tensor_tensor(x, x, scale(g), buf[:, g % 2, :, :], ALU.mult,
                                             ALU.mult).then_inc(norm_applied.sem, 1)

            def gate(r, g0, groups, src, buf, z, gain, hi_made, lo_made):
                for g in range(groups + 1):
                    if g < groups:
                        x = src[:, 2 * g:2 * g + 2, :]
                        dve.wait_ge(norm_scaled.sem, norm_scaled.at(r + g))
                        dve.scalar_tensor_tensor(x, x, gain, buf[:, g % 2, :, :], ALU.mult,
                                                 ALU.mult).then_inc(norm_applied.sem, 1)
                        dve.wait_ge(norm_applied.sem, norm_applied.at(r + g))
                        dve.tensor_tensor(x, x, z[:, 2 * g:2 * g + 2, :], ALU.mult).then_inc(norm_gated.sem, 1)
                    if g == groups:
                        for a in range(2 * groups):
                            dve.wait_ge(norm_gated.sem, norm_gated.at(g0 + a // 2))
                            dve.wait_ge(hi_made.sem, hi_made.at(0, a))
                            dve.tensor_tensor(x_lo[:, a, :], src[:, a, :], x_hi[:, a, :].bitcast(F32),
                                              ALU.subtract).then_inc(lo_made.sem, 1)

            def add_residual(m, n, f, tile, scale):
                dve.wait_ge(tile_done[m].sem, (n if m else f) + 1)
                hold()
                dve.scalar_tensor_tensor(halves(h[:, tile, :]), halves(h[:, tile, :]), scale, pair(m),
                                         ALU.mult, ALU.add).then_inc(evac[m].sem, 1)

            def clear_sum():
                dve.memset(ln_sum[:, :], 0.0).then_inc(ln_partial.sem, 1)

            def add_to_sum(r, m, evacuated, tile):
                dve.wait_ge(evac[m].sem, evacuated)
                dve.wait_ge(ln_partial.sem, ln_partial.at(r, tile))
                hold()
                dve.tensor_tensor(ln_sum[:, :], ln_sum[:, :], h[:, tile, :], ALU.add).then_inc(ln_partial.sem, 1)

            def out_projection(name, r):
                n0, f0, e0 = AT[name]
                clear_sum()
                with dve.Fori(0, 2) as i:
                    for u in range(2):
                        for m in range(2):
                            add_residual(m, i * 2 + (n0 + u), i * 2 + (f0 + u), i * 4 + (2 * u + m), ALPHA)
                            add_to_sum(r, m, i * 2 + (e0 + u + 1), i * 4 + (2 * u + m))

            def layer_norm(r, after):
                for m in range(2):
                    dve.wait_ge(evac[m].sem, AT[after][2])
                dve.wait_ge(ln_mean_ready.sem, ln_mean_ready.at(r))
                for k in range(KT):
                    dve.tensor_tensor(halves(h[:, k, :]), halves(h[:, k, :]), PS[:, 4:6, 0:HALF],
                                      ALU.subtract).then_inc(ln_centered.sem, 1)
                dve.wait_ge(ln_rstd_made.sem, ln_rstd_made.at(r))
                dve.wait_ge(ln_centered.sem, ln_centered.at(r))
                for k in range(KT + 1):
                    if k < KT:
                        gain = par[:, P_LNG + r * KT + k:P_LNG + r * KT + k + 1]
                        dve.scalar_tensor_tensor(h[:, k, :], h[:, k, :], gain, rstd[:, :],
                                                 ALU.mult, ALU.mult).then_inc(ln_scaled.sem, 1)
                    if k and r < 3:
                        shift = par[:, P_LNB + r * KT + k - 1:P_LNB + r * KT + k]
                        dve.wait_ge(ln_scaled.sem, ln_scaled.at(r, k - 1))
                        dve.wait_ge(x_hi_made.sem, x_hi_made.at(r + 1, k - 1))
                        dve.scalar_tensor_tensor(x_lo[:, k - 1, :], h[:, k - 1, :], shift, x_hi[:, k - 1, :].bitcast(F32),
                                                 ALU.add, ALU.subtract).then_inc(x_lo_made.sem, 1)
                if r < 3:
                    for k in range(KT):
                        shift = par[:, P_LNB + r * KT + k:P_LNB + r * KT + k + 1]
                        dve.tensor_scalar(h[:, k, :], h[:, k, :], shift, None, ALU.add).then_inc(ln_shifted.sem, 1)
                    dve.wait_ge(ln_shifted.sem, ln_shifted.at(r))

            def mlp(name, r):
                n0, f0, e0 = AT[name]
                for hf in range(2):
                    n1, f1, e1, rr = n0 + 16 * hf, f0 + 16 * hf, e0 + 12 * hf, r * 2 + hf
                    with dve.Fori(0, 4) as i:
                        for u in range(2):
                            for m in range(2):
                                t = i * 4 + (2 * u + m)
                                dve.wait_ge(evac[m].sem, i * 2 + (e1 + u + 1))
                                dve.tensor_tensor(sqr[:, m, :], relu[:, m, :], relu[:, m, :],
                                                  ALU.mult).then_inc(hidden_squared.sem, 1)
                                dve.wait_ge(hidden_hi_made.sem, hidden_hi_made.at(rr, t))
                                dve.wait_ge(hidden_squared.sem, hidden_squared.at(rr, t))
                                dve.tensor_tensor(hid_lo[:, t, :], sqr[:, m, :], hid_hi[:, t, :].bitcast(F32),
                                                  ALU.subtract).then_inc(hidden_lo_made.sem, 1)
                    if hf == 1:
                        clear_sum()
                    with dve.Fori(0, 4) as i:
                        for m in range(2):
                            add_residual(m, i * 2 + (n1 + 9), i * 2 + (f1 + 9), i * 2 + m, ALPHA if hf == 0 else 1.0)
                            if hf == 1:
                                add_to_sum(2 * r + 1, m, i + (e1 + 9), i * 2 + m)
                    if hf == 0:
                        for m in range(2):
                            dve.wait_ge(evac[m].sem, AT[name][2] + 12)

            dve.memset(wg[:, :, :], 0.0).then_inc(wg_cleared.sem, 1)
            dve.memset(ones[:, :], 1.0)
            dve.memset(ones_d[:, :], 1.0 / D)
            dve.memset(ones_h[:, :], 1.0 / P)
            dve.memset(small[:, 0:1], LN_EPS)
            dve.memset(small[:, 1:2], RMS_EPS)
            dve.memset(small[:, 2:3], 1.0)
            dve.memset(conv_in[:, :, 0:3], 0.0)
            dve.wait_ge(consts_loaded.sem, consts_loaded.at(N_CONST_LOADS - 1))
            dve.tensor_copy(hmask[:, :, :], mask_in)
            dve.tensor_copy(ident_b[:, :], ident[:, :]).then_inc(evac[0].sem, 1)
            dve.tensor_copy(neg_b[:, :], con[:, C_NEG:C_NEG + P]).then_inc(evac[1].sem, 1)
            raw0, raw1 = par[:, P_LB:P_LB + HH], par[:, P_LB + HH:P_LB + 2 * HH]
            L = [lbt[:, x, :] for x in range(8)]
            lbs = lb_step
            dve.tensor_tensor(L[2], raw0, raw1, ALU.max).then_inc(lbs.sem, 1)
            dve.wait_ge(lbs.sem, lbs.at(0, 0))
            dve.tensor_tensor(L[3], raw0, L[2], ALU.subtract)
            dve.tensor_tensor(L[4], raw1, L[2], ALU.subtract).then_inc(consts_made.sem, 1)
            for k in range(KT):
                dve.wait_ge(x_hi_made.sem, x_hi_made.at(0, k))
                dve.tensor_tensor(x_lo[:, k, :], h[:, k, :], x_hi[:, k, :].bitcast(F32),
                                  ALU.subtract).then_inc(x_lo_made.sem, 1)

            e0 = AT["qkv"][2]
            with dve.Fori(0, 3) as i:
                for u in range(2):
                    for m in range(2):
                        q = i * 4 + (2 * u + m)
                        dve.wait_ge(evac[m].sem, i * 2 + (e0 + u + 1))
                        hold()
                        for tap in range(4):
                            weight = par[:, bass.ds(q * 4 + (P_CONV + tap), 1)]
                            x = conv_in[:, m, tap:tap + T]
                            if tap == 0:
                                ins = dve.tensor_scalar(conv_acc[:, m, :], x, weight, None, ALU.mult)
                            else:
                                dve.wait_ge(conv_tap_added.sem, conv_tap_added.at(q, tap - 1))
                                ins = dve.scalar_tensor_tensor(conv_acc[:, m, :], x, weight, conv_acc[:, m, :],
                                                               ALU.mult, ALU.add)
                            ins.then_inc(conv_tap_added.sem, 1)

            dve.wait_ge(gates_done.sem, gates_done.at(0))
            dve.tensor_scalar(halves(gtmp[:, 0, :]), PS[32:32 + GH, 4:6, 0:HALF], gp[:, 1:2], None,
                              ALU.add).then_inc(decay_logit_made.sem, 1)
            dve.wait_ge(gate_soft.sem, gate_soft.at(0))
            dve.wait_ge(decay_logit_made.sem, decay_logit_made.at(0))
            dve.scalar_tensor_tensor(gtmp[:, 2, :], gtmp[:, 0, :], 0.0, gtmp[:, 1, :], ALU.max, ALU.add).then_inc(softplus0.sem, 1)
            dve.wait_ge(softplus0.sem, softplus0.at(0))
            dve.wait_ge(rate_made.sem, rate_made.at(0))
            dve.tensor_scalar(gtmp[:, 0, :], gtmp[:, 2, :], gp[:, 2:3], -1.0, ALU.mult, ALU.mult).then_inc(g_made.sem, 1)
            dve.wait_ge(g_made.sem, g_made.at(0))
            for c in range(N_FULL + 1):
                n = min(P, T - c * P)
                dve.tensor_tensor_scan(gcum[:, c * P:c * P + n], ones[0:GH, 0:n], gtmp[:, 0, c * P:c * P + n], 0.0,
                                       ALU.mult, ALU.add).then_inc(gcum_made.sem, 1)
            head_norms(0, 4, qkv, nrm_a, lambda g: P ** -0.5 if g < 2 else 1.0)
            dve.wait_ge(norm_applied.sem, norm_applied.at(3))
            dve.memset(SS[:, :, :], 0.0).then_inc(state_ready.sem, 1)

            def gdn_chunk(i, n, last, filled):
                bank = [PS[0:n, b, :].rearrange("p (h t) -> p h t", h=GH) for b in range(8)]
                dve.tensor_copy(gcol[0:n], colg[0:n, i, 1, :])
                dve.tensor_copy(bcol[0:n], colg[0:n, i, 0, :]).then_inc(gcol_staged.sem, 1)
                dve.wait_ge(gb_made.sem, gb_made.at(i))
                dve.wait_ge(gcol_staged.sem, gcol_staged.at(i))
                dve.tensor_tensor(gdiff[0:n], gcol[0:n], GB[0:n, :, n - 1], ALU.subtract).then_inc(gdiff_made.sem, 1)
                for a in range(GH):
                    ins = dve.tensor_scalar(DM[0:n, a, 0:n], GB[0:n, a, 0:n], gcol[0:n, a:a + 1], 0.0, ALU.subtract, ALU.min)
                ins.then_inc(dm_exponent.sem, 1)
                dve.wait_ge(dm_exp.sem, dm_exp.at(i))
                dve.tensor_tensor(DM[0:n, :, 0:n], DM[0:n, :, 0:n], heads(ge_mask[0:n, 0:n], n), ALU.mult).then_inc(dm_made.sem, 1)
                dve.wait_ge(kk_done.sem, kk_done.at(i))
                dve.wait_ge(dm_made.sem, dm_made.at(i))
                dve.tensor_tensor(MT[0:n, :, 0:n], bank[6][:, :, 0:n], DM[0:n, :, 0:n], ALU.mult).then_inc(m_made.sem, 1)
                dve.wait_ge(m_made.sem, m_made.at(i, 0))
                dve.wait_ge(bb_made.sem, bb_made.at(i))
                dve.tensor_tensor(MT[0:n, :, 0:n], MT[0:n, :, 0:n], BB[0:n, :, 0:n], ALU.mult).then_inc(m_made.sem, 1)
                dve.wait_ge(m_made.sem, m_made.at(i, 1))
                dve.tensor_tensor(XS[0:n, :, 0:n], MT[0:n, :, 0:n], heads(level_mask(n, 0), n), ALU.mult).then_inc(m_first.sem, 1)
                dve.wait_ge(m_first.sem, m_first.at(i))
                dve.tensor_tensor(TT[0:n, :, 0:n], heads(ident[0:n, 0:n], n), XS[0:n, :, 0:n], ALU.subtract).then_inc(tt_first.sem, 1)
                dve.wait_ge(qk_done.sem, qk_done.at(i))
                dve.tensor_tensor(AT0[0:n, :, 0:n], bank[7][:, :, 0:n], DM[0:n, :, 0:n], ALU.mult).then_inc(a_made.sem, 1)
                dve.wait_ge(col_decay_made.sem, col_decay_made.at(i))
                dve.wait_ge(k_turned.sem, k_turned.at(i))
                for a in range(GH):
                    ins = dve.tensor_scalar(KD[0:n, a, :], bank[4][:, a, :], kd4[0:n, a:a + 1], None, ALU.mult)
                ins.then_inc(kd_made.sem, 1)
                dve.wait_ge(v_turned.sem, v_turned.at(i))
                for a in range(GH):
                    dve.tensor_scalar(VB[0:n, a, :], bank[5][:, a, :], bcol[0:n, a:a + 1], None, ALU.mult)
                dve.scalar_tensor_tensor(nb4[0:n], eg4[0:n], -1.0, bcol[0:n], ALU.mult, ALU.mult).then_inc(vb_made.sem, 1)
                dve.wait_ge(eg_made.sem, eg_made.at(i))
                dve.tensor_tensor(qS[:, :, 0:n], qS[:, :, 0:n], EG[:, :, 0:n], ALU.mult).then_inc(qd_made.sem, 1)
                lv = levels(n)
                for l, _ in lv:
                    if l < len(lv) - 1:
                        dve.wait_ge(p1_done.sem, p1_done.at(i, l))
                        if l == 0:
                            dve.wait_ge(t_first.sem, t_first.at(i))
                        else:
                            dve.wait_ge(t_updated.sem, t_updated.at(i, l - 1))
                        dve.tensor_tensor(TM[0:n, :, 0:n], TM[0:n, :, 0:n], bank[4][:, :, 0:n], ALU.subtract).then_inc(t_updated.sem, 1)
                    dve.wait_ge(p2_done.sem, p2_done.at(i, l))
                    if l == 0:
                        dve.wait_ge(tt_first.sem, tt_first.at(i))
                    else:
                        dve.wait_ge(tt_updated.sem, tt_updated.at(i, l - 1))
                    dve.tensor_tensor(TT[0:n, :, 0:n], TT[0:n, :, 0:n], bank[5][:, :, 0:n], ALU.subtract).then_inc(tt_updated.sem, 1)
                dve.wait_ge(ks_done.sem, ks_done.at(i))
                dve.wait_ge(vb_made.sem, vb_made.at(i))
                for a in range(GH):
                    ins = dve.scalar_tensor_tensor(RR[0:n, a, :], bank[6][:, a, :], nb4[0:n, a:a + 1], VB[0:n, a, :], ALU.mult, ALU.add)
                ins.then_inc(r_made.sem, 1)
                if not last:
                    dve.wait_ge(kv_done.sem, kv_done.at(i))
                    dve.wait_ge(state_ready.sem, state_ready.at(i))
                    for a in range(GH):
                        ins = dve.scalar_tensor_tensor(SS[:, a, :], SS[:, a, :], EG[:, a, n - 1:n], PS[:, 5, a * P:(a + 1) * P],
                                                       ALU.mult, ALU.add)
                    ins.then_inc(state_ready.sem, 1)

            with dve.Fori(0, FILLED) as i:
                gdn_chunk(i, P, False, True)
            gdn_chunk(FILLED, P, False, False)
            gdn_chunk(N_FULL, TAIL, True, False)

            dve.wait_ge(o_copied.sem, o_copied.at(N_FULL))
            dve.memset(vt[:, 4, :], 0.0)
            dve.memset(sq_k[:, T:640], 0.0)
            dve.memset(sq_q[:, T:QPAD], 0.0).then_inc(pads_cleared.sem, 1)
            with dve.Fori(0, SH // 2) as i:
                tail = [r.rearrange("p (b t) -> p b t", b=2) for r in (zs[:, 0, 512:ZW], zs[:, 1, 512:ZW])]
                for a in range(2):
                    dve.wait_ge(z_done.sem, z_done.at(i, a))
                    dve.tensor_scalar(zs[:, a, 0:512], PS[:, 3 * a, :], SD ** -0.5, None, ALU.mult)
                    dve.tensor_scalar(tail[a], PS[:, 3 * a + 1:3 * a + 3, 0:432], SD ** -0.5, None,
                                      ALU.mult).then_inc(z_copied.sem, 1)
                for a in range(2):
                    dve.wait_ge(z_log.sem, z_log.at(i, a))
                    dve.wait_ge(z_copied.sem, z_copied.at(i, a))
                    dve.scalar_tensor_tensor(sp[:, a, :], zs[:, a, :], 0.0, sp[:, a, :], ALU.max, ALU.add).then_inc(softplus_made.sem, 1)
                for a in range(2):
                    dve.wait_ge(suffix_done.sem, suffix_done.at(i, a))
                    dve.tensor_tensor(zs[:, a, 0:512], zs[:, a, 0:512], PS[:, 3 * a, :], ALU.subtract)
                    dve.tensor_tensor(tail[a], tail[a], PS[:, 3 * a + 1:3 * a + 3, 0:432],
                                      ALU.subtract).then_inc(logits_made.sem, 1)
                dve.wait_ge(pair_hi_made.sem, pair_hi_made.at(i))
                hold()
                dve.tensor_tensor(x_lo[:, i + GH, 0:512], PS[:, 6, :], x_hi[:, i + GH, 0:512].bitcast(F32), ALU.subtract)
                dve.tensor_tensor(x_lo[:, i + GH, 512:T], PS[:, 7, 0:TAIL], x_hi[:, i + GH, 512:T].bitcast(F32),
                                  ALU.subtract).then_inc(pair_lo_made.sem, 1)

            gate(4, 0, 2, qkv, nrm_b, z0, par[:, P_GN:P_GN + 1], gdn_hi_made, gdn_lo_made)
            out_projection("out0", 0)
            layer_norm(0, "mlp0")
            mlp("mlp0", 0)
            layer_norm(1, "f")

            L = [lbt[:, x, :] for x in range(8)]
            dve.wait_ge(lb_exp.sem, lb_exp.at(0))
            steps = [(L[5], L[6], L[7], ALU.add), None, (L[6], L[6], L[5], ALU.mult), (L[7], L[7], L[5], ALU.mult),
                     (L[7], L[6], L[7], ALU.add), (L[0], L[7], L[6], ALU.subtract), None]
            for x, step in enumerate(steps):
                if x == 1:
                    ins = dve.reciprocal(L[5], L[5])
                elif x == 6:
                    ins = dve.tensor_scalar(L[1], L[0], -1.0, 1.0, ALU.mult, ALU.add)
                else:
                    ins = dve.tensor_tensor(*step)
                ins.then_inc(lbs.sem, 1)
                dve.wait_ge(lbs.sem, lbs.at(0, x + 1))
            _, _, e0 = AT["f"]
            with dve.Fori(0, 2) as i:
                for u in range(2):
                    for m in range(2):
                        t = i * 4 + (2 * u + m)
                        dve.wait_ge(evac[m].sem, i * 2 + (e0 + u + 1))
                        hold()
                        dve.tensor_scalar(fg[:, t, :], fg[:, t, :], lbt[:, 1, bass.ds(t, 1)], lbt[:, 0, bass.ds(t, 1)],
                                          ALU.mult, ALU.add).then_inc(f_made.sem, 1)
            dve.wait_ge(f_made.sem, f_made.at(HH - 1))
            for m in range(2):
                dve.wait_ge(evac[m].sem, AT["out1"][2])
            for hb in head_sets:
                dve.memset(hb.scores, 0.0)
                dve.memset(hb.kt, 0.0).then_inc(hg_cleared.sem, 1)
            dve.wait_ge(hg_cleared.sem, hg_cleared.at(0))
            with dve.Fori(0, HH // 2) as i:
                def take(a, hb, l):
                    m = LEVELS[l]

                    def blocks(ap):
                        return ap.rearrange("p (b r) -> p b r", r=m)
                    dve.wait_ge(level_product[a].sem, level_product[a].at(i, l))
                    dve.wait_ge(level_taken[a].sem, level_taken[a].at(i, l))
                    hold()
                    dve.copy_predicated(part(hb.scores, m, 1), blocks(hmask[:, l, 0:SEQ // 2]),
                                        blocks(PS[:, 2 * a + l % 2, 0:SEQ // 2])).then_inc(level_taken[a].sem, 1)

                for a, hb in enumerate(head_sets):
                    dve.wait_ge(logf_made[a].sem, logf_made[a].at(i))
                    for c in range(N_FULL + 1):
                        t0, t1 = (N_META + (c - 1) * P, N_META + c * P) if c else (0, N_META)
                        dve.tensor_tensor_scan(hb.b[:, t0:t1], ones[:, 0:t1 - t0], hb.e[:, t0:t1], 0.0,
                                               ALU.mult, ALU.add).then_inc(b_made[a].sem, 1)
                    dve.tensor_scalar(hb.k, fg[:, i * 2 + a, :], -1.0, 1.0, ALU.mult, ALU.add).then_inc(k_made[a].sem, 1)
                for a, hb in enumerate(head_sets):
                    dve.wait_ge(b_made[a].sem, b_made[a].at(i))
                    dve.tensor_tensor(hb.kh[:, 0:N_META], hb.b[:, 0:N_META],
                                      hb.b[:, N_META - 1:N_META].broadcast_to((P, N_META)), ALU.subtract)
                    own, last = (x.rearrange("p (c t) -> p c t", c=3) for x in (hb.kh[:, N_META:KH], hb.b[:, N_META:KH]))
                    dve.tensor_tensor(own, last, last[:, :, P - 1:P].broadcast_to((P, 3, P)),
                                      ALU.subtract).then_inc(kh_exponent[a].sem, 1)
                for a, hb in enumerate(head_sets):
                    dve.wait_ge(eb_made[a].sem, eb_made[a].at(i))
                    dve.tensor_copy(hb.decay, hb.e[:, N_META + P - 1:KH:P]).then_inc(chunk_decay_made[a].sem, 1)
                    dve.wait_ge(chunk_decay_made[a].sem, chunk_decay_made[a].at(i))
                    hold()
                    dve.tensor_tensor(hb.e[:, N_META:T], hb.e[:, N_META:T], q1[:, i * 2 + a, N_META:T],
                                      ALU.mult).then_inc(qd1_made[a].sem, 1)
                for l, m in enumerate(LEVELS):
                    for a, hb in enumerate(head_sets):
                        if l == 0:
                            dve.wait_ge(k_made[a].sem, k_made[a].at(i))
                        dve.wait_ge(level_exp[a].sem, level_exp[a].at(i, l))
                        if l > 1:
                            dve.wait_ge(level_product[a].sem, level_product[a].at(i, l - 2))
                        hold()
                        dve.tensor_tensor(part(hb.kt[:, l % 2, :], m, 0), part(hb.k[:, N_META:T], m, 0),
                                          part(hb.ee[:, l % 2, :], m, 0), ALU.mult)
                        dve.tensor_tensor(hb.qt[:, l % 2, :].rearrange("p (b r) -> p b r", r=m),
                                          part(q1[:, i * 2 + a, N_META:T], m, 1),
                                          part(hb.ee[:, l % 2, :], m, 1), ALU.mult).then_inc(level_scaled[a].sem, 1)
                    for a, hb in enumerate(head_sets):
                        if l == 0:
                            dve.wait_ge(kh_exp[a].sem, kh_exp[a].at(i))
                            dve.tensor_tensor(hb.kh[:, 0:KH], hb.k[:, 0:KH], hb.kh[:, 0:KH], ALU.mult).then_inc(kh_made[a].sem, 1)
                            dve.wait_ge(diag_product[a].sem, diag_product[a].at(i))
                            hold()
                            dve.copy_predicated(hb.scores, dmask, PS[:, 6 + a, :]).then_inc(level_taken[a].sem, 1)
                        else:
                            take(a, hb, l - 1)
                        if l == 3:
                            dve.wait_ge(kv1_done[a].sem, kv1_done[a].at(i))
                            dve.tensor_copy(hb.states[:, 0, :], PS[:, 6 + a, 3 * P:4 * P]).then_inc(states_made[a].sem, 1)
                            for c in range(N_FULL - 1):
                                dve.wait_ge(states_made[a].sem, states_made[a].at(i, c))
                                dve.scalar_tensor_tensor(hb.states[:, c + 1, :], hb.states[:, c, :], hb.decay[:, c:c + 1],
                                                         PS[:, 6 + a, c * P:(c + 1) * P],
                                                         ALU.mult, ALU.add).then_inc(states_made[a].sem, 1)
                for a, hb in enumerate(head_sets):
                    take(a, hb, len(LEVELS) - 1)
            gate(6, 2, 4, fg, nrm_c, z1, par[:, P_GN + 1:P_GN + 2], hg_hi_made, hg_lo_made)
            out_projection("out1", 2)
            layer_norm(2, "mlp1")
            mlp("mlp1", 1)
            layer_norm(3, "end")


def _columns(a):
    return a.reshape(-1, P).T


def kernel(x, meta_tokens, ab_w_in, ab_conv_w, ab_a_log, ab_dt_bias, ab_gnorm_g, ab_w_out, c_w_in, c_lb_raw,
           c_gnorm_g, c_w_out, ln_mix_g, ln_mix_b, mlp_w1, mlp_w2, ln_ffn_g, ln_ffn_b):
    import numpy as np
    import concourse.bacc as bacc
    from concourse.bass_utils import run_bass_kernel_spmd

    w_ab, w_c = ab_w_in[0], c_w_in[0]
    cut = 2048

    def stages(w):
        k, n = w.shape
        return w.reshape(k // D, KT, P, n // COLS, COLS).transpose(3, 0, 2, 1, 4).reshape(-1, P, KT * COLS)

    def mlp(l):
        for half in range(2):
            yield stages(mlp_w1[l][:, half * 2048:(half + 1) * 2048])
            yield stages(mlp_w2[l][half * 2048:(half + 1) * 2048])

    sb_at = cut + 2 * GH
    stream = [stages(w_ab[:, 0:1536]), stages(w_ab[:, 1536:2048]), stages(w_ab[:, sb_at:sb_at + 1024]),
              stages(w_ab[:, sb_at + 1024:sb_at + 1536]), stages(ab_w_out[0]), *mlp(0),
              stages(w_c[:, 1024:2048]), stages(w_c[:, 2048:3072]), stages(w_c[:, 0:1024]), stages(w_c[:, 3072:4096]),
              stages(c_w_out[0]), *mlp(1)]
    wstream = np.ascontiguousarray(np.concatenate(stream))
    gates = w_ab[:, cut:sb_at].reshape(KT, P, 2, GH).transpose(2, 1, 0, 3)

    j, i = np.arange(P)[:, None], np.arange(P)[None, :]
    tables = [j == i, i >= j, j >= i, np.where(j >= i, NEG, 0.0)]
    tables += [(j // (2 * m) == i // (2 * m)) & (j % (2 * m) < m) & (i % (2 * m) >= m) for m in LEVELS]
    tables += [j * np.ones((1, P)) == a for a in range(GH)]
    consts = np.concatenate([np.asarray(t, np.float32) for t in tables], 1)
    hmasks = np.zeros((P, 10, HALF), np.float32)
    for l, m in enumerate(LEVELS):
        t = np.arange(SEQ).reshape(-1, 2 * m)[:, m:].reshape(-1) % P
        hmasks[:, l, :len(t)] = (j // (2 * m) == t[None] // (2 * m)) & (j % (2 * m) < m)
    hmasks[:, 8:10, :] = (j == np.arange(T)[None] % P).reshape(P, 2, HALF)

    lngs = [ln_mix_g[0], ln_ffn_g[0], ln_mix_g[1], ln_ffn_g[1]]
    lnbs = [ln_mix_b[0], ln_ffn_b[0], ln_mix_b[1], ln_ffn_b[1]]
    conv = ab_conv_w[0].reshape(4, 12, P).transpose(2, 1, 0).reshape(P, 48)
    params = np.concatenate([_columns(g) for g in lngs] + [_columns(b) for b in lnbs]
                            + [conv, _columns(c_lb_raw[0]), _columns(c_lb_raw[1]), ab_gnorm_g.T, c_gnorm_g.T], 1)
    h_in = np.concatenate([meta_tokens, x[0]]).T.reshape(KT, P, T).transpose(1, 0, 2)

    arrays = {"h_in": h_in, "wstream": wstream, "wgate": gates, "consts": consts, "hmasks": hmasks,
              "params": params, "gate_params": np.stack([ab_a_log[0], ab_dt_bias[0]], 1)}
    arrays = {k: np.ascontiguousarray(v) for k, v in arrays.items()}
    nc = bacc.Bacc("TRN2", target_bir_lowering=False, num_devices=1)
    args = [nc.dram_tensor(k, v.shape, mybir.dt.from_np(v.dtype), kind="ExternalInput").ap() for k, v in arrays.items()]
    out = nc.dram_tensor("out", (KT, P, SEQ), F32, kind="ExternalOutput").ap()
    hybrid_trunk(nc, *args, out)
    result = run_bass_kernel_spmd(nc, [arrays], core_ids=[0])
    got = result.results[0]["out"]
    return np.ascontiguousarray(got.reshape(D, SEQ).T.reshape(1, SEQ, D))
```

```python
from contextlib import ExitStack

import concourse.bass as bass
from concourse import mybir

ALU = mybir.AluOpType
ACT = mybir.ActivationFunctionType
F32 = mybir.dt.float32
F32R = mybir.dt.float32r
BF16 = mybir.dt.bfloat16

P = 128
D = 1024
KT = D // P
SEQ, N_META = 512, 16
T = SEQ + N_META
HALF = T // 2
N_FULL = T // P
TAIL = T - N_FULL * P
DEPTH = 2
GH = 4
SH, SD = 8, 64
HH = 8
COLS = 256
ALPHA = float((2 * DEPTH) ** 0.25)
LN_EPS, RMS_EPS, L2_EPS = 1e-5, 1e-6, 1e-6
EXP_LN = "natural_log_exp_and_others"
LEVELS = [1, 2, 4, 8, 16, 32, 64]
NEG = -1e30

C_GE, C_SUFFIX, C_NEG, C_SHARED = 0, P, 2 * P, 3 * P
C_LEVEL, C_SEL = 0, len(LEVELS) * P
C_GDN = C_SEL + GH * P
P_LNG, P_LNB = 0, 4 * KT
P_CONV = 8 * KT
P_LB = P_CONV + 12 * 4
P_GN = P_LB + 2 * HH
P_ALL = P_GN + 2
ZW = 1376
Z_PARTS = [(0, 0, 512, 0), (1, 128, 400, 512), (0, 512, 16, 912), (4, 512, 16, 928),
           (2, 256, 272, 944), (3, 384, 160, 1216)]
Z_LAST = 928
Z_BANKS = [(0, 0, 512), (1, 512, 432), (2, 944, 432)]
QPAD = T + 16
KH = T - P
ALL, KEPT = slice(0, T), slice(N_META, T)

FILLED = 2
STEPS = 2 * KT
V_STEPS = 5 * KT

N_CONST_LOADS = 4
PHASES = [("qkv", 6), ("z0", 2), ("qk", 4), ("v0", 2), ("out0", 4), ("mlp0", 32),
          ("f", 4), ("v1", 4), ("q1", 4), ("z1", 4), ("out1", 4), ("mlp1", 32)]
N_STAGES = sum(n for _, n in PHASES)


def _counts():
    at, stages, feature, evacs = {}, 0, 0, 1
    for name, n in PHASES:
        at[name] = (stages, feature, evacs)
        stages += n
        if name not in ("v0", "v1"):
            feature += n
            evacs += n // 2 + n // 4 if name.startswith("mlp") else n
    at["end"] = (stages, feature, evacs)
    return at


AT = _counts()


def z_where(col):
    for bank, first, n in Z_BANKS:
        if first <= col < first + n:
            return bank, col - first


LATER = {3: (384, ZW - 160), 2: (256, ZW - 160 - 272), 1: (128, ZW - 160 - 272 - 400)}


def z_runs(tile, q0, q1):
    return [(c + max(s, q0) - s, max(s, q0), min(s + n, q1) - max(s, q0))
            for j, s, n, c in Z_PARTS if j == tile and max(s, q0) < min(s + n, q1)]


class Signal:

    def __init__(self, sem, per=1, step=1):
        self.sem, self.per, self.step = sem, per, step

    def at(self, i, k=None):
        k = self.per - 1 if k is None else k
        return i * (self.per * self.step) + (k + 1) * self.step


class HeadSignal:

    def __init__(self, both, a, together):
        self.sem, self.both, self.a, self.together = both.sem, both, a, together

    def at(self, i, k=None):
        per = self.both.per // 2
        k = per - 1 if k is None else k
        return self.both.at(i, self.a * per + k if self.together else 2 * k + self.a)


class HeadBuffers:

    FIRST, SECOND = 3 * T + 5 * SEQ, 4 * SEQ + T + P + 4

    def __init__(self, first, second):
        self.b, self.k, self.e = (first[:, x * T:(x + 1) * T] for x in range(3))
        rest = first[:, 3 * T:self.FIRST]
        self.ee, self.kt = (rest[:, x * 2 * SEQ:(x + 1) * 2 * SEQ].rearrange("p (s t) -> p s t", s=2) for x in range(2))
        self.qt = rest[:, 4 * SEQ:5 * SEQ].rearrange("p (s t) -> p s t", s=2)
        self.scores, kh_turned, states = (second[:, x * SEQ:(x + 1) * SEQ] for x in range(3))
        self.kh_turned, self.states = (x.rearrange("p (c t) -> p c t", c=4) for x in (kh_turned, states))
        self.kh = second[:, 3 * SEQ:3 * SEQ + T]
        self.v = second[:, 3 * SEQ + T:4 * SEQ + T + P].rearrange("p (c t) -> p c t", c=5)
        self.decay = second[:, 4 * SEQ + T + P:4 * SEQ + T + P + 3]


def hybrid_trunk(nc, h_in, wstream, wgate, consts, hmasks, params, gate_params, out):
    ctx = ExitStack()
    with ctx:
        def levels(n):
            return [(x, x + 1) for x, m in enumerate(LEVELS[1:]) if 2 * m <= n]

        def sb(name, shape, dt=F32, c=ctx):
            return c.enter_context(nc.sbuf_tensor(name, shape, dt))

        def sig(name, per=1, step=1):
            return Signal(ctx.enter_context(nc.semaphore(name)), per, step)

        def head_sigs(name, per=1, together=False):
            both = sig(name, 2 * per)
            return [HeadSignal(both, a, together) for a in range(2)]

        PS = ctx.enter_context(nc.psum_tensor("banks", [P, 8, 512], F32))

        xs = ExitStack()
        x_hi = sb("x_hi", [P, KT, T], F32R, c=xs)
        x_lo = sb("x_lo", [P, KT, T], F32R, c=xs)
        xs.close()
        head_1 = sb("head_1", [P, 2 * KT * T])
        h = sb("h", [P, KT, T])
        w_raw = sb("w_raw", [P, 2, KT * COLS])
        w_hi = sb("w_hi", [P, 2, KT * COLS], F32R)
        w_lo = sb("w_lo", [P, 2, KT * COLS], F32R)
        ident = sb("ident", [P, P])
        hmask = sb("hmask", [P, len(LEVELS) + 3, HALF], mybir.dt.uint8)
        dmask = hmask[:, 8:10, :].rearrange("p a t -> p (a t)")[:, 0:SEQ]
        par = sb("par", [P, P_ALL])
        ident_b = sb("ident_b", [P, P], BF16)
        neg_b = sb("neg_b", [P, P], BF16)
        ones = sb("ones", [P, P])
        ones_d = sb("ones_d", [P, P])
        ones_h = sb("ones_h", [P, P])
        small = sb("small", [P, 4])
        eps_ln, eps_rms = small[:, 0:1], small[:, 1:2]
        gp = sb("gp", [GH, 3])
        lbt = sb("lbt", [P, 8, HH])
        lb, one_minus_lb = lbt[:, 0, :], lbt[:, 1, :]

        m0 = ExitStack()
        qkv = sb("qkv", [P, 12, T], c=m0)
        zqk = sb("zqk", [P, 3 * GH, T], c=m0)
        z0, qk = zqk[:, 0:GH, :], zqk[:, GH:3 * GH, :]
        vt = sb("vt", [P, 5, SH * SD], c=m0)
        con = sb("con", [P, C_SHARED], c=m0)
        ge_mask = con[:, C_GE:C_GE + P]
        suffix = con[:, C_SUFFIX:C_SUFFIX + P]

        def level_mask(n, l):
            return gdn_con[0:n, C_LEVEL + l * P:C_LEVEL + l * P + n]

        def heads(ap, n):
            return ap.rearrange("p (o n) -> p o n", o=1).broadcast_to((n, GH, n))

        def sel_of(a):
            return gdn_con[0:GH, C_SEL + a * P:C_SEL + (a + 1) * P]

        ga = ExitStack()
        gdn_con = sb("gdn_con", [P, C_GDN], c=ga)
        wg = sb("wg", [P, KT, 36], c=ga)
        beta = sb("beta", [GH, T], c=ga)
        gcum = sb("gcum", [GH, T], c=ga)
        colg = sb("colg", [P, N_FULL + 1, 2, GH], c=ga)
        cv = ExitStack()
        conv_in = sb("conv_in", [P, 2, T + 3], c=cv)
        conv_acc = sb("conv_acc", [P, 2, T], c=cv)
        nrm_a = sb("nrm_a", [P, 2, 2, T], c=cv)
        gtmp = sb("gtmp", [GH, 3, T], c=cv)
        cv.close()
        lp = ExitStack()
        kS, qS, vS, GB, BB, DM, MT, TT, XS, AT0, VB, EG, SS = (
            sb(n, [P, GH, P], c=lp) for n in ("kS", "qS", "vS", "GB", "BB", "DM", "MT", "TT", "XS", "AT0", "VB",
                    "EG", "SS"))
        TM, KD = BB, DM
        RR, VN = GB, MT
        ML = sb("ML", [P, 2, GH, P], c=lp)
        gsm = sb("gsm", [P, 6, GH], c=lp)
        gcol, bcol, gdiff, kd4, eg4, nb4 = (gsm[:, x, :] for x in range(6))
        gsel = sb("gsel", [GH, 2, P], c=lp)
        lp.close()
        ga.close()
        at = ExitStack()
        sq_k = sb("sq_k", [P, 640], c=at)
        sq_q = sb("sq_q", [P, QPAD], c=at)
        sq_v = sb("sq_v", [P, 5, P], c=at)
        zs = sb("zs", [P, 2, ZW], c=at)
        nb = ExitStack()
        nrm_b = sb("nrm_b", [P, 2, 2, T], c=nb)
        nb.close()
        sp = sb("sp", [P, 2, ZW], c=at)
        wt = sb("wt", [P, 2, ZW], c=at)
        at.close()
        m0.close()
        ln = ExitStack()
        rstd = sb("rstd", [P, T], c=ln)
        lnsq = sb("lnsq", [P, 4, T], c=ln)
        ln.close()
        ml = ExitStack()
        hid_hi = sb("hid_hi", [P, 16, T], F32R, c=ml)
        hid_lo = sb("hid_lo", [P, 16, T], F32R, c=ml)
        relu = sb("relu", [P, 2, T], c=ml)
        sqr = sb("sqr", [P, 2, T], c=ml)
        ln_sum = sb("ln_sum", [P, T], c=ml)
        ml.close()
        m1 = ExitStack()
        fg = sb("fg", [P, HH, T], c=m1)
        q1 = sb("q1", [P, HH, T], c=m1)
        z1 = sb("z1", [P, HH, T], c=m1)
        v1 = sb("v1", [P, 5, D], c=m1)
        hl = ExitStack()
        mk = ExitStack()
        mask_in = sb("mask_in", [P, len(LEVELS) + 3, HALF], c=mk)
        mk.close()
        head_sets = [HeadBuffers(sb("head_0a", [P, HeadBuffers.FIRST], c=hl)[:, :],
                                 sb("head_0b", [P, HeadBuffers.SECOND], c=hl)[:, :]),
                     HeadBuffers(head_1[:, 0:HeadBuffers.FIRST], head_1[:, KT * T:KT * T + HeadBuffers.SECOND])]
        hl.close()
        nrm_c = sb("nrm_c", [P, 2, 2, T], c=m1)
        m1.close()

        consts_loaded = sig("consts_loaded", step=16)
        h_loaded = [sig(f"h_loaded{x}", step=16) for x in range(2)]
        gdn_consts_loaded, masks_loaded = sig("gdn_consts_loaded", step=16), sig("masks_loaded", step=16)
        masks_made = sig("masks_made")
        wgate_loaded = sig("wgate_loaded", step=16)
        out_stored = sig("out_stored", step=16)
        w_loaded = [sig(f"w_loaded{u}", step=16) for u in range(2)]
        w_hi_made, w_lo_made = sig("w_hi_made"), sig("w_lo_made")
        half_done, stage_done = sig("half_done"), sig("stage_done")
        evac = [sig("evacuated0"), sig("evacuated1")]
        act_waited, dve_waited, pool_waited = sig("act_waited"), sig("dve_waited"), sig("pool_waited")
        tile_done = [half_done, stage_done]
        v_tile_done0 = sig("v_tile_done0", 4)
        v_tile_done1 = sig("v_tile_done1", 4)
        v_evacuated0 = sig("v_evacuated0", 5)
        v_evacuated1 = sig("v_evacuated1", 5)
        gdn_hi_made = sig("gdn_hi_made", GH)
        hg_hi_made = sig("hg_hi_made", HH)
        x_lo_made = sig("x_lo_made", KT)
        out_ready = sig("out_ready", KT)
        m_made = sig("m_made", 2)
        x_done = sig("x_done", 6)
        level_masked = sig("level_masked", 6)
        b_made = head_sigs("b_made", 5, together=True)
        level_scaled = head_sigs("level_scaled", 7)
        level_exponent = head_sigs("level_exponent", 7)
        norm_squared = sig("norm_squared")
        norm_summed = sig("norm_summed")
        norm_logged = sig("norm_logged")
        ln_mean_ready = sig("ln_mean_ready")
        ln_squared = sig("ln_squared", KT)
        ln_square_used = sig("ln_square_used", KT // 2)
        ln_paired = sig("ln_paired", KT // 2)
        hidden_lo_made = sig("hidden_lo_made", 16)
        consts_made = sig("consts_made")
        gates_done = sig("gates_done")
        beta_made = sig("beta_made")
        gcum_made = sig("gcum_made", 5)
        columns_done = sig("columns_done")
        columns_made = sig("columns_made")
        gate_rows_staged = sig("gate_rows_staged")
        decay_rows_done = sig("decay_rows_done")
        beta_rows_done = sig("beta_rows_done")
        heads_staged = sig("heads_staged")
        kk_done = sig("kk_done")
        qk_done = sig("qk_done")
        k_turned = sig("k_turned")
        state_ready = sig("state_ready")
        v_turned = sig("v_turned")
        tt_first = sig("tt_first")
        t_turned = sig("t_turned")
        t_first = sig("t_first")
        t_updated = sig("t_updated", 5)
        tt_updated = sig("tt_updated", 6)
        x_copied = sig("x_copied", 6)
        p1_done = sig("p1_done", 5)
        p2_done = sig("p2_done", 6)
        ks_done = sig("ks_done")
        r_made = sig("r_made")
        a_made = sig("a_made")
        vnew_done = sig("vnew_done")
        vnew_copied = sig("vnew_copied")
        qd_made = sig("qd_made")
        kd_made = sig("kd_made")
        o_done = sig("o_done")
        kv_done = sig("kv_done")
        o_copied = sig("o_copied")
        pair_staged = sig("pair_staged")
        z_done = sig("z_done", 2)
        softplus_made = sig("softplus_made", 2)
        later_summed = sig("later_summed", 6)
        z_copied = sig("z_copied", 2)
        suffix_done = sig("suffix_done", 2)
        weights_made = sig("weights_made", 2)
        values_staged = sig("values_staged")
        values_done = sig("values_done", 2)
        pair_free = sig("pair_free")
        z0_gated = sig("z0_gated")
        gdn_lo_made = sig("gdn_lo_made", GH)
        level_taken = head_sigs("level_taken", 8)
        level_product = head_sigs("level_product", 7)
        diag_product = head_sigs("diag_product")
        kh_made = head_sigs("kh_made")
        kh_turned = head_sigs("kh_turned")
        kh_copied = head_sigs("kh_copied")
        kv1_done = head_sigs("kv1_done")
        states_made = head_sigs("states_made", 4)
        qd1_made = head_sigs("qd1_made")
        o1_done = head_sigs("o1_done")
        o_bank_free = head_sigs("o_bank_free")
        hg_lo_made = sig("hg_lo_made", HH)
        norm_scaled = sig("norm_scaled")
        ln_centered = sig("ln_centered", KT)
        ln_logged = sig("ln_logged")
        ln_rstd_made = sig("ln_rstd_made")
        ln_scaled = sig("ln_scaled", KT)
        x_hi_made = sig("x_hi_made", KT)
        hidden_squared = sig("hidden_squared", 16)
        hidden_hi_made = sig("hidden_hi_made", 16)
        wg_cleared = sig("wg_cleared")
        conv_tap_added = sig("conv_tap_added", 4)
        qkv_made = sig("qkv_made")
        rate_made = sig("rate_made")
        lb_exp = sig("lb_exp")
        decay_logit_made = sig("decay_logit_made")
        gate_soft = sig("gate_soft", 3)
        norm_applied = sig("norm_applied")
        gb_made = sig("gb_made")
        eg_made = sig("eg_made")
        bb_made = sig("bb_made")
        gdiff_made = sig("gdiff_made")
        col_decay_made = sig("col_decay_made")
        dm_exponent = sig("dm_exponent")
        dm_exp = sig("dm_exp")
        pads_cleared = sig("pads_cleared")
        z_abs = sig("z_abs", 2)
        z_exp = sig("z_exp", 2)
        z_log = sig("z_log", 2)
        logits_made = sig("logits_made", 2)
        pair_hi_made = sig("pair_hi_made")
        norm_gated = sig("norm_gated")
        ln_partial = sig("ln_partial", KT + 1)
        f_made = sig("f_made")
        logf_made = head_sigs("logf_made")
        eb_made = head_sigs("eb_made")
        level_exp = head_sigs("level_exp", 7)
        kh_exponent = head_sigs("kh_exponent")
        kh_exp = head_sigs("kh_exp")
        ln_shifted = sig("ln_shifted", KT)
        lb_step = sig("lb_step", 9)
        softplus0 = sig("softplus0")
        g_made = sig("g_made")
        gcol_staged = sig("gcol_staged")
        dm_made = sig("dm_made")
        m_first = sig("m_first")
        vb_made = sig("vb_made")
        hg_cleared = sig("hg_cleared", 2)
        k_made = head_sigs("k_made")
        chunk_decay_made = head_sigs("chunk_decay_made")

        block = ctx.enter_context(nc.Block())

        def part(ap, m, which):
            return ap.rearrange("p (b s r) -> p b s r", s=2, r=m)[:, :, which, :]

        def halves(ap):
            return ap.rearrange("p (a t) -> p a t", a=2)

        def norm_bank(r, g):
            return 4 if r == 0 else 4 * (g % 2)

        def half(tokens):
            return (tokens.stop - tokens.start) // 2

        def pair(m, tokens=ALL):
            return PS[:, 2 * m:2 * m + 2, 0:half(tokens)]

        @block.sync
        def _(sp_):
            def load_stage(n, u):
                sp_.dma_start(w_raw[:, u, :], wstream[n]).then_inc(w_loaded[u].sem, 16)

            load_stage(0, 0)
            for x in range(2):
                tiles = slice(x * KT // 2, (x + 1) * KT // 2)
                sp_.dma_start(h[:, tiles, :], h_in[:, tiles, :]).then_inc(h_loaded[x].sem, 16)
            load_stage(1, 1)
            with sp_.Fori(1, N_STAGES // 2) as i:
                for u in range(2):
                    sp_.wait_ge(w_lo_made.sem, i * 2 + (u - 1))
                    load_stage(i * 2 + u, u)
            for k in range(KT):
                sp_.wait_ge(out_ready.sem, out_ready.at(0, k))
                sp_.dma_start(out[k], h[:, k, N_META:T]).then_inc(out_stored.sem, 16)
            sp_.wait_ge(out_stored.sem, 16 * KT)

        @block.gpsimd
        def _(pool):
            def split_hi(n, u, first, round_):
                pool.wait_ge(w_loaded[u].sem, w_loaded[u].at(round_))
                if not first:
                    pool.wait_ge(stage_done.sem, n - 1)
                pool.sem_inc(pool_waited.sem, 1)
                pool.tensor_scalar(w_hi[:, u, :], w_raw[:, u, :], 1.0, 0.0, ALU.mult,
                        ALU.add).then_inc(w_hi_made.sem, 1)

            def split_lo(n, u):
                pool.wait_ge(w_hi_made.sem, w_hi_made.at(n))
                pool.tensor_tensor(w_lo[:, u, :], w_raw[:, u, :], w_hi[:, u, :].bitcast(F32),
                                   ALU.subtract).then_inc(w_lo_made.sem, 1)

            def split(n, u, first, round_):
                split_hi(n, u, first, round_)
                split_lo(n, u)

            def split_rounds(a, b):
                with pool.Fori(a, b) as i:
                    for u in range(2):
                        split(i * 2 + u, u, False, i)

            for u in range(2):
                split(u, u, True, 0)
            split_rounds(1, AT["qk"][0] // 2 + 1)

            pool.wait_ge(gdn_consts_loaded.sem, gdn_consts_loaded.at(0))

            def mask_level(i, n, l):
                pool.wait_ge(m_made.sem, m_made.at(i))
                if l > 1:
                    pool.wait_ge(x_done.sem, x_done.at(i, l - 2))
                pool.tensor_tensor(ML[0:n, l % 2, :, 0:n], MT[0:n, :, 0:n], heads(level_mask(n, l + 1), n),
                                   ALU.mult).then_inc(level_masked.sem, 1)

            n0 = AT["qk"][0]
            with pool.Fori(0, FILLED) as i:
                mask_level(i, P, 0)
                mask_level(i, P, 1)
                mask_level(i, P, 2)
                mask_level(i, P, 3)
                mask_level(i, P, 4)
                split_hi(i * 2 + (n0 + 2), 0, False, i + (n0 // 2 + 1))
                mask_level(i, P, 5)
                split_lo(i * 2 + (n0 + 2), 0)
                split(i * 2 + (n0 + 3), 1, False, i + (n0 // 2 + 1))
            n0 = AT["v0"][0]
            for i in range(FILLED, N_FULL):
                for l, _ in levels(P):
                    mask_level(i, P, l)
                split(n0 + i, i - FILLED, False, n0 // 2 + 1)
            for l, _ in levels(TAIL):
                mask_level(N_FULL, TAIL, l)
            split_rounds(n0 // 2 + 2, AT["out1"][0] // 2)

            with pool.Fori(0, HH // 2) as i:
                for l, m in enumerate(LEVELS):
                    for a, hb in enumerate(head_sets):
                        first, second = part(hb.b[:, N_META:T], m, 0), part(hb.b[:, N_META:T], m, 1)
                        middle = first[:, :, m - 1:m].broadcast_to((P, SEQ // (2 * m), m))
                        if l == 0:
                            pool.wait_ge(b_made[a].sem, b_made[a].at(i))
                        if l > 1:
                            pool.wait_ge(level_scaled[a].sem, level_scaled[a].at(i, l - 2))
                        pool.tensor_tensor(part(hb.ee[:, l % 2, :], m, 0), middle, first, ALU.subtract)
                        pool.tensor_tensor(part(hb.ee[:, l % 2, :], m, 1), second, middle,
                                           ALU.subtract).then_inc(level_exponent[a].sem, 1)
            split_rounds(AT["out1"][0] // 2, N_STAGES // 2)

        @block.tensor
        def _(pe):
            def stage_fm(n, u, rhs, evacuated, start=True, stop=True, fresh=None,
                         halves=(0, 1), made=x_lo_made, tokens=ALL):
                pe.wait_ge(w_lo_made.sem, w_lo_made.at(n))
                t0, width = tokens.start, half(tokens)
                for m in halves:
                    if evacuated is not None:
                        pe.wait_ge(evac[m].sem, evacuated)
                    for k in range(KT):
                        w = slice(k * COLS + m * P, k * COLS + m * P + P)
                        hi, lo = rhs(k)
                        if fresh is not None and m == 0:
                            pe.wait_ge(made.sem, made.at(fresh, k))
                        for w_part, x_part in ((w_hi, hi), (w_hi, lo), (w_lo, hi)):
                            for j in range(2):
                                mm = pe.matmul(PS[:, 2 * m + j, 0:width], w_part[:, u, w],
                                               x_part[:, t0 + j * width:t0 + (j + 1) * width],
                                               start=start and k == 0 and w_part is w_hi and x_part is hi,
                                               stop=stop and k == KT - 1 and w_part is w_lo)
                    mm.then_inc((stage_done if m else half_done).sem, 1)

            def x_tile(k):
                return x_hi[:, k, :], x_lo[:, k, :]

            def project(name, rounds, fresh=None, made=x_lo_made, tokens=ALL):
                n0, _, e0 = AT[name]
                if fresh is not None:
                    for u in range(2):
                        stage_fm(n0 + u, u, x_tile, e0 + u, fresh=fresh if u == 0 else None, made=made,
                                 tokens=tokens)
                with pe.Fori(0 if fresh is None else 1, rounds) as i:
                    for u in range(2):
                        stage_fm(i * 2 + (n0 + u), u, x_tile, i * 2 + (e0 + u), tokens=tokens)

            def project_tokens(name, v_done, v_evac, rounds, first_full):
                n0 = AT[name][0]
                
                def stage(n, u, since, first):
                    pe.wait_ge(w_lo_made.sem, w_lo_made.at(n))
                    for j in range(5):
                        rows = min(P, T - j * P)
                        if not first:
                            pe.wait_ge(v_evac.sem, v_evac.at(since - 1, j))
                        at = first_full + j * P if j < N_FULL else 0
                        for k in range(KT):
                            for x_part, w_part in ((x_hi, w_hi), (x_hi, w_lo), (x_lo, w_hi)):
                                mm = pe.matmul(PS[0:rows, j, 0:COLS], x_part[:, k, at:at + rows],
                                               w_part[:, u, k * COLS:(k + 1) * COLS],
                                               start=k == 0 and x_part is x_hi and w_part is w_hi,
                                               stop=k == KT - 1 and x_part is x_lo)
                        mm.then_inc((stage_done if j == 4 else v_done).sem, 1)

                for m in range(2):
                    pe.wait_ge(evac[m].sem, AT[name][2])
                stage(n0, 0, 0, True)
                stage(n0 + 1, 1, 1, False)
                if rounds > 1:
                    with pe.Fori(1, rounds) as i:
                        for u in range(2):
                            stage(i * 2 + (n0 + u), u, i * 2 + u, False)
                pe.wait_ge(v_evac.sem, v_evac.at(2 * rounds - 1))

            def head_norm_sums(r, groups, sq, weight, tokens=ALL):
                for g in groups:
                    pe.wait_ge(norm_squared.sem, norm_squared.at(r + g))
                    before = 1 if r == 0 else 2
                    if g >= before:
                        pe.wait_ge(norm_logged.sem, norm_logged.at(r + g - before))
                    for a in range(2):
                        for j in range(2):
                            first, width = tokens.start + j * half(tokens), half(tokens)
                            mm = pe.matmul(PS[:, norm_bank(r, g) + 2 * a + j, 0:width], weight[:, :],
                                           sq[:, g % 2, a, first:first + width], start=True, stop=True)
                    mm.then_inc(norm_summed.sem, 1)

            def layer_norm_sums(r, after, tokens=ALL):
                for m in range(2):
                    pe.wait_ge(evac[m].sem, AT[after][2])
                pe.wait_ge(ln_partial.sem, ln_partial.at(r))
                t0, width = tokens.start, half(tokens)
                for j in range(2):
                    mm = pe.matmul(PS[:, 4 + j, 0:width], ones_d[:, :],
                            ln_sum[:, t0 + j * width:t0 + (j + 1) * width],
                                   start=True, stop=True)
                mm.then_inc(ln_mean_ready.sem, 1)
                for pair_ in range(KT // 2):
                    pe.wait_ge(ln_paired.sem, ln_paired.at(r, pair_))
                    for j in range(2):
                        mm = pe.matmul(PS[:, 6 + j, 0:width], ones_d[:, :],
                                       lnsq[:, 2 * pair_ % 4, t0 + j * width:t0 + (j + 1) * width],
                                       start=pair_ == 0, stop=pair_ == KT // 2 - 1)
                    mm.then_inc(ln_square_used.sem, 1)

            def mlp(name, r, fresh, tokens=ALL):
                n0, _, e0 = AT[name]
                for hf in range(2):
                    n1, e1 = n0 + 16 * hf, e0 + 12 * hf
                    if hf == 0:
                        for u in range(2):
                            stage_fm(n1 + u, u, x_tile, e1 + u, fresh=fresh if u == 0 else None, tokens=tokens)
                    with pe.Fori(1 if hf == 0 else 0, 4) as i:
                        for u in range(2):
                            stage_fm(i * 2 + (n1 + u), u, x_tile, i * 2 + (e1 + u), tokens=tokens)
                    with pe.Fori(0, 4) as i:
                        for u in range(2):
                            pe.wait_ge(hidden_lo_made.sem, hidden_lo_made.at(r * 2 + hf, 8 * u + 7))
                            stage_fm(i * 2 + (n1 + 8 + u), u,
                                     lambda k: (hid_hi[:, 8 * u + k, :], hid_lo[:, 8 * u + k, :]),
                                     i + (e1 + 8) if u == 0 else None, start=u == 0, stop=u == 1, tokens=tokens)

            project("qkv", 3, 0)

            pe.wait_ge(wgate_loaded.sem, 32)
            pe.wait_ge(consts_loaded.sem, consts_loaded.at(N_CONST_LOADS - 1))
            pe.wait_ge(consts_made.sem, consts_made.at(0))
            pe.wait_ge(gdn_consts_loaded.sem, gdn_consts_loaded.at(0))
            for j in range(2):
                for k in range(KT):
                    mm = pe.matmul(PS[0:36, 4 + j, 0:HALF], wg[:, k, :], h[:, k, j * HALF:(j + 1) * HALF],
                                   start=k == 0, stop=k == KT - 1)
            mm.then_inc(gates_done.sem, 1)
            n0, _, e0 = AT["z0"]
            stage_fm(n0, 0, x_tile, e0)
            pe.wait_ge(beta_made.sem, beta_made.at(0))
            pe.wait_ge(gcum_made.sem, gcum_made.at(0))
            for c in range(N_FULL + 1):
                n = min(P, T - c * P)
                pe.transpose(PS[0:n, 6, 8 * c:8 * c + 4], beta[:, c * P:c * P + n], ident[0:GH, 0:GH])
                mm = pe.transpose(PS[0:n, 6, 8 * c + 4:8 * c + 8], gcum[:, c * P:c * P + n], ident[0:GH, 0:GH])
            mm.then_inc(columns_done.sem, 1)
            pe.wait_ge(columns_made.sem, columns_made.at(0))
            head_norm_sums(0, range(1), nrm_a, ones)
            stage_fm(n0 + 1, 1, x_tile, e0 + 1, halves=(0,))
            head_norm_sums(0, range(1, 2), nrm_a, ones)
            stage_fm(n0 + 1, 1, x_tile, e0 + 1, halves=(1,))
            head_norm_sums(0, range(2, 4), nrm_a, ones)
            pe.wait_ge(norm_logged.sem, norm_logged.at(3))

            def v0_steps(u, s0, s1):
                n = AT["v0"][0] + u
                for step in range(s0, s1):
                    j, k = step // KT, step % KT
                    rows, count = min(P, T - j * P), 5 * u + j
                    if step == 0:
                        pe.wait_ge(w_lo_made.sem, w_lo_made.at(n))
                    if k == 0 and count < 4:
                        pe.wait_ge(evac[count // 2].sem, AT["v0"][2])
                    elif k == 0:
                        pe.wait_ge(v_evacuated0.sem, v_evacuated0.at(0, count - 4))
                    for x_part, w_part in ((x_hi, w_hi), (x_hi, w_lo), (x_lo, w_hi)):
                        mm = pe.matmul(PS[0:rows, count % 4, 0:COLS], x_part[:, k, j * P:j * P + rows],
                                       w_part[:, u, k * COLS:(k + 1) * COLS],
                                       start=k == 0 and x_part is x_hi and w_part is w_hi,
                                       stop=k == KT - 1 and x_part is x_lo)
                    if k == KT - 1:
                        mm.then_inc((stage_done if j == 4 else v_tile_done0).sem, 1)

            def gdn_chunk(i, n, last, filled):
                n0, _, e0 = AT["qk"]

                def fill(s0, s1):
                    if filled == "v":
                        v0_steps(i - FILLED, s0 * V_STEPS // (2 * STEPS), s1 * V_STEPS // (2 * STEPS))
                    if filled != "qk":
                        return
                    for step in range(s0, s1):
                        u, m, k = step // STEPS, step // KT % 2, step % KT
                        if m == 0 and k == 0:
                            pe.wait_ge(w_lo_made.sem, w_lo_made.at(i * 2 + (n0 + u)))
                        if k == 0:
                            pe.wait_ge(evac[m].sem, i * 2 + (e0 + u))
                        w = slice(k * COLS + m * P, k * COLS + m * P + P)
                        for w_part, x_part in ((w_hi, x_hi), (w_hi, x_lo), (w_lo, x_hi)):
                            for j in range(2):
                                mm = pe.matmul(PS[:, 2 * m + j, 0:HALF], w_part[:, u, w],
                                               x_part[:, k, j * HALF:(j + 1) * HALF],
                                               start=k == 0 and w_part is w_hi and x_part is x_hi,
                                               stop=k == KT - 1 and w_part is w_lo)
                        if k == KT - 1:
                            mm.then_inc(tile_done[m].sem, 1)

                def each(bank, lhs, rhs, width=P, rows=n, signal=None, start=True, stop=True):
                    for a in range(GH):
                        mm = pe.matmul(PS[0:rows, bank, a * P:a * P + width], lhs(a), rhs(a), start=start, stop=stop)
                    if signal is not None:
                        mm.then_inc(signal.sem, 1)

                fill(0, 2)
                pe.wait_ge(gate_rows_staged.sem, gate_rows_staged.at(i))
                each(4, lambda a: sel_of(a), lambda a: gsel[0:GH, 0, 0:n], n, P, decay_rows_done)
                pe.wait_ge(state_ready.sem, state_ready.at(i))
                each(5, lambda a: sel_of(a), lambda a: gsel[0:GH, 1, 0:n], n, P, beta_rows_done)
                pe.wait_ge(heads_staged.sem, heads_staged.at(i))
                each(6, lambda a: kS[:, a, 0:n], lambda a: kS[:, a, 0:n], n, n, kk_done)
                each(7, lambda a: kS[:, a, 0:n], lambda a: qS[:, a, 0:n], n, n, qk_done)
                pe.wait_ge(gb_made.sem, gb_made.at(i))
                pe.wait_ge(eg_made.sem, eg_made.at(i))
                for a in range(GH):
                    mm = pe.transpose(PS[0:n, 4, a * P:(a + 1) * P], kS[:, a, 0:n], ident[:, :])
                mm.then_inc(k_turned.sem, 1)
                pe.wait_ge(bb_made.sem, bb_made.at(i))
                for a in range(GH):
                    mm = pe.transpose(PS[0:n, 5, a * P:(a + 1) * P], vS[:, a, 0:n], ident[:, :])
                mm.then_inc(v_turned.sem, 1)
                fill(2, 4)
                pe.wait_ge(tt_first.sem, tt_first.at(i))
                for a in range(GH):
                    mm = pe.transpose(PS[0:n, 6, a * P:a * P + n], TT[0:n, a, 0:n], ident[0:n, 0:n])
                mm.then_inc(t_turned.sem, 1)
                fill(4, 5)
                pe.wait_ge(t_first.sem, t_first.at(i))
                pe.wait_ge(a_made.sem, a_made.at(i))
                last_level = len(levels(n)) - 1
                for l, _ in levels(n):
                    pe.wait_ge(level_masked.sem, level_masked.at(i, l))
                    if l:
                        pe.wait_ge(t_updated.sem, t_updated.at(i, l - 1))
                        pe.wait_ge(tt_updated.sem, tt_updated.at(i, l - 1))
                    each(7, lambda a: ML[0:n, l % 2, a, 0:n], lambda a: TM[0:n, a, 0:n], n, n, x_done)
                    fill(4 * l + 5, 4 * l + 7)
                    pe.wait_ge(x_copied.sem, x_copied.at(i, l))
                    if l == 0:
                        pe.wait_ge(kd_made.sem, kd_made.at(i))
                        pe.wait_ge(vb_made.sem, vb_made.at(i))
                    if l < last_level:
                        each(4, lambda a: TT[0:n, a, 0:n], lambda a: XS[0:n, a, 0:n], n, n, p1_done)
                    each(5, lambda a: XS[0:n, a, 0:n], lambda a: TT[0:n, a, 0:n], n, n, p2_done)
                    fill(4 * l + 7, 4 * l + 9)
                each(6, lambda a: kS[:, a, 0:n], lambda a: SS[:, a, :], P, n, ks_done)
                fill(29, 30)
                pe.wait_ge(tt_updated.sem, tt_updated.at(i, last_level))
                pe.wait_ge(r_made.sem, r_made.at(i))
                each(7, lambda a: TT[0:n, a, 0:n], lambda a: RR[0:n, a, :], P, n, vnew_done)
                fill(30, 31)
                pe.wait_ge(vnew_copied.sem, vnew_copied.at(i))
                pe.wait_ge(qd_made.sem, qd_made.at(i))
                for a in range(GH):
                    pe.matmul(PS[:, 4, a * P:a * P + n], VN[0:n, a, :], AT0[0:n, a, 0:n], start=True, stop=False)
                    mm = pe.matmul(PS[:, 4, a * P:a * P + n], SS[:, a, :], qS[:, a, 0:n], start=False, stop=True)
                mm.then_inc(o_done.sem, 1)
                if not last:
                    each(5, lambda a: KD[0:n, a, :], lambda a: VN[0:n, a, :], P, P, kv_done)
                    fill(31, 32)
                    pe.wait_ge(o_copied.sem, o_copied.at(i))

            with pe.Fori(0, FILLED) as i:
                gdn_chunk(i, P, False, "qk")
            for i in range(FILLED, N_FULL):
                gdn_chunk(i, P, False, "v")
            gdn_chunk(N_FULL, TAIL, True, None)
            pe.wait_ge(o_copied.sem, o_copied.at(N_FULL))

            head_norm_sums(4, range(2), nrm_b, ones_h)
            pe.wait_ge(norm_logged.sem, norm_logged.at(5))

            def scores(i, a, first=False):
                if a == 0:
                    pe.wait_ge(pair_staged.sem, pair_staged.at(i))
                if not first:
                    pe.wait_ge(logits_made.sem, logits_made.at(i - 1, a))
                rows = slice(a * SD, (a + 1) * SD)
                for j, q0, cnt, col in Z_PARTS:
                    bank, c = z_where(col)
                    diag = q0 == j * P
                    mm = pe.matmul(PS[:, 3 * a + bank, c:c + cnt], sq_k[rows, j * P:(j + 1) * P],
                                   sq_q[rows, q0:q0 + cnt], start=True, stop=not diag)
                    if diag:
                        w = min(P, cnt)
                        mm = pe.matmul(PS[:, 3 * a + bank, c:c + w], ident_b[:, :], neg_b[:, 0:w],
                                       start=False, stop=True)
                mm.then_inc(z_done.sem, 1)

            def suffix_sums(i, a):
                pe.wait_ge(softplus_made.sem, softplus_made.at(i, a))
                for j, q0, cnt, col in sorted(Z_PARTS, key=lambda part: -part[0]):
                    bank, c = z_where(col)
                    q, end = max(q0, (j + 1) * P), min(q0 + cnt, T)
                    later = q < end
                    mm = pe.matmul(PS[:, 3 * a + bank, c:c + cnt], suffix[:, :], sp[:, a, col:col + cnt],
                                   start=True, stop=not later)
                    if later and j == 3:
                        mm = pe.matmul(PS[:, 3 * a + bank, c + q - q0:c + end - q0], ones[:, :],
                                       sp[:, a, Z_LAST:Z_LAST + end - q], start=False, stop=True)
                    elif later:
                        first, at = LATER[j + 1]
                        if q0 == j * P:
                            pe.wait_ge(later_summed.sem, later_summed.at(i, 3 * a + 2 - j))
                        mm = pe.matmul(PS[:, 3 * a + bank, c + q - q0:c + end - q0], ones[:, :],
                                       wt[:, a, at + q - first:at + end - first], start=False, stop=True)
                mm.then_inc(suffix_done.sem, 1)

            def weighted_values(i, a):
                if a == 0:
                    pe.wait_ge(pair_free.sem, pair_free.at(i))
                    pe.wait_ge(values_staged.sem, values_staged.at(i))
                pe.wait_ge(weights_made.sem, weights_made.at(i, a))
                rows = slice(a * SD, (a + 1) * SD)
                for bank, qa, qb in ((6, 0, 512), (7, 512, T)):
                    runs = [(j, r, q, m) for j in range(5) for r, q, m in z_runs(j, qa, qb)]
                    for x, (j, r, q, m) in enumerate(runs):
                        mm = pe.matmul(PS[rows, bank, q - qa:q - qa + m], sq_v[:, j, rows], wt[:, a, r:r + m],
                                       start=x == 0, stop=x == len(runs) - 1)
                mm.then_inc(values_done.sem, 1)

            pe.wait_ge(pads_cleared.sem, pads_cleared.at(0))
            scores(0, 0, True)
            scores(0, 1, True)
            with pe.Fori(0, SH // 2 - 1) as i:
                suffix_sums(i, 0)
                suffix_sums(i, 1)
                scores(i + 1, 0)
                scores(i + 1, 1)
                weighted_values(i, 0)
                weighted_values(i, 1)
            for a in range(2):
                suffix_sums(SH // 2 - 1, a)
            for a in range(2):
                weighted_values(SH // 2 - 1, a)
            pe.wait_ge(pair_free.sem, pair_free.at(SH // 2))

            pe.wait_ge(gdn_lo_made.sem, gdn_lo_made.at(0))
            project("out0", 2)
            layer_norm_sums(0, "mlp0")
            mlp("mlp0", 0, 1)
            layer_norm_sums(1, "f")

            project("f", 2, 2)
            project_tokens("v1", v_tile_done1, v_evacuated1, 2, N_META)
            project("q1", 2, tokens=KEPT)
            project("z1", 2, tokens=KEPT)
            for m in range(2):
                pe.wait_ge(evac[m].sem, AT["out1"][2])

            with pe.Fori(0, HH // 2) as i:
                def chunk(c):
                    return slice(N_META + c * P, N_META + (c + 1) * P)

                def diagonal(a, hb):
                    pe.wait_ge(k_made[a].sem, k_made[a].at(i))
                    for c in range(N_FULL):
                        mm = pe.matmul(PS[:, 6 + a, c * P:(c + 1) * P], hb.k[:, chunk(c)], q1[:, i * 2 + a, chunk(c)],
                                       start=True, stop=True)
                    mm.then_inc(diag_product[a].sem, 1)

                for l, m in enumerate(LEVELS):
                    for a, hb in enumerate(head_sets):
                        if l == 0:
                            diagonal(a, hb)
                        pe.wait_ge(level_scaled[a].sem, level_scaled[a].at(i, l))
                        if l > 1:
                            pe.wait_ge(level_taken[a].sem, level_taken[a].at(i, l - 1))
                        for c in range(N_FULL):
                            mm = pe.matmul(PS[:, 2 * a + l % 2, 64 * c:64 * c + 64],
                                    hb.kt[:, l % 2, c * P:(c + 1) * P],
                                           hb.qt[:, l % 2, 64 * c:64 * c + 64], start=True, stop=True)
                        mm.then_inc(level_product[a].sem, 1)
                    if l == 0:
                        for a, hb in enumerate(head_sets):
                            pe.wait_ge(kh_made[a].sem, kh_made[a].at(i))
                            pe.wait_ge(o_bank_free[a].sem, o_bank_free[a].at(i))
                            for c in range(N_FULL - 1):
                                pe.transpose(PS[:, 4 + a, c * P:(c + 1) * P], hb.kh[:, chunk(c)], ident[:, :])
                            mm = pe.transpose(PS[0:N_META, 4 + a, 3 * P:4 * P], hb.kh[:, 0:N_META], ident[:, :])
                            mm.then_inc(kh_turned[a].sem, 1)
                    if l == 1:
                        for a, hb in enumerate(head_sets):
                            pe.wait_ge(kh_copied[a].sem, kh_copied[a].at(i))
                            pe.wait_ge(level_taken[a].sem, level_taken[a].at(i, 0))
                            for c in range(N_FULL - 1):
                                pe.matmul(PS[:, 6 + a, c * P:(c + 1) * P], hb.kh_turned[:, c, :], hb.v[:, c, :],
                                          start=True, stop=True)
                            mm = pe.matmul(PS[:, 6 + a, 3 * P:4 * P], hb.kh_turned[0:N_META, 3, :],
                                    hb.v[0:N_META, 4, :],
                                           start=True, stop=True)
                            mm.then_inc(kv1_done[a].sem, 1)
                for a, hb in enumerate(head_sets):
                    pe.wait_ge(states_made[a].sem, states_made[a].at(i))
                    pe.wait_ge(qd1_made[a].sem, qd1_made[a].at(i))
                    pe.wait_ge(level_taken[a].sem, level_taken[a].at(i))
                    for c in range(N_FULL):
                        dst = PS[:, 4 + a, c * P:(c + 1) * P]
                        pe.matmul(dst, hb.v[:, c, :], hb.scores[:, c * P:(c + 1) * P], start=True, stop=False)
                        mm = pe.matmul(dst, hb.states[:, c, :], hb.e[:, chunk(c)], start=False, stop=True)
                    mm.then_inc(o1_done[a].sem, 1)
            head_norm_sums(6, range(4), nrm_c, ones_h, KEPT)
            pe.wait_ge(norm_logged.sem, norm_logged.at(9))
            project("out1", 2, 0, hg_lo_made, KEPT)
            layer_norm_sums(2, "mlp1", KEPT)
            mlp("mlp1", 1, 3, KEPT)
            layer_norm_sums(3, "end", KEPT)

        @block.scalar
        def _(act):
            def hold():
                act.sem_inc(act_waited.sem, 1)

            def from_tile(m, n, f, dst, func, tokens=ALL):
                act.wait_ge(tile_done[m].sem, (n if m else f) + 1)
                hold()
                act.activation(halves(dst[:, tokens]), pair(m, tokens), func).then_inc(evac[m].sem, 1)

            def evacuate(name, rounds, dst, func, tokens=ALL):
                n0, f0, _ = AT[name]
                with act.Fori(0, rounds) as i:
                    for u in range(2):
                        for m in range(2):
                            from_tile(m, i * 2 + (n0 + u), i * 2 + (f0 + u), dst[:, i * 4 + (2 * u + m), :], func,
                                      tokens)

            def evacuate_tokens(name, v_done, v_evac, rounds, dst):
                n0 = AT[name][0]
                with act.Fori(0, rounds) as i:
                    for u in range(2):
                        for j in range(5):
                            rows = min(P, T - j * P)
                            if j < 4:
                                act.wait_ge(v_done.sem, v_done.at(i * 2 + u, j))
                            else:
                                act.wait_ge(stage_done.sem, i * 2 + (n0 + u + 1))
                            hold()
                            act.activation(dst[0:rows, j, bass.ds(i * (2 * COLS) + u * COLS, COLS)],
                                           PS[0:rows, j, 0:COLS],
                                           ACT.Copy).then_inc(v_evac.sem, 1)

            def gate(g0, src, tiles, hi_made, tokens=ALL):
                for a in tiles:
                    act.wait_ge(norm_gated.sem, norm_gated.at(g0 + a // 2))
                    act.activation(x_hi[:, a, tokens], src[:, a, tokens], ACT.Copy).then_inc(hi_made.sem, 1)

            def head_norms(r, groups, src, buf, meanwhile=None, tokens=ALL,
                           squared=None):
                for g in range(groups + 1):
                    if g < groups:
                        if g > 1:
                            act.wait_ge(norm_applied.sem, norm_applied.at(r + g - 2))
                        act.activation(buf[:, g % 2, :, tokens], src[:, 2 * g:2 * g + 2, tokens],
                                       ACT.Square).then_inc(norm_squared.sem, 1)
                    if g == 1 and squared is not None:
                        squared()
                    if g:
                        b = (g - 1) % 2
                        act.wait_ge(norm_summed.sem, norm_summed.at(r + g - 1))
                        act.activation(buf[:, b, :, tokens].rearrange("p h (a t) -> p h a t", a=2),
                                       PS[:, norm_bank(r, g - 1):norm_bank(r, g - 1) + 4, 0:half(tokens)].rearrange(
                                           "p (h a) t -> p h a t", h=2), ACT.Ln, bias=eps_rms).then_inc(norm_logged.sem, 1)
                        act.wait_ge(norm_logged.sem, norm_logged.at(r + g - 1))
                        act.activation(buf[:, b, :, tokens], buf[:, b, :, tokens], ACT.Exp,
                                scale=-0.5).then_inc(norm_scaled.sem, 1)
                        if meanwhile is not None:
                            meanwhile(g - 1)

            def layer_norm(r, tokens=ALL):
                for k in range(KT):
                    act.wait_ge(ln_centered.sem, ln_centered.at(r, k))
                    if k > 3:
                        act.wait_ge(ln_square_used.sem, ln_square_used.at(r, (k - 4) // 2))
                    act.activation(lnsq[:, k % 4, tokens], h[:, k, tokens], ACT.Square).then_inc(ln_squared.sem, 1)
                act.wait_ge(ln_square_used.sem, ln_square_used.at(r))
                act.activation(halves(rstd[:, tokens]), PS[:, 6:8, 0:half(tokens)], ACT.Ln,
                        bias=eps_ln).then_inc(ln_logged.sem, 1)
                act.wait_ge(ln_logged.sem, ln_logged.at(r))
                act.activation(rstd[:, tokens], rstd[:, tokens], ACT.Exp, scale=-0.5).then_inc(ln_rstd_made.sem, 1)
                for k in range(KT):
                    act.wait_ge(ln_scaled.sem, ln_scaled.at(r, k))
                    col = P_LNB + r * KT + k
                    dst, done = (x_hi, x_hi_made) if r < 3 else (h, out_ready)
                    act.activation(dst[:, k, tokens], h[:, k, tokens], ACT.Identity,
                            bias=par[:, col:col + 1]).then_inc(done.sem, 1)

            def mlp(name, r, tokens=ALL):
                n0, f0, _ = AT[name]
                for hf in range(2):
                    with act.Fori(0, 4) as i:
                        for u in range(2):
                            for m in range(2):
                                t = i * 4 + (2 * u + m)
                                from_tile(m, i * 2 + (n0 + 16 * hf + u), i * 2 + (f0 + 16 * hf + u),
                                        relu[:, m, :], ACT.Relu,
                                          tokens)
                                act.wait_ge(hidden_squared.sem, hidden_squared.at(r * 2 + hf, t))
                                hold()
                                act.activation(hid_hi[:, t, tokens], sqr[:, m, tokens],
                                               ACT.Copy).then_inc(hidden_hi_made.sem, 1)

            for dst, src in ((par[:], params), (gp[:, 0:2], gate_params), (ident[:], consts[:, 0:P]),
                             (con[:], consts[:, P:P + C_SHARED])):
                act.dma_start(dst, src).then_inc(consts_loaded.sem, 16)
            act.wait_ge(wg_cleared.sem, wg_cleared.at(0))
            act.dma_start(wg[:, :, 0:GH], wgate[0]).then_inc(wgate_loaded.sem, 16)
            act.dma_start(wg[:, :, 32:32 + GH], wgate[1]).then_inc(wgate_loaded.sem, 16)
            act.dma_start(gdn_con[:], consts[:, P + C_SHARED:]).then_inc(gdn_consts_loaded.sem, 16)
            for k in range(KT):
                if k % (KT // 2) == 0:
                    half_loaded = h_loaded[2 * k // KT]
                    act.wait_ge(half_loaded.sem, half_loaded.at(0))
                act.activation(x_hi[:, k, :], h[:, k, :], ACT.Copy).then_inc(x_hi_made.sem, 1)

            act.wait_ge(consts_loaded.sem, consts_loaded.at(N_CONST_LOADS - 1))
            act.wait_ge(consts_made.sem, consts_made.at(0))
            n0, f0, _ = AT["qkv"]
            with act.Fori(0, 3) as i:
                for u in range(2):
                    for m in range(2):
                        from_tile(m, i * 2 + (n0 + u), i * 2 + (f0 + u), conv_in[:, m, 3:3 + T], ACT.Copy)
                        act.wait_ge(conv_tap_added.sem, conv_tap_added.at(i * 4 + (2 * u + m)))
                        hold()
                        act.activation(qkv[:, i * 4 + (2 * u + m), :], conv_acc[:, m, :],
                                ACT.Silu).then_inc(qkv_made.sem, 1)
            act.wait_ge(gates_done.sem, gates_done.at(0))
            act.activation(halves(beta[:, :]), PS[0:GH, 4:6, 0:HALF], ACT.Sigmoid).then_inc(beta_made.sem, 1)
            act.preload_act_table_set(EXP_LN)
            act.activation(gp[:, 2:3], gp[:, 0:1], ACT.Exp).then_inc(rate_made.sem, 1)
            act.activation(lbt[:, 6, :], lbt[:, 3, :], ACT.Exp)
            act.activation(lbt[:, 7, :], lbt[:, 4, :], ACT.Exp).then_inc(lb_exp.sem, 1)
            act.wait_ge(decay_logit_made.sem, decay_logit_made.at(0))
            act.activation(gtmp[:, 1, :], gtmp[:, 0, :], ACT.Abs).then_inc(gate_soft.sem, 1)
            act.wait_ge(gate_soft.sem, gate_soft.at(0, 0))
            act.activation(gtmp[:, 1, :], gtmp[:, 1, :], ACT.Exp, scale=-1.0).then_inc(gate_soft.sem, 1)
            act.wait_ge(gate_soft.sem, gate_soft.at(0, 1))
            act.activation(gtmp[:, 1, :], gtmp[:, 1, :], ACT.Ln, bias=small[0:GH, 2:3]).then_inc(gate_soft.sem, 1)
            n0, f0, _ = AT["z0"]
            for m in range(2):
                from_tile(m, n0, f0, z0[:, m, :], ACT.Copy)

            def z_tile(g):
                if g < 2:
                    from_tile(g, n0 + 1, f0 + 1, z0[:, 2 + g, :], ACT.Copy)

            act.wait_ge(columns_done.sem, columns_done.at(0))
            full = PS[:, 6, 0:8 * N_FULL].rearrange("p (c w h) -> p c w h", c=N_FULL, w=2)
            act.activation(colg[:, 0:N_FULL, :, :], full, ACT.Copy)
            act.activation(colg[0:TAIL, N_FULL, :, :],
                    PS[0:TAIL, 6, 8 * N_FULL:8 * N_FULL + 8].rearrange("p (w h) -> p w h", w=2),
                           ACT.Copy).then_inc(columns_made.sem, 1)
            act.wait_ge(qkv_made.sem, qkv_made.at(11))
            head_norms(0, 4, qkv[:, 0:2 * GH, :], nrm_a, z_tile)
            act.wait_ge(norm_applied.sem, norm_applied.at(3))

            def gdn_chunk(i, n, last, filled):
                n0, f0, _ = AT["qk"]

                def take_tile(half):
                    if filled == "qk":
                        u, m = half // 2, half % 2
                        from_tile(m, i * 2 + (n0 + u), i * 2 + (f0 + u), qk[:, i * 4 + half, :], ACT.Copy)

                def take_values(j):
                    if filled == "v":
                        u, rows = i - FILLED, min(P, T - j * P)
                        if j < 4:
                            act.wait_ge(v_tile_done0.sem, v_tile_done0.at(u, j))
                        else:
                            act.wait_ge(stage_done.sem, AT["v0"][0] + u + 1)
                        act.activation(vt[0:rows, j, u * COLS:(u + 1) * COLS], PS[0:rows, (5 * u + j) % 4, 0:COLS],
                                       ACT.Copy).then_inc(v_evacuated0.sem, 1)

                cols = bass.ds(i * P, n)
                act.activation(gsel[:, 0, 0:n], gcum[:, cols], ACT.Copy)
                act.activation(gsel[:, 1, 0:n], beta[:, cols], ACT.Copy).then_inc(gate_rows_staged.sem, 1)
                for g, dst in ((1, kS), (0, qS), (2, vS)):
                    ins = act.activation(dst[:, :, 0:n], qkv[:, g * GH:(g + 1) * GH, cols], ACT.Copy)
                ins.then_inc(heads_staged.sem, 1)
                act.wait_ge(decay_rows_done.sem, decay_rows_done.at(i))
                rows = PS[:, 4, :].rearrange("p (h t) -> p h t", h=GH)[:, :, 0:n]
                act.activation(GB[:, :, 0:n], rows, ACT.Copy).then_inc(gb_made.sem, 1)
                act.wait_ge(state_ready.sem, state_ready.at(i))
                act.activation(EG[:, :, 0:n], rows, ACT.Exp).then_inc(eg_made.sem, 1)
                act.wait_ge(beta_rows_done.sem, beta_rows_done.at(i))
                rows = PS[:, 5, :].rearrange("p (h t) -> p h t", h=GH)[:, :, 0:n]
                act.activation(BB[:, :, 0:n], rows, ACT.Copy).then_inc(bb_made.sem, 1)
                act.wait_ge(gdiff_made.sem, gdiff_made.at(i))
                act.activation(kd4[0:n], gdiff[0:n], ACT.Exp, scale=-1.0)
                act.activation(eg4[0:n], gcol[0:n], ACT.Exp).then_inc(col_decay_made.sem, 1)
                act.wait_ge(dm_exponent.sem, dm_exponent.at(i))
                act.activation(DM[0:n, :, 0:n], DM[0:n, :, 0:n], ACT.Exp).then_inc(dm_exp.sem, 1)
                act.wait_ge(t_turned.sem, t_turned.at(i))
                bank = [PS[0:n, b, :].rearrange("p (h t) -> p h t", h=GH) for b in range(8)]
                act.activation(TM[0:n, :, 0:n], bank[6][:, :, 0:n], ACT.Copy).then_inc(t_first.sem, 1)
                for l, _ in levels(n):
                    act.wait_ge(x_done.sem, x_done.at(i, l))
                    act.activation(XS[0:n, :, 0:n], bank[7][:, :, 0:n], ACT.Copy).then_inc(x_copied.sem, 1)
                    if l % 2:
                        take_tile(l // 2)
                    if l in (1, 3, 4):
                        take_values((1, 3, 4).index(l))
                act.wait_ge(vnew_done.sem, vnew_done.at(i))
                act.activation(VN[0:n, :, :], bank[7], ACT.Copy).then_inc(vnew_copied.sem, 1)
                take_values(3)
                act.wait_ge(o_done.sem, o_done.at(i))
                o = PS[:, 4, :].rearrange("p (h t) -> p h t", h=GH)[:, :, 0:n]
                hold()
                act.activation(qkv[:, 0:GH, cols], o, ACT.Copy).then_inc(o_copied.sem, 1)
                take_tile(3)
                take_values(4)

            with act.Fori(0, FILLED) as i:
                gdn_chunk(i, P, False, "qk")
            for i in range(FILLED, N_FULL):
                gdn_chunk(i, P, False, "v")
            gdn_chunk(N_FULL, TAIL, True, None)

            def stage_pair(i):
                act.activation(sq_k[:, 0:T], qk[:, i + GH, :], ACT.Copy)
                act.activation(sq_q[:, 0:T], qk[:, i, :], ACT.Copy).then_inc(pair_staged.sem, 1)

            def stage_values(i):
                act.activation(sq_v[:, :, :], vt[:, :, bass.ds(i * P, P)], ACT.Copy).then_inc(values_staged.sem, 1)

            act.wait_ge(o_copied.sem, o_copied.at(N_FULL))
            head_norms(4, 2, qkv[:, 0:GH, :], nrm_b, squared=lambda: (stage_pair(0), stage_values(0)))
            def softplus(i, a):
                act.wait_ge(z_copied.sem, z_copied.at(i, a))
                act.activation(sp[:, a, :], zs[:, a, :], ACT.Abs).then_inc(z_abs.sem, 1)
                act.wait_ge(z_abs.sem, z_abs.at(i, a))
                act.activation(sp[:, a, :], sp[:, a, :], ACT.Exp, scale=-1.0).then_inc(z_exp.sem, 1)
                act.wait_ge(z_exp.sem, z_exp.at(i, a))
                act.activation(sp[:, a, :], sp[:, a, :], ACT.Ln, bias=small[:, 2:3]).then_inc(z_log.sem, 1)

            def weights(i, a):
                act.wait_ge(logits_made.sem, logits_made.at(i, a))
                act.activation(wt[:, a, :], zs[:, a, :], ACT.Exp).then_inc(weights_made.sem, 1)

            def pair_out(i):
                act.wait_ge(values_done.sem, values_done.at(i))
                hold()
                act.activation(x_hi[:, i + GH, 0:512], PS[:, 6, :], ACT.Copy)
                act.activation(x_hi[:, i + GH, 512:T], PS[:, 7, 0:TAIL], ACT.Copy).then_inc(pair_hi_made.sem, 1)

            softplus(0, 0)
            softplus(0, 1)
            act.activation(z0, z0, ACT.Silu).then_inc(z0_gated.sem, 1)
            act.preload_act_table_set(EXP_LN)
            gate(0, qkv, range(GH), gdn_hi_made)
            with act.Fori(0, SH // 2 - 1) as i:
                stage_pair(i + 1)
                weights(i, 0)
                weights(i, 1)
                softplus(i + 1, 0)
                softplus(i + 1, 1)
                pair_out(i)
                stage_values(i + 1)
            weights(SH // 2 - 1, 0)
            weights(SH // 2 - 1, 1)
            pair_out(SH // 2 - 1)


            act.wait_ge(o_copied.sem, o_copied.at(N_FULL))
            act.wait_ge(gdn_lo_made.sem, gdn_lo_made.at(0))
            layer_norm(0)
            mlp("mlp0", 0)
            act.preload_act_table_set(EXP_LN)
            layer_norm(1)

            act.dma_start(mask_in[:], hmasks).then_inc(masks_loaded.sem, 16)
            evacuate("f", 2, fg, ACT.Sigmoid)
            evacuate_tokens("v1", v_tile_done1, v_evacuated1, 2, v1)
            evacuate("q1", 2, q1, ACT.Silu, KEPT)
            evacuate("z1", 1, z1, ACT.Silu, KEPT)
            n0, f0, _ = AT["z1"]
            for m in range(2):
                from_tile(m, n0 + 2, f0 + 2, z1[:, 4 + m, :], ACT.Silu, KEPT)
            act.preload_act_table_set(EXP_LN)
            act.wait_ge(f_made.sem, f_made.at(HH - 1))
            def log_f(i, a, hb):
                act.activation(hb.kh, fg[:, i * 2 + a, :], ACT.Ln).then_inc(logf_made[a].sem, 1)

            def level_exp_of(i, l, a, hb):
                act.wait_ge(level_exponent[a].sem, level_exponent[a].at(i, l))
                act.activation(hb.ee[:, l % 2, :], hb.ee[:, l % 2, :], ACT.Exp).then_inc(level_exp[a].sem, 1)

            def kh_exp_of(i, a, hb):
                act.wait_ge(kh_exponent[a].sem, kh_exponent[a].at(i))
                act.activation(hb.kh[:, 0:KH], hb.kh[:, 0:KH], ACT.Exp, scale=-1.0).then_inc(kh_exp[a].sem, 1)

            def head_pair(i, last):
                for a, hb in enumerate(head_sets):
                    level_exp_of(i, 1, a, hb)
                for a, hb in enumerate(head_sets):
                    act.wait_ge(b_made[a].sem, b_made[a].at(i))
                    act.activation(hb.e, hb.b, ACT.Exp).then_inc(eb_made[a].sem, 1)
                for a, hb in enumerate(head_sets):
                    cols = bass.ds(i * (2 * P) + a * P, P)
                    act.activation(hb.v[:, 0:N_FULL, :], v1[:, 0:N_FULL, cols], ACT.Copy)
                    act.activation(hb.v[0:N_META, N_FULL, :], v1[0:N_META, N_FULL, cols], ACT.Copy)
                for l in range(1, len(LEVELS)):
                    for a, hb in enumerate(head_sets):
                        if l > 1:
                            level_exp_of(i, l, a, hb)
                    if l == 1:
                        for a, hb in enumerate(head_sets):
                            act.wait_ge(kh_turned[a].sem, kh_turned[a].at(i))
                            turned = PS[:, 4 + a, :].rearrange("p (c t) -> p c t", c=4)
                            act.activation(hb.kh_turned[:, 0:3, :], turned[:, 0:3, :], ACT.Copy)
                            act.activation(hb.kh_turned[0:N_META, 3, :], turned[0:N_META, 3, :],
                                           ACT.Copy).then_inc(kh_copied[a].sem, 1)
                    if l == 4 and not last:
                        for a, hb in enumerate(head_sets):
                            log_f(i + 1, a, hb)
                if not last:
                    for a, hb in enumerate(head_sets):
                        level_exp_of(i + 1, 0, a, hb)
                    for a, hb in enumerate(head_sets):
                        kh_exp_of(i + 1, a, hb)
                for a, hb in enumerate(head_sets):
                    act.wait_ge(o1_done[a].sem, o1_done[a].at(i))
                    hold()
                    act.activation(fg[:, i * 2 + a, N_META:T], PS[:, 4 + a, :],
                            ACT.Copy).then_inc(o_bank_free[a].sem, 1)

            for a in range(2):
                act.sem_inc(o_bank_free[a].sem, 1)
            log_f(0, 0, head_sets[0])
            level_exp_of(0, 0, 0, head_sets[0])
            for m in range(2):
                from_tile(m, n0 + 3, f0 + 3, z1[:, 6 + m, :], ACT.Silu, KEPT)
            act.preload_act_table_set(EXP_LN)
            log_f(0, 1, head_sets[1])
            level_exp_of(0, 0, 1, head_sets[1])
            for a, hb in enumerate(head_sets):
                kh_exp_of(0, a, hb)
            with act.Fori(0, HH // 2 - 1) as i:
                head_pair(i, False)
            head_pair(HH // 2 - 1, True)
            for a in range(2):
                act.wait_ge(o_bank_free[a].sem, o_bank_free[a].at(HH // 2))
            head_norms(6, 4, fg, nrm_c,
                    lambda g: gate(2, fg, range(2 * g - 2, 2 * g), hg_hi_made, KEPT) if g else None,
                       KEPT)
            gate(2, fg, range(HH - 2, HH), hg_hi_made, KEPT)
            layer_norm(2, KEPT)
            mlp("mlp1", 1, KEPT)
            act.preload_act_table_set(EXP_LN)
            layer_norm(3, KEPT)

        @block.vector
        def _(dve):
            def hold():
                dve.sem_inc(dve_waited.sem, 1)

            def head_norms(r, groups, src, buf, scale):
                for g in range(groups):
                    x = src[:, 2 * g:2 * g + 2, :]
                    dve.wait_ge(norm_scaled.sem, norm_scaled.at(r + g))
                    dve.scalar_tensor_tensor(x, x, scale(g), buf[:, g % 2, :, :], ALU.mult,
                                             ALU.mult).then_inc(norm_applied.sem, 1)

            def apply_norm(r, groups, src, buf, gain, tokens=ALL):
                for g in groups:
                    x = src[:, 2 * g:2 * g + 2, tokens]
                    dve.wait_ge(norm_scaled.sem, norm_scaled.at(r + g))
                    dve.scalar_tensor_tensor(x, x, gain, buf[:, g % 2, :, tokens], ALU.mult,
                                             ALU.mult).then_inc(norm_applied.sem, 1)

            def gate(r, groups, src, z, tokens=ALL):
                for g in groups:
                    x = src[:, 2 * g:2 * g + 2, tokens]
                    dve.wait_ge(norm_applied.sem, norm_applied.at(r + g))
                    if r == 4:
                        dve.wait_ge(z0_gated.sem, z0_gated.at(0))
                    dve.tensor_tensor(x, x, z[:, 2 * g:2 * g + 2, tokens], ALU.mult).then_inc(norm_gated.sem, 1)

            def gate_low(g0, tiles, src, hi_made, lo_made, tokens=ALL):
                for a in tiles:
                    dve.wait_ge(norm_gated.sem, norm_gated.at(g0 + a // 2))
                    dve.wait_ge(hi_made.sem, hi_made.at(0, a))
                    dve.tensor_tensor(x_lo[:, a, tokens], src[:, a, tokens], x_hi[:, a, tokens].bitcast(F32),
                                      ALU.subtract).then_inc(lo_made.sem, 1)

            def add_residual(m, n, f, tile, scale, tokens):
                dve.wait_ge(tile_done[m].sem, (n if m else f) + 1)
                hold()
                dve.scalar_tensor_tensor(halves(h[:, tile, tokens]), halves(h[:, tile, tokens]), scale,
                        pair(m, tokens),
                                         ALU.mult, ALU.add).then_inc(evac[m].sem, 1)

            def clear_sum():
                dve.memset(ln_sum[:, :], 0.0).then_inc(ln_partial.sem, 1)

            def add_to_sum(r, m, evacuated, tile, tokens):
                dve.wait_ge(evac[m].sem, evacuated)
                dve.wait_ge(ln_partial.sem, ln_partial.at(r, tile))
                hold()
                dve.tensor_tensor(ln_sum[:, tokens], ln_sum[:, tokens], h[:, tile, tokens],
                        ALU.add).then_inc(ln_partial.sem, 1)

            def out_projection(name, r, tokens=ALL):
                n0, f0, e0 = AT[name]
                clear_sum()
                with dve.Fori(0, 2) as i:
                    for u in range(2):
                        for m in range(2):
                            add_residual(m, i * 2 + (n0 + u), i * 2 + (f0 + u), i * 4 + (2 * u + m), ALPHA,
                                         tokens)
                            add_to_sum(r, m, i * 2 + (e0 + u + 1), i * 4 + (2 * u + m), tokens)

            def add_squares(r, pair_, tokens):
                dve.wait_ge(ln_squared.sem, ln_squared.at(r, 2 * pair_ + 1))
                first, second = lnsq[:, 2 * pair_ % 4, tokens], lnsq[:, 2 * pair_ % 4 + 1, tokens]
                dve.tensor_tensor(first, first, second, ALU.add).then_inc(ln_paired.sem, 1)

            def layer_norm(r, after, tokens=ALL):
                for m in range(2):
                    dve.wait_ge(evac[m].sem, AT[after][2])
                dve.wait_ge(ln_mean_ready.sem, ln_mean_ready.at(r))
                for k in range(KT):
                    dve.tensor_tensor(halves(h[:, k, tokens]), halves(h[:, k, tokens]), PS[:, 4:6, 0:half(tokens)],
                                      ALU.subtract).then_inc(ln_centered.sem, 1)
                    if k in (2, 4, 6):
                        add_squares(r, k // 2 - 1, tokens)
                add_squares(r, KT // 2 - 1, tokens)
                dve.wait_ge(ln_rstd_made.sem, ln_rstd_made.at(r))
                dve.wait_ge(ln_centered.sem, ln_centered.at(r))
                for k in range(KT + 1):
                    if k < KT:
                        gain = par[:, P_LNG + r * KT + k:P_LNG + r * KT + k + 1]
                        dve.scalar_tensor_tensor(h[:, k, tokens], h[:, k, tokens], gain, rstd[:, tokens],
                                                 ALU.mult, ALU.mult).then_inc(ln_scaled.sem, 1)
                    if k and r < 3:
                        shift = par[:, P_LNB + r * KT + k - 1:P_LNB + r * KT + k]
                        dve.wait_ge(ln_scaled.sem, ln_scaled.at(r, k - 1))
                        dve.wait_ge(x_hi_made.sem, x_hi_made.at(r + 1, k - 1))
                        dve.scalar_tensor_tensor(x_lo[:, k - 1, tokens], h[:, k - 1, tokens], shift,
                                                 x_hi[:, k - 1, tokens].bitcast(F32),
                                                 ALU.add, ALU.subtract).then_inc(x_lo_made.sem, 1)
                if r < 3:
                    for k in range(KT):
                        shift = par[:, P_LNB + r * KT + k:P_LNB + r * KT + k + 1]
                        dve.tensor_scalar(h[:, k, tokens], h[:, k, tokens], shift, None,
                                ALU.add).then_inc(ln_shifted.sem, 1)
                    dve.wait_ge(ln_shifted.sem, ln_shifted.at(r))

            def mlp(name, r, tokens=ALL):
                n0, f0, e0 = AT[name]
                for hf in range(2):
                    n1, f1, e1, rr = n0 + 16 * hf, f0 + 16 * hf, e0 + 12 * hf, r * 2 + hf
                    with dve.Fori(0, 4) as i:
                        for u in range(2):
                            for m in range(2):
                                t = i * 4 + (2 * u + m)
                                dve.wait_ge(evac[m].sem, i * 2 + (e1 + u + 1))
                                dve.tensor_tensor(sqr[:, m, tokens], relu[:, m, tokens], relu[:, m, tokens],
                                                  ALU.mult).then_inc(hidden_squared.sem, 1)
                                dve.wait_ge(hidden_hi_made.sem, hidden_hi_made.at(rr, t))
                                dve.wait_ge(hidden_squared.sem, hidden_squared.at(rr, t))
                                dve.tensor_tensor(hid_lo[:, t, tokens], sqr[:, m, tokens],
                                        hid_hi[:, t, tokens].bitcast(F32),
                                                  ALU.subtract).then_inc(hidden_lo_made.sem, 1)
                    if hf == 1:
                        clear_sum()
                    with dve.Fori(0, 4) as i:
                        for m in range(2):
                            add_residual(m, i * 2 + (n1 + 9), i * 2 + (f1 + 9), i * 2 + m, ALPHA if hf == 0 else 1.0,
                                         tokens)
                            if hf == 1:
                                add_to_sum(2 * r + 1, m, i + (e1 + 9), i * 2 + m, tokens)
                    if hf == 0:
                        for m in range(2):
                            dve.wait_ge(evac[m].sem, AT[name][2] + 12)

            dve.memset(wg[:, :, :], 0.0).then_inc(wg_cleared.sem, 1)
            dve.memset(ones[:, :], 1.0)
            dve.memset(ones_d[:, :], 1.0 / D)
            dve.memset(ones_h[:, :], 1.0 / P)
            dve.memset(small[:, 0:1], LN_EPS)
            dve.memset(small[:, 1:2], RMS_EPS)
            dve.memset(small[:, 2:3], 1.0)
            dve.memset(conv_in[:, :, 0:3], 0.0)
            for m in range(2):
                dve.sem_inc(evac[m].sem, 1)
            for k in range(KT):
                dve.wait_ge(x_hi_made.sem, x_hi_made.at(0, k))
                dve.tensor_tensor(x_lo[:, k, :], h[:, k, :], x_hi[:, k, :].bitcast(F32),
                                  ALU.subtract).then_inc(x_lo_made.sem, 1)

            dve.wait_ge(consts_loaded.sem, consts_loaded.at(N_CONST_LOADS - 1))
            dve.tensor_copy(ident_b[:, :], ident[:, :])
            dve.tensor_copy(neg_b[:, :], con[:, C_NEG:C_NEG + P])
            raw0, raw1 = par[:, P_LB:P_LB + HH], par[:, P_LB + HH:P_LB + 2 * HH]
            L = [lbt[:, x, :] for x in range(8)]
            lbs = lb_step
            dve.tensor_tensor(L[2], raw0, raw1, ALU.max).then_inc(lbs.sem, 1)
            dve.wait_ge(lbs.sem, lbs.at(0, 0))
            dve.tensor_tensor(L[3], raw0, L[2], ALU.subtract)
            dve.tensor_tensor(L[4], raw1, L[2], ALU.subtract).then_inc(consts_made.sem, 1)
            e0 = AT["qkv"][2]
            with dve.Fori(0, 3) as i:
                for u in range(2):
                    for m in range(2):
                        q = i * 4 + (2 * u + m)
                        dve.wait_ge(evac[m].sem, i * 2 + (e0 + u + 1))
                        hold()
                        for tap in range(4):
                            weight = par[:, bass.ds(q * 4 + (P_CONV + tap), 1)]
                            x = conv_in[:, m, tap:tap + T]
                            if tap == 0:
                                ins = dve.tensor_scalar(conv_acc[:, m, :], x, weight, None, ALU.mult)
                            else:
                                dve.wait_ge(conv_tap_added.sem, conv_tap_added.at(q, tap - 1))
                                ins = dve.scalar_tensor_tensor(conv_acc[:, m, :], x, weight, conv_acc[:, m, :],
                                                               ALU.mult, ALU.add)
                            ins.then_inc(conv_tap_added.sem, 1)

            dve.wait_ge(gates_done.sem, gates_done.at(0))
            dve.wait_ge(gdn_consts_loaded.sem, gdn_consts_loaded.at(0))
            dve.tensor_scalar(halves(gtmp[:, 0, :]), PS[32:32 + GH, 4:6, 0:HALF], gp[:, 1:2], None,
                              ALU.add).then_inc(decay_logit_made.sem, 1)
            dve.wait_ge(gate_soft.sem, gate_soft.at(0))
            dve.wait_ge(decay_logit_made.sem, decay_logit_made.at(0))
            dve.scalar_tensor_tensor(gtmp[:, 2, :], gtmp[:, 0, :], 0.0, gtmp[:, 1, :], ALU.max,
                    ALU.add).then_inc(softplus0.sem, 1)
            dve.wait_ge(softplus0.sem, softplus0.at(0))
            dve.wait_ge(rate_made.sem, rate_made.at(0))
            dve.tensor_scalar(gtmp[:, 0, :], gtmp[:, 2, :], gp[:, 2:3], -1.0, ALU.mult,
                    ALU.mult).then_inc(g_made.sem, 1)
            dve.wait_ge(g_made.sem, g_made.at(0))
            for c in range(N_FULL + 1):
                n = min(P, T - c * P)
                dve.tensor_tensor_scan(gcum[:, c * P:c * P + n], ones[0:GH, 0:n], gtmp[:, 0, c * P:c * P + n], 0.0,
                                       ALU.mult, ALU.add).then_inc(gcum_made.sem, 1)
            head_norms(0, 4, qkv, nrm_a, lambda g: P ** -0.5 if g < 2 else 1.0)
            dve.wait_ge(norm_applied.sem, norm_applied.at(3))
            dve.memset(vt[:, 4, :], 0.0)
            dve.memset(SS[:, :, :], 0.0).then_inc(state_ready.sem, 1)

            def gdn_chunk(i, n, last, filled):
                bank = [PS[0:n, b, :].rearrange("p (h t) -> p h t", h=GH) for b in range(8)]
                dve.tensor_copy(gcol[0:n], colg[0:n, i, 1, :])
                dve.tensor_copy(bcol[0:n], colg[0:n, i, 0, :]).then_inc(gcol_staged.sem, 1)
                dve.wait_ge(gb_made.sem, gb_made.at(i))
                dve.wait_ge(gcol_staged.sem, gcol_staged.at(i))
                dve.tensor_tensor(gdiff[0:n], gcol[0:n], GB[0:n, :, n - 1], ALU.subtract).then_inc(gdiff_made.sem, 1)
                for a in range(GH):
                    ins = dve.tensor_scalar(DM[0:n, a, 0:n], GB[0:n, a, 0:n], gcol[0:n, a:a + 1], 0.0,
                            ALU.subtract, ALU.min)
                ins.then_inc(dm_exponent.sem, 1)
                dve.wait_ge(dm_exp.sem, dm_exp.at(i))
                dve.tensor_tensor(DM[0:n, :, 0:n], DM[0:n, :, 0:n], heads(ge_mask[0:n, 0:n], n),
                        ALU.mult).then_inc(dm_made.sem, 1)
                dve.wait_ge(kk_done.sem, kk_done.at(i))
                dve.wait_ge(dm_made.sem, dm_made.at(i))
                dve.tensor_tensor(MT[0:n, :, 0:n], bank[6][:, :, 0:n], DM[0:n, :, 0:n],
                        ALU.mult).then_inc(m_made.sem, 1)
                dve.wait_ge(m_made.sem, m_made.at(i, 0))
                dve.wait_ge(bb_made.sem, bb_made.at(i))
                dve.tensor_tensor(MT[0:n, :, 0:n], MT[0:n, :, 0:n], BB[0:n, :, 0:n], ALU.mult).then_inc(m_made.sem, 1)
                dve.wait_ge(m_made.sem, m_made.at(i, 1))
                dve.tensor_tensor(XS[0:n, :, 0:n], MT[0:n, :, 0:n], heads(level_mask(n, 0), n),
                        ALU.mult).then_inc(m_first.sem, 1)
                dve.wait_ge(m_first.sem, m_first.at(i))
                dve.tensor_tensor(TT[0:n, :, 0:n], heads(ident[0:n, 0:n], n), XS[0:n, :, 0:n],
                        ALU.subtract).then_inc(tt_first.sem, 1)
                dve.wait_ge(qk_done.sem, qk_done.at(i))
                dve.tensor_tensor(AT0[0:n, :, 0:n], bank[7][:, :, 0:n], DM[0:n, :, 0:n],
                        ALU.mult).then_inc(a_made.sem, 1)
                dve.wait_ge(col_decay_made.sem, col_decay_made.at(i))
                dve.wait_ge(k_turned.sem, k_turned.at(i))
                dve.wait_ge(a_made.sem, a_made.at(i))
                for a in range(GH):
                    ins = dve.tensor_scalar(KD[0:n, a, :], bank[4][:, a, :], kd4[0:n, a:a + 1], None, ALU.mult)
                ins.then_inc(kd_made.sem, 1)
                dve.wait_ge(v_turned.sem, v_turned.at(i))
                for a in range(GH):
                    dve.tensor_scalar(VB[0:n, a, :], bank[5][:, a, :], bcol[0:n, a:a + 1], None, ALU.mult)
                dve.scalar_tensor_tensor(nb4[0:n], eg4[0:n], -1.0, bcol[0:n], ALU.mult,
                        ALU.mult).then_inc(vb_made.sem, 1)
                dve.wait_ge(eg_made.sem, eg_made.at(i))
                dve.tensor_tensor(qS[:, :, 0:n], qS[:, :, 0:n], EG[:, :, 0:n], ALU.mult).then_inc(qd_made.sem, 1)
                lv = levels(n)
                for l, _ in lv:
                    if l < len(lv) - 1:
                        dve.wait_ge(p1_done.sem, p1_done.at(i, l))
                        if l == 0:
                            dve.wait_ge(t_first.sem, t_first.at(i))
                        else:
                            dve.wait_ge(t_updated.sem, t_updated.at(i, l - 1))
                        dve.tensor_tensor(TM[0:n, :, 0:n], TM[0:n, :, 0:n], bank[4][:, :, 0:n],
                                ALU.subtract).then_inc(t_updated.sem, 1)
                    dve.wait_ge(p2_done.sem, p2_done.at(i, l))
                    if l == 0:
                        dve.wait_ge(tt_first.sem, tt_first.at(i))
                    else:
                        dve.wait_ge(tt_updated.sem, tt_updated.at(i, l - 1))
                    dve.tensor_tensor(TT[0:n, :, 0:n], TT[0:n, :, 0:n], bank[5][:, :, 0:n],
                            ALU.subtract).then_inc(tt_updated.sem, 1)
                dve.wait_ge(ks_done.sem, ks_done.at(i))
                dve.wait_ge(vb_made.sem, vb_made.at(i))
                for a in range(GH):
                    ins = dve.scalar_tensor_tensor(RR[0:n, a, :], bank[6][:, a, :], nb4[0:n, a:a + 1],
                            VB[0:n, a, :], ALU.mult, ALU.add)
                ins.then_inc(r_made.sem, 1)
                if not last:
                    dve.wait_ge(kv_done.sem, kv_done.at(i))
                    dve.wait_ge(state_ready.sem, state_ready.at(i))
                    for a in range(GH):
                        ins = dve.scalar_tensor_tensor(SS[:, a, :], SS[:, a, :], EG[:, a, n - 1:n],
                                PS[:, 5, a * P:(a + 1) * P],
                                                       ALU.mult, ALU.add)
                    ins.then_inc(state_ready.sem, 1)

            with dve.Fori(0, FILLED) as i:
                gdn_chunk(i, P, False, "qk")
            for i in range(FILLED, N_FULL):
                gdn_chunk(i, P, False, "v")
            gdn_chunk(N_FULL, TAIL, True, None)

            dve.wait_ge(o_copied.sem, o_copied.at(N_FULL))
            dve.memset(sq_k[:, T:640], 0.0)
            dve.memset(sq_q[:, T:QPAD], 0.0).then_inc(pads_cleared.sem, 1)
            apply_norm(4, range(2), qkv, nrm_b, par[:, P_GN:P_GN + 1])
            dve.sem_inc(pair_free.sem, 1)
            tail = [r.rearrange("p (b t) -> p b t", b=2) for r in (zs[:, 0, 512:ZW], zs[:, 1, 512:ZW])]

            def copy_scores(i, a, first=False):
                dve.wait_ge(z_done.sem, z_done.at(i, a))
                if not first:
                    dve.wait_ge(weights_made.sem, weights_made.at(i - 1, a))
                dve.tensor_scalar(zs[:, a, 0:512], PS[:, 3 * a, :], SD ** -0.5, None, ALU.mult)
                dve.tensor_scalar(tail[a], PS[:, 3 * a + 1:3 * a + 3, 0:432], SD ** -0.5, None,
                                  ALU.mult).then_inc(z_copied.sem, 1)

            def softplus(i, a):
                dve.wait_ge(z_log.sem, z_log.at(i, a))
                dve.wait_ge(z_copied.sem, z_copied.at(i, a))
                dve.scalar_tensor_tensor(sp[:, a, :], zs[:, a, :], 0.0, sp[:, a, :], ALU.max,
                                         ALU.add).then_inc(softplus_made.sem, 1)

            def sum_later(i, a, first=False):
                dve.wait_ge(softplus_made.sem, softplus_made.at(i, a))
                if not first:
                    dve.wait_ge(values_done.sem, values_done.at(i - 1, a))
                own = {j: col for j, q0, _, col in Z_PARTS if q0 == j * P}
                for j in (3, 2, 1):
                    col, at, n = own[j], LATER[j][1], T - (j + 1) * P
                    if j == 3:
                        src = sp[:, a, Z_LAST:Z_LAST + n]
                    else:
                        src = wt[:, a, LATER[j + 1][1]:LATER[j + 1][1] + n]
                        dve.wait_ge(later_summed.sem, later_summed.at(i, 3 * a + 2 - j))
                    dve.tensor_copy(wt[:, a, at:at + P], sp[:, a, col:col + P])
                    dve.tensor_tensor(wt[:, a, at + P:at + P + n], sp[:, a, col + P:col + P + n], src,
                                      ALU.add).then_inc(later_summed.sem, 1)

            def logits(i, a):
                dve.wait_ge(suffix_done.sem, suffix_done.at(i, a))
                dve.tensor_tensor(zs[:, a, 0:512], zs[:, a, 0:512], PS[:, 3 * a, :], ALU.subtract)
                dve.tensor_tensor(tail[a], tail[a], PS[:, 3 * a + 1:3 * a + 3, 0:432],
                                  ALU.subtract).then_inc(logits_made.sem, 1)

            def pair_out(i):
                dve.wait_ge(pair_hi_made.sem, pair_hi_made.at(i))
                hold()
                dve.tensor_tensor(x_lo[:, i + GH, 0:512], PS[:, 6, :], x_hi[:, i + GH, 0:512].bitcast(F32),
                        ALU.subtract)
                dve.tensor_tensor(x_lo[:, i + GH, 512:T], PS[:, 7, 0:TAIL], x_hi[:, i + GH, 512:T].bitcast(F32),
                                  ALU.subtract).then_inc(pair_free.sem, 1)

            for a in range(2):
                copy_scores(0, a, True)
            for a in range(2):
                softplus(0, a)
                sum_later(0, a, True)
            gate(4, range(2), qkv, z0)
            gate_low(0, range(GH), qkv, gdn_hi_made, gdn_lo_made)
            with dve.Fori(0, SH // 2 - 1) as i:
                logits(i, 0)
                logits(i, 1)
                copy_scores(i + 1, 0)
                copy_scores(i + 1, 1)
                softplus(i + 1, 0)
                sum_later(i + 1, 0)
                softplus(i + 1, 1)
                sum_later(i + 1, 1)
                pair_out(i)
            logits(SH // 2 - 1, 0)
            logits(SH // 2 - 1, 1)
            pair_out(SH // 2 - 1)

            out_projection("out0", 0)
            layer_norm(0, "mlp0")
            mlp("mlp0", 0)
            layer_norm(1, "f")

            L = [lbt[:, x, :] for x in range(8)]
            dve.wait_ge(lb_exp.sem, lb_exp.at(0))
            steps = [(L[5], L[6], L[7], ALU.add), None, (L[6], L[6], L[5], ALU.mult), (L[7], L[7], L[5], ALU.mult),
                     (L[7], L[6], L[7], ALU.add), (L[0], L[7], L[6], ALU.subtract), None]
            for x, step in enumerate(steps):
                if x == 1:
                    ins = dve.reciprocal(L[5], L[5])
                elif x == 6:
                    ins = dve.tensor_scalar(L[1], L[0], -1.0, 1.0, ALU.mult, ALU.add)
                else:
                    ins = dve.tensor_tensor(*step)
                ins.then_inc(lbs.sem, 1)
                dve.wait_ge(lbs.sem, lbs.at(0, x + 1))
            _, _, e0 = AT["f"]
            with dve.Fori(0, 2) as i:
                for u in range(2):
                    for m in range(2):
                        t = i * 4 + (2 * u + m)
                        dve.wait_ge(evac[m].sem, i * 2 + (e0 + u + 1))
                        hold()
                        dve.tensor_scalar(fg[:, t, :], fg[:, t, :], lbt[:, 1, bass.ds(t, 1)],
                                lbt[:, 0, bass.ds(t, 1)],
                                          ALU.mult, ALU.add).then_inc(f_made.sem, 1)
            dve.wait_ge(f_made.sem, f_made.at(HH - 1))
            for m in range(2):
                dve.wait_ge(evac[m].sem, AT["z1"][2])

            dve.wait_ge(masks_loaded.sem, masks_loaded.at(0))
            dve.tensor_copy(hmask[:, :, :], mask_in[:, :, :]).then_inc(masks_made.sem, 1)
            dve.wait_ge(masks_made.sem, masks_made.at(0))

            def clear(hb):
                dve.memset(hb.scores, 0.0)
                dve.memset(hb.kt, 0.0).then_inc(hg_cleared.sem, 1)

            def take(i, a, hb, l):
                m = LEVELS[l]

                def blocks(ap):
                    return ap.rearrange("p (b r) -> p b r", r=m)
                dve.wait_ge(level_product[a].sem, level_product[a].at(i, l))
                dve.wait_ge(level_taken[a].sem, level_taken[a].at(i, l))
                hold()
                dve.copy_predicated(part(hb.scores, m, 1), blocks(hmask[:, l, 0:SEQ // 2]),
                                    blocks(PS[:, 2 * a + l % 2, 0:SEQ // 2])).then_inc(level_taken[a].sem, 1)

            def sum_decays(i, a, hb):
                dve.wait_ge(logf_made[a].sem, logf_made[a].at(i))
                for c in range(N_FULL + 1):
                    t0, t1 = (N_META + (c - 1) * P, N_META + c * P) if c else (0, N_META)
                    dve.tensor_tensor_scan(hb.b[:, t0:t1], ones[:, 0:t1 - t0], hb.kh[:, t0:t1], 0.0,
                                           ALU.mult, ALU.add).then_inc(b_made[a].sem, 1)

            def keys(i, a, hb):
                dve.tensor_scalar(hb.k, fg[:, i * 2 + a, :], -1.0, 1.0, ALU.mult, ALU.add).then_inc(k_made[a].sem, 1)
                dve.wait_ge(b_made[a].sem, b_made[a].at(i))
                dve.tensor_tensor(hb.kh[:, 0:N_META], hb.b[:, 0:N_META],
                                  hb.b[:, N_META - 1:N_META].broadcast_to((P, N_META)), ALU.subtract)
                own, last = (x.rearrange("p (c t) -> p c t", c=3) for x in (hb.kh[:, N_META:KH], hb.b[:, N_META:KH]))
                dve.tensor_tensor(own, last, last[:, :, P - 1:P].broadcast_to((P, 3, P)),
                                  ALU.subtract).then_inc(kh_exponent[a].sem, 1)

            def scale(i, a, hb, l):
                m = LEVELS[l]
                if l == 0:
                    dve.wait_ge(k_made[a].sem, k_made[a].at(i))
                dve.wait_ge(level_exp[a].sem, level_exp[a].at(i, l))
                if l > 1:
                    dve.wait_ge(level_product[a].sem, level_product[a].at(i, l - 2))
                hold()
                dve.tensor_tensor(part(hb.kt[:, l % 2, :], m, 0), part(hb.k[:, N_META:T], m, 0),
                                  part(hb.ee[:, l % 2, :], m, 0), ALU.mult)
                dve.tensor_tensor(hb.qt[:, l % 2, :].rearrange("p (b r) -> p b r", r=m),
                                  part(q1[:, i * 2 + a, N_META:T], m, 1),
                                  part(hb.ee[:, l % 2, :], m, 1), ALU.mult).then_inc(level_scaled[a].sem, 1)

            def head_pair(i, last):
                both = list(enumerate(head_sets))
                for l in range(len(LEVELS)):
                    for a, hb in both:
                        if l:
                            scale(i, a, hb, l)
                    for a, hb in both:
                        if l == 0:
                            dve.wait_ge(kh_exp[a].sem, kh_exp[a].at(i))
                            dve.tensor_tensor(hb.kh[:, 0:KH], hb.k[:, 0:KH], hb.kh[:, 0:KH],
                                    ALU.mult).then_inc(kh_made[a].sem, 1)
                            dve.wait_ge(diag_product[a].sem, diag_product[a].at(i))
                            hold()
                            dve.copy_predicated(hb.scores, dmask, PS[:, 6 + a, :]).then_inc(level_taken[a].sem, 1)
                        else:
                            take(i, a, hb, l - 1)
                        if l == 2:
                            dve.wait_ge(eb_made[a].sem, eb_made[a].at(i))
                            dve.tensor_copy(hb.decay,
                                    hb.e[:, N_META + P - 1:KH:P]).then_inc(chunk_decay_made[a].sem, 1)
                        if l == 2 + a:
                            dve.wait_ge(chunk_decay_made[a].sem, chunk_decay_made[a].at(i))
                            hold()
                            dve.tensor_tensor(hb.e[:, N_META:T], hb.e[:, N_META:T], q1[:, i * 2 + a, N_META:T],
                                              ALU.mult).then_inc(qd1_made[a].sem, 1)
                        if l == 3:
                            dve.wait_ge(kv1_done[a].sem, kv1_done[a].at(i))
                            dve.tensor_copy(hb.states[:, 0, :],
                                    PS[:, 6 + a, 3 * P:4 * P]).then_inc(states_made[a].sem, 1)
                        elif l > 3:
                            c = l - 4
                            dve.wait_ge(states_made[a].sem, states_made[a].at(i, c))
                            dve.scalar_tensor_tensor(hb.states[:, c + 1, :], hb.states[:, c, :], hb.decay[:, c:c + 1],
                                                     PS[:, 6 + a, c * P:(c + 1) * P],
                                                     ALU.mult, ALU.add).then_inc(states_made[a].sem, 1)
                for a, hb in both:
                    if not last:
                        sum_decays(i + 1, a, hb)
                    take(i, a, hb, len(LEVELS) - 1)
                if not last:
                    for a, hb in both:
                        dve.wait_ge(level_scaled[a].sem, level_scaled[a].at(i))
                        keys(i + 1, a, hb)
                    for a, hb in both:
                        scale(i + 1, a, hb, 0)

            for a, hb in enumerate(head_sets):
                if a:
                    for m in range(2):
                        dve.wait_ge(evac[m].sem, AT["out1"][2])
                clear(hb)
                dve.wait_ge(hg_cleared.sem, hg_cleared.at(0, a))
                sum_decays(0, a, hb)
                keys(0, a, hb)
                scale(0, a, hb, 0)
            with dve.Fori(0, HH // 2 - 1) as i:
                head_pair(i, False)
            head_pair(HH // 2 - 1, True)
            for g in range(4):
                apply_norm(6, range(g, g + 1), fg, nrm_c, par[:, P_GN + 1:P_GN + 2], KEPT)
                gate(6, range(g, g + 1), fg, z1, KEPT)
                if g:
                    gate_low(2, range(2 * g - 2, 2 * g), fg, hg_hi_made, hg_lo_made, KEPT)
            gate_low(2, range(HH - 2, HH), fg, hg_hi_made, hg_lo_made, KEPT)
            out_projection("out1", 2, KEPT)
            layer_norm(2, "mlp1", KEPT)
            mlp("mlp1", 1, KEPT)
            layer_norm(3, "end", KEPT)


def _columns(a):
    return a.reshape(-1, P).T


def kernel(x, meta_tokens, ab_w_in, ab_conv_w, ab_a_log, ab_dt_bias, ab_gnorm_g, ab_w_out, c_w_in, c_lb_raw,
           c_gnorm_g, c_w_out, ln_mix_g, ln_mix_b, mlp_w1, mlp_w2, ln_ffn_g, ln_ffn_b):
    import numpy as np
    import concourse.bacc as bacc
    from concourse.bass_utils import run_bass_kernel_spmd

    w_ab, w_c = ab_w_in[0], c_w_in[0]
    cut = 2048

    def stages(w):
        k, n = w.shape
        return w.reshape(k // D, KT, P, n // COLS, COLS).transpose(3, 0, 2, 1, 4).reshape(-1, P, KT * COLS)

    def mlp(l):
        for half in range(2):
            yield stages(mlp_w1[l][:, half * 2048:(half + 1) * 2048])
            yield stages(mlp_w2[l][half * 2048:(half + 1) * 2048])

    sb_at = cut + 2 * GH
    stream = [stages(w_ab[:, 0:1536]), stages(w_ab[:, 1536:2048]), stages(w_ab[:, sb_at:sb_at + 1024]),
              stages(w_ab[:, sb_at + 1024:sb_at + 1536]), stages(ab_w_out[0]), *mlp(0),
              stages(w_c[:, 1024:2048]), stages(w_c[:, 2048:3072]), stages(w_c[:, 0:1024]), stages(w_c[:, 3072:4096]),
              stages(c_w_out[0]), *mlp(1)]
    wstream = np.ascontiguousarray(np.concatenate(stream))
    gates = w_ab[:, cut:sb_at].reshape(KT, P, 2, GH).transpose(2, 1, 0, 3)

    j, i = np.arange(P)[:, None], np.arange(P)[None, :]
    tables = [j == i, i >= j, j >= i, np.where(j >= i, NEG, 0.0)]
    tables += [(j // (2 * m) == i // (2 * m)) & (j % (2 * m) < m) & (i % (2 * m) >= m) for m in LEVELS]
    tables += [j * np.ones((1, P)) == a for a in range(GH)]
    consts = np.concatenate([np.asarray(t, np.float32) for t in tables], 1)
    hmasks = np.zeros((P, 10, HALF), np.float32)
    for l, m in enumerate(LEVELS):
        t = np.arange(SEQ).reshape(-1, 2 * m)[:, m:].reshape(-1) % P
        hmasks[:, l, :len(t)] = (j // (2 * m) == t[None] // (2 * m)) & (j % (2 * m) < m)
    hmasks[:, 8:10, :] = (j == np.arange(T)[None] % P).reshape(P, 2, HALF)

    lngs = [ln_mix_g[0], ln_ffn_g[0], ln_mix_g[1], ln_ffn_g[1]]
    lnbs = [ln_mix_b[0], ln_ffn_b[0], ln_mix_b[1], ln_ffn_b[1]]
    conv = ab_conv_w[0].reshape(4, 12, P).transpose(2, 1, 0).reshape(P, 48)
    params = np.concatenate([_columns(g) for g in lngs] + [_columns(b) for b in lnbs]
                            + [conv, _columns(c_lb_raw[0]), _columns(c_lb_raw[1]), ab_gnorm_g.T, c_gnorm_g.T], 1)
    h_in = np.concatenate([meta_tokens, x[0]]).T.reshape(KT, P, T).transpose(1, 0, 2)

    arrays = {"h_in": h_in, "wstream": wstream, "wgate": gates, "consts": consts, "hmasks": hmasks,
              "params": params, "gate_params": np.stack([ab_a_log[0], ab_dt_bias[0]], 1)}
    arrays = {k: np.ascontiguousarray(v) for k, v in arrays.items()}
    nc = bacc.Bacc("TRN2", target_bir_lowering=False, num_devices=1)
    args = [nc.dram_tensor(k, v.shape, mybir.dt.from_np(v.dtype), kind="ExternalInput").ap() for k,
            v in arrays.items()]
    out = nc.dram_tensor("out", (KT, P, SEQ), F32, kind="ExternalOutput").ap()
    hybrid_trunk(nc, *args, out)
    result = run_bass_kernel_spmd(nc, [arrays], core_ids=[0])
    got = result.results[0]["out"]
    return np.ascontiguousarray(got.reshape(D, SEQ).T.reshape(1, SEQ, D))
```
